# Optimizing a Trainium2 kernel written in Bass

```python
import math
import jax, jax.numpy as jnp
from jax import lax
import numpy as np

D_MODEL = 1024
BATCH = 1
SEQ = 512
DEPTH = 1

CTX_LEN = 256
GRID_W = 64
N_HEADS = 8
QK_NOPE = 64
QK_ROPE = 32
QK_DIM = QK_NOPE + QK_ROPE
V_DIM = 64
Q_LORA = 384
KV_LORA = 256
ATTN_WIDTH = N_HEADS * V_DIM
ROPE_THETA = 10000.0
ROPE_AXIS_PAIRS = QK_ROPE // 4
Q_BLOCK = 128
SSM_WIDTH = 512
SSM_GROUP = 16
SSM_GROUPS = SSM_WIDTH // SSM_GROUP
SSM_STATE = 64
FFN_HIDDEN = 2816
CONV_W = 3
N_BRANCH = 2
EPS = 1e-6
IN_SPLITS = (Q_LORA, Q_LORA + KV_LORA, Q_LORA + KV_LORA + QK_ROPE,
             Q_LORA + KV_LORA + QK_ROPE + SSM_WIDTH)
IN_WIDTH = Q_LORA + KV_LORA + QK_ROPE + SSM_WIDTH + N_BRANCH * D_MODEL

kernel_name = "hybrid_mla_s5_convffn_prefix_ctx"

def rmsnorm(x, g):
    xf = x.astype(jnp.float32)
    y = xf * lax.rsqrt(jnp.mean(xf * xf, axis=-1, keepdims=True) + EPS)
    return (y * g.astype(jnp.float32)).astype(x.dtype)

def modulate(h, shift, scale):
    return h * (1.0 + scale) + shift

def axial_rope(rows):
    row = jnp.repeat(jnp.arange(rows), GRID_W)
    col = jnp.tile(jnp.arange(GRID_W), rows)
    freqs = ROPE_THETA ** (-jnp.arange(ROPE_AXIS_PAIRS, dtype=jnp.float32) / ROPE_AXIS_PAIRS)
    ang = jnp.concatenate([row[:, None] * freqs, col[:, None] * freqs], axis=-1)
    return jnp.cos(ang), jnp.sin(ang)

def apply_rope(t, cos, sin):
    nope, rope = t[..., :QK_NOPE], t[..., QK_NOPE:]
    r1, r2 = jnp.split(rope, 2, axis=-1)
    cs = cos[:, None, :].astype(t.dtype)
    sn = sin[:, None, :].astype(t.dtype)
    return jnp.concatenate([nope, r1 * cs - r2 * sn, r1 * sn + r2 * cs], axis=-1)

def mla_q(cq, p, cos, sin):
    b, n = cq.shape[:2]
    q = (rmsnorm(cq, p["q_a_g"]) @ p["w_uq"]).reshape(b, n, N_HEADS, QK_DIM)
    q = rmsnorm(q, p["q_norm_g"])
    return q if cos is None else apply_rope(q, cos, sin)

def mla_kv(ckv, krope, p, cos, sin):
    b, n = ckv.shape[:2]
    kv = (rmsnorm(ckv, p["kv_a_g"]) @ p["w_ukv"]).reshape(b, n, N_HEADS, QK_NOPE + V_DIM)
    k_nope, v = jnp.split(kv, [QK_NOPE], axis=-1)
    k_pe = jnp.broadcast_to(krope[:, :, None, :], (b, n, N_HEADS, QK_ROPE))
    k = rmsnorm(jnp.concatenate([k_nope, k_pe], axis=-1), p["k_norm_g"])
    if cos is not None:
        k = apply_rope(k, cos, sin)
    return k, v

def attend(q, k, v):
    s = jnp.einsum("bqhd,bkhd->bhqk", q, k, preferred_element_type=jnp.float32) * (QK_DIM ** -0.5)
    w = jax.nn.softmax(s, axis=-1).astype(v.dtype)
    return jnp.einsum("bhqk,bkhd->bqhd", w, v)

def latent_attention(q, k_lat, v_lat, k_ctx, v_ctx):
    k = jnp.concatenate([k_lat, k_ctx], axis=1)
    v = jnp.concatenate([v_lat, v_ctx], axis=1)
    b, n = q.shape[:2]
    qb = q.reshape(b, n // Q_BLOCK, Q_BLOCK, N_HEADS, QK_DIM).swapaxes(0, 1)
    o = lax.map(lambda qi: attend(qi, k, v), qb)
    return o.swapaxes(0, 1).reshape(b, n, ATTN_WIDTH)

def _ssm_combine(e_i, e_j):
    a_i, b_i = e_i
    a_j, b_j = e_j
    return a_j * a_i, a_j * b_i + b_j

def s5_states(u, p, init_f, init_b):
    b, n = u.shape[:2]
    ug = u.astype(jnp.float32).reshape(b, n, SSM_GROUPS, SSM_GROUP)
    bmat = lax.complex(p["b_re"].astype(jnp.float32), p["b_im"].astype(jnp.float32))
    out = []
    for sfx, init, reverse in (("f", init_f, False), ("b", init_b, True)):
        lam = lax.complex(p["lam_re_" + sfx].astype(jnp.float32), p["lam_im_" + sfx].astype(jnp.float32))
        dt = jnp.exp(p["log_dt_" + sfx].astype(jnp.float32))[:, None]
        lam_bar = jnp.exp(lam * dt)
        b_bar = ((lam_bar - 1.0) / lam)[..., None] * bmat
        bu = jnp.einsum("gnc,bsgc->bsgn", b_bar, ug)
        if init is not None:
            edge = n - 1 if reverse else 0
            bu = bu.at[:, edge].add(lam_bar * init)
        a = jnp.broadcast_to(lam_bar, bu.shape)
        _, xs = lax.associative_scan(_ssm_combine, (a, bu), reverse=reverse, axis=1)
        out.append(xs)
    return out[0], out[1]

def s5_readout(u, xs_f, xs_b, p):
    b, n = u.shape[:2]
    y = u.astype(jnp.float32) * p["d_skip"].astype(jnp.float32)
    for sfx, xs in (("f", xs_f), ("b", xs_b)):
        cm = lax.complex(p["c_re_" + sfx].astype(jnp.float32), p["c_im_" + sfx].astype(jnp.float32))
        y = y + jnp.einsum("gcn,bsgn->bsgc", cm, xs).real.reshape(b, n, SSM_WIDTH)
    return y.astype(u.dtype)

def ssm_glu(y, w_glu):
    val, gate = jnp.split(jax.nn.gelu(y) @ w_glu, 2, axis=-1)
    return val * jax.nn.sigmoid(gate)

def merge_branches(a, s, gate_logits, w_out):
    ga, gs = jnp.split(gate_logits, N_BRANCH, axis=-1)
    return (jax.nn.sigmoid(ga) * a + jax.nn.sigmoid(gs) * s) @ w_out

def dwconv3(u, w, bias):
    up = jnp.pad(u, ((0, 0), (1, 1), (0, 0)))
    return up[:, :-2] * w[0] + up[:, 1:-1] * w[1] + up[:, 2:] * w[2] + bias

def conv_ffn(h, p):
    u = dwconv3(h @ p["w_up"], p["conv_w"], p["conv_b"])
    val, gate = jnp.split(u, 2, axis=-1)
    return (jax.nn.silu(gate) * val) @ p["w_down"]

def hybrid_layer(x, ctx, c, c_ctx, p, cos, sin, update_ctx):
    mod = jax.nn.silu(c) @ p["w_mod"] + p["b_mod"]
    mod_ctx = jax.nn.silu(c_ctx) @ p["w_mod"] + p["b_mod"]
    sh1, sc1, g1, sh2, sc2, g2 = jnp.split(mod[:, None, :], 6, axis=-1)
    csh1, csc1, cg1, csh2, csc2, cg2 = jnp.split(mod_ctx, 6, axis=-1)

    h = modulate(rmsnorm(x, p["norm1_g"]), sh1, sc1)
    hc = modulate(rmsnorm(ctx, p["norm1_g"]), csh1, csc1)
    cq, ckv, kr, u, gl = jnp.split(h @ p["w_in"], IN_SPLITS, axis=-1)
    ccq, cckv, ckr, cu, cgl = jnp.split(hc @ p["w_in"], IN_SPLITS, axis=-1)

    k_c, v_c = mla_kv(cckv, ckr, p, None, None)
    xs_cf, xs_cb = s5_states(cu, p, None, None)

    q_l = mla_q(cq, p, cos, sin)
    k_l, v_l = mla_kv(ckv, kr, p, cos, sin)
    a_l = latent_attention(q_l, k_l, v_l, k_c, v_c) @ p["w_o_attn"]
    xs_f, xs_b = s5_states(u, p, xs_cf[:, -1], xs_cb[:, 0])
    s_l = ssm_glu(s5_readout(u, xs_f, xs_b, p), p["w_glu"])
    x = x + g1 * merge_branches(a_l, s_l, gl, p["w_out"])

    if update_ctx:
        a_c = attend(mla_q(ccq, p, None, None), k_c, v_c).reshape(ctx.shape[0], ctx.shape[1], ATTN_WIDTH)
        s_c = ssm_glu(s5_readout(cu, xs_cf, xs_cb, p), p["w_glu"])
        ctx = ctx + cg1 * merge_branches(a_c @ p["w_o_attn"], s_c, cgl, p["w_out"])

    x = x + g2 * conv_ffn(modulate(rmsnorm(x, p["norm2_g"]), sh2, sc2), p)
    if update_ctx:
        ctx = ctx + cg2 * conv_ffn(modulate(rmsnorm(ctx, p["norm2_g"]), csh2, csc2), p)
    return x, ctx

def setup_inputs(seed: int = 0) -> dict:
    key = jax.random.key(seed)
    ks = iter(jax.random.split(key, 48))
    L, D, G, N, F = DEPTH, D_MODEL, SSM_GROUPS, SSM_STATE, FFN_HIDDEN

    def nrm(shape, scale):
        return jax.random.normal(next(ks), shape, jnp.float32) * scale

    def gain(n):
        return 1.0 + nrm((L, n), 0.02)

    n_idx = jnp.arange(N, dtype=jnp.float32)
    out = {}
    out["x"] = nrm((BATCH, SEQ, D), 1.0)
    out["c"] = nrm((BATCH, D), 1.0)
    out["ctx"] = nrm((BATCH, CTX_LEN, D), 1.0)
    out["c_ctx"] = nrm((D,), 1.0)
    out["w_mod"] = nrm((L, D, 6 * D), 0.5 * D ** -0.5)
    out["b_mod"] = nrm((L, 6 * D), 0.01)
    out["norm1_g"] = gain(D)
    out["norm2_g"] = gain(D)
    out["w_in"] = nrm((L, D, IN_WIDTH), D ** -0.5)
    out["q_a_g"] = gain(Q_LORA)
    out["w_uq"] = nrm((L, Q_LORA, N_HEADS * QK_DIM), Q_LORA ** -0.5)
    out["kv_a_g"] = gain(KV_LORA)
    out["w_ukv"] = nrm((L, KV_LORA, N_HEADS * (QK_NOPE + V_DIM)), KV_LORA ** -0.5)
    out["q_norm_g"] = gain(QK_DIM)
    out["k_norm_g"] = gain(QK_DIM)
    out["w_o_attn"] = nrm((L, ATTN_WIDTH, D), ATTN_WIDTH ** -0.5)
    for sfx in ("f", "b"):
        out["lam_re_" + sfx] = -0.5 + nrm((L, G, N), 0.01)
        out["lam_im_" + sfx] = math.pi * n_idx + nrm((L, G, N), 0.01)
        out["log_dt_" + sfx] = jax.random.uniform(next(ks), (L, G), jnp.float32,
                                                  math.log(1e-3), math.log(1e-1))
        out["c_re_" + sfx] = nrm((L, G, SSM_GROUP, N), (2.0 * N) ** -0.5)
        out["c_im_" + sfx] = nrm((L, G, SSM_GROUP, N), (2.0 * N) ** -0.5)
    out["b_re"] = nrm((L, G, N, SSM_GROUP), (2.0 * SSM_GROUP) ** -0.5)
    out["b_im"] = nrm((L, G, N, SSM_GROUP), (2.0 * SSM_GROUP) ** -0.5)
    out["d_skip"] = nrm((L, SSM_WIDTH), 1.0)
    out["w_glu"] = nrm((L, SSM_WIDTH, 2 * D), SSM_WIDTH ** -0.5)
    out["w_out"] = nrm((L, D, D), D ** -0.5)
    out["w_up"] = nrm((L, D, 2 * F), D ** -0.5)
    out["conv_w"] = nrm((L, CONV_W, 2 * F), CONV_W ** -0.5)
    out["conv_b"] = nrm((L, 2 * F), 0.01)
    out["w_down"] = nrm((L, F, D), F ** -0.5)
    return out

def reference(x, c, ctx, c_ctx, w_mod, b_mod, norm1_g, norm2_g, w_in, q_a_g, w_uq, kv_a_g, w_ukv,
              q_norm_g, k_norm_g, w_o_attn,
              lam_re_f, lam_im_f, log_dt_f, c_re_f, c_im_f,
              lam_re_b, lam_im_b, log_dt_b, c_re_b, c_im_b,
              b_re, b_im, d_skip, w_glu, w_out, w_up, conv_w, conv_b, w_down):
    rows = x.shape[1] // GRID_W
    cos, sin = axial_rope(rows)
    for l in range(DEPTH):
        p = dict(w_mod=w_mod[l], b_mod=b_mod[l], norm1_g=norm1_g[l], norm2_g=norm2_g[l], w_in=w_in[l],
                 q_a_g=q_a_g[l], w_uq=w_uq[l], kv_a_g=kv_a_g[l], w_ukv=w_ukv[l],
                 q_norm_g=q_norm_g[l], k_norm_g=k_norm_g[l], w_o_attn=w_o_attn[l],
                 lam_re_f=lam_re_f[l], lam_im_f=lam_im_f[l], log_dt_f=log_dt_f[l],
                 c_re_f=c_re_f[l], c_im_f=c_im_f[l],
                 lam_re_b=lam_re_b[l], lam_im_b=lam_im_b[l], log_dt_b=log_dt_b[l],
                 c_re_b=c_re_b[l], c_im_b=c_im_b[l],
                 b_re=b_re[l], b_im=b_im[l], d_skip=d_skip[l], w_glu=w_glu[l], w_out=w_out[l],
                 w_up=w_up[l], conv_w=conv_w[l], conv_b=conv_b[l], w_down=w_down[l])
        x, ctx = hybrid_layer(x, ctx, c, c_ctx, p, cos, sin, update_ctx=(l < DEPTH - 1))
    return x


_drawn_inputs = setup_inputs


def setup_inputs(seed=0):
    import zlib

    import numpy as np

    out = dict(_drawn_inputs(seed))
    spreads = {}
    factors = {'ctx': 8.0,
     'c_ctx': 3.608,
     'b_mod': 6.231,
     'norm1_g': 8.0,
     'norm2_g': 8.0,
     'q_a_g': 8.0,
     'w_uq': 4.326,
     'kv_a_g': 8.0,
     'q_norm_g': 8.0,
     'k_norm_g': 8.0,
     'lam_re_f': 64.0,
     'lam_im_f': 64.0,
     'log_dt_f': 64.0,
     'c_re_f': 64.0,
     'c_im_f': 64.0,
     'lam_re_b': 64.0,
     'lam_im_b': 64.0,
     'log_dt_b': 64.0,
     'c_re_b': 64.0,
     'c_im_b': 64.0,
     'b_re': 64.0,
     'b_im': 64.0,
     'conv_b': 33.945}
    for name, (base, spread) in spreads.items():
        noise = np.random.default_rng([zlib.crc32(name.encode()), seed]).standard_normal(out[name].shape)
        drawn = base * np.exp(spread * noise) if base else spread * noise
        out[name] = __import__('jax').numpy.asarray(drawn.astype(out[name].dtype))
    for name, factor in factors.items():
        out[name] = (out[name] * factor).astype(out[name].dtype)
    return out
```

```python
from contextlib import ExitStack

import numpy as np

import concourse.bass as bass
from concourse import mybir
from concourse.alu_op_type import AluOpType as ALU

F32 = mybir.dt.float32
F32R = mybir.dt.float32r
I32 = mybir.dt.int32
ACT = mybir.ActivationFunctionType
AX = mybir.AxisListType

P = 128
D = 1024
KD = D // P
T = 512
C = 256
TT_N, CT_N = T // P, C // P
H, NOPE, ROPE, VD = 8, 64, 32, 64
QK = NOPE + ROPE
QL, KVL = 384, 256
SSM = 512
G, GC, NS = 32, 16, 64
NP = G // 2
L = 8
CK, CC = T // L, C // L
NK = CC + CK
NB, GB, PB = 4, 8, 4
FF = 2816
KF = FF // P
IN_W = QL + KVL + ROPE + SSM + 2 * D
U0 = QL + KVL + ROPE
GATE0 = U0 + SSM
PW = 2048
EPS = 1e-6
SCALE = QK ** -0.5

V_BMOD, V_N1, V_N2, V_DSKIP, V_QAG, V_KVAG = 0, 48, 56, 64, 68, 71
V_W0, V_W1, V_W2, V_CB = 73, 117, 161, 205
V_LAM, V_LDT, V_END = 249, 313, 345

GATE_ORDER = ("gate", "mod2", "mod2", "mod2", "mod2", "gate") * 4
STREAM = ["mod1"] * 4 + ["lat"] * 3 + ["u"] * 2 + list(GATE_ORDER) + ["uq"] * 2 + ["ukv"] + ["glu"] * 4 \
    + ["wo"] * 2 + ["wout"] * 4 + ["up"] * 22 + ["down"] * 12


def positions():
    n_of, s_of, s_at, is_split = {}, {}, [], []
    s = 0
    for n, stage in enumerate(STREAM):
        n_of.setdefault(stage, []).append(n)
        split = not stage.startswith("mod")
        is_split.append(split)
        s_at.append(s)
        if split:
            s_of.setdefault(stage, []).append(s)
            s += 1
    return n_of, s_of, s_at, is_split


N_OF, S_OF, S_AT, IS_SPLIT = positions()
N_OF_SPLIT = [n for n in range(len(STREAM)) if IS_SPLIT[n]]

TILES = {"lat": 9, "u": 12, "gate": 16, "uq": 8, "ukv": 12, "glu": 16, "wo": 8, "wout": 8,
         "up": 44, "down": 8}
TILE0 = {}
_t = 0
for _name, _n in TILES.items():
    TILE0[_name] = _t
    _t += _n


class Chain:

    def __init__(self, eng, sem):
        self.eng, self.sem, self.base, self.local = eng, sem, 0, 0

    def __call__(self, ins):
        ins.then_inc(self.sem, 1)
        self.local += 1

    def wait(self):
        self.eng.wait_ge(self.sem, self.base + self.local)

    def step(self, ins):
        self(ins)
        self.wait()

    def enter(self, i, per_round):
        self.outer = self.base + self.local
        self.per_round = per_round
        self.base, self.local = self.outer + i * per_round, 0

    def leave(self, rounds):
        assert self.local == self.per_round, (self.local, self.per_round)
        self.base, self.local = self.outer + rounds * self.per_round, 0


def rope_tables():
    pos = np.arange(T)
    freqs = (10000.0 ** (-np.arange(ROPE // 4, dtype=np.float32) / (ROPE // 4))).astype(np.float32)
    row = (pos // 64).astype(np.float32)[:, None] * freqs
    col = (pos % 64).astype(np.float32)[:, None] * freqs
    ang = np.concatenate([row, col], axis=-1).astype(np.float64)
    return np.concatenate([np.cos(ang), np.sin(ang)], axis=-1).astype(np.float32)


def build(nc, a, out):
    ctx = ExitStack()
    with ctx:
        def sem(name):
            return ctx.enter_context(nc.semaphore(name))

        ORIGIN = 16512

        def at(name, kb, shape, dt=F32):
            return nc.alloc_sbuf_tensor_at(name, shape, dt, offset=ORIGIN + int(kb * 1024))

        raw = [at(f"raw{i}", 8 * i, [P, PW]) for i in range(2)]
        whi = [at(f"w_hi{i}", 16 + 8 * i, [P, PW], F32R) for i in range(2)]
        wlo = [at(f"w_lo{i}", 32 + 8 * i, [P, PW], F32R) for i in range(2)]
        early = [at(f"early{i}", 16 + 8 * i, [P, PW]) for i in range(4)]
        xT = at("xT", 48, [P, KD, T])
        o = [64.0]

        def small(name, shape, dt=F32):
            t = at(name, o[0], shape, dt)
            n = 1
            for d in shape[1:]:
                n *= d
            o[0] += ((n * 4 + 31) // 32 * 32) / 1024
            assert o[0] <= 70.01, (name, o[0])
            return t

        ident = small("ident", [P, P])
        ones = small("ones", [P, P])
        VEC = small("VEC", [P, V_END])
        modb = small("modb", [P, 48, 2])
        gain1 = small("gain1", [P, 2, KD])
        gain2 = small("gain2", [P, KD])
        LP = small("LP", [P, 2, 9, 32])
        r8 = small("r8", [P, 32])
        cs = small("cs", [P, KD, 2])
        dmask = small("dmask", [P, GC])
        stv = small("stv", [P, 10])
        sty = small("sty", [P, 10])
        stt = small("stt", [P, 10])
        smx = small("smx", [P, 4, 4])

        h_hi = at("h_hi", 70, [P, KD, T], F32R)
        h_lo = at("h_lo", 86, [P, KD, T], F32R)
        cq = at("cq", 102, [P, 3, T])
        ckv = at("ckv", 108, [P, 2, C + T])
        hc_hi = at("hc_hi", 114, [P, KD, C], F32R)
        hc_lo = at("hc_lo", 122, [P, KD, C], F32R)
        utok = at("utok", 130, [P, NB, GB * L * GC])
        ustage = at("ustage", 179, [P, L, SSM])
        CP = at("CP", 146, [P, 2, 2, PB, 9 * GC])
        BP = at("BP", 155, [P, 2, 2, PB, P])
        bbd = at("bbd", 163, [P, 2, 2, PB, 32])
        E = at("E", 165, [P, 2, 8, NK])
        CT = at("CT", 171, [P, 2, 2, NP, GC])
        BB = at("BB", 175, [P, 2, 2, NP, GC])
        xtok = at("xtok", 70, [P, TT_N, D])
        ctok = at("ctok", 86, [P, CT_N, D])
        ctile = at("ctile", 114, [P, 4, NB, 2, NS])
        junk = at("junk", 122, [P, D])
        diag = at("diag", 126, [P, 6, P])
        Bld = at("Bld", 152, [P, 2, NP, GC])
        TMP = at("TMP", 146, [P, 44, 32])
        rowsA = at("rowsA", 138, [73, P])
        rowsB = at("rowsB", 138.5, [88, P])
        rowsC = at("rowsC", 139, [88, P])
        rowsL = at("rowsL", 139.5, [64, P])
        ldt = at("ldt", 140, [32, 2])
        rowsT = at("rowsT", 140.5, [32, P])
        ccld = at("ccld", 141, [P, 2, KD])
        bbt = at("bbt", 154, [P, 2, NP, GC])
        macc1 = at("macc1", 102, [P, 4, 2, 256])
        xn = at("xn", 179, [P, KD, T])
        cn = at("cn", 94, [P, KD, C])
        rstdb = at("rstdb", 203, [P, C + T])
        hf = [at(f"hf{i}", 130 + 3 * i, [P, C + T]) for i in range(2)]
        sqq = at("sqq", 179, [P, 3, T])
        sqk = at("sqk", 185, [P, 2, C + T])
        diag2 = at("diag2", 137, [P, 10, P])
        krT = at("krT", 142, [ROPE, C + T])
        ust = [at(f"ust{i}", 191 + i, [P, 256]) for i in range(4)]
        WinT = at("WinT", 114, [P, 2, 2, PB, P])
        TTm = at("TTm", 122, [P, GB, P])
        SBD = [at("SBD0", 126, [P, 2, PB, 2, CK]), at("SBD1", 191, [P, 2, PB, 2, CK])]
        U = at("U", 179, [P, GB, NK])
        Ub = at("Ub", 182, [P, GB, NK])
        W = at("W", 185, [P, 2, 2, PB, NK])
        Ysb = at("Ysb", 185, [P, GB, CK])
        zp = at("zp", 200, [P, 7, 2, 32])
        pt1 = at("pt1", 195, [P, 512])
        ytok = at("ytok", 187, [64, L, P])
        tmpA = at("tmpA", 197, [P, PB, NK])
        tmpB = at("tmpB", 198.5, [P, PB, NK])
        Kf = at("Kf", 190, [P, 15 * GC])
        gst = [at(f"gst{i}", 202 + 2 * i, [P, T]) for i in range(2)]
        kr = at("kr", 206, [P, 6, ROPE])
        y_hi = at("y_hi", 70, [P, 4, T], F32R)
        y_lo = at("y_lo", 78, [P, 4, T], F32R)
        sT = at("sT", 86, [P, KD, T])
        qT = at("qT", 102, [QK, H, T])
        V = at("V", 118, [P, 6, H * VD])
        kT = at("kT", 130, [QK, H, C + T])
        cq_hi = at("cq_hi", 146, [P, 3, T], F32R)
        cq_lo = at("cq_lo", 152, [P, 3, T], F32R)
        ckv_hi = at("ckv_hi", 158, [P, 2, C + T], F32R)
        ckv_lo = at("ckv_lo", 164, [P, 2, C + T], F32R)
        gload = [at(f"gload{i}", 154 + 2 * i, [P, T]) for i in range(4)]
        sg = [at(f"sg{i}", 162 + 2 * i, [P, T]) for i in range(2)]
        qsb = at("qsb", 170, [P, TT_N, H, QK])
        ksb = at("ksb", 182, [P, 6, H, QK])
        sqt = [at(f"sqt{i}", 200 + 2 * i, [P, T]) for i in range(2)]
        tq = at("tq", 130, [P, 4, 512])
        qkg = at("qkg", 204, [P, 2, QK])
        rope = at("rope", 204.75, [P, TT_N, 32])
        stq = at("stq", 205.25, [P, 2, 80])
        stq3 = at("stq3", 206.75, [P, 6])
        Pm = [at(f"Pm{i}", 170 + 3 * i, [P, C + T]) for i in range(2)]
        PT = [at(f"PT{i}", 176 + 3 * i, [P, 6, P]) for i in range(2)]
        otok = at("otok", 182, [P, TT_N, H * VD])
        oT_hi = at("oT_hi", 190, [P, 4, T], F32R)
        oT_lo = at("oT_lo", 198, [P, 4, T], F32R)
        mg_hi = at("mg_hi", 102, [P, KD, T], F32R)
        mg_lo = at("mg_lo", 118, [P, KD, T], F32R)
        mgf = [at(f"mgf{i}", 162 + 2 * i, [P, T]) for i in range(2)]
        sqx = at("sqx", 134, [P, KD, T])
        h2_hi = at("h2_hi", 70, [P, KD, T], F32R)
        h2_lo = at("h2_lo", 86, [P, KD, T], F32R)
        nx = [at(f"nx{i}", 190 + 2 * i, [P, T]) for i in range(2)]
        nh = [at(f"nh{i}", 194 + 2 * i, [P, T]) for i in range(2)]
        diag3 = at("diag3", 198, [P, TT_N, P])
        act_hi = at("act_hi", 102, [P, KF, T], F32R)
        act_lo = at("act_lo", 146, [P, KF, T], F32R)
        cv = [[at(f"cv{v}{i}", 190 + 4 * v + 2 * i, [P, T]) for i in range(2)] for v in range(2)]
        sl = [at(f"sl{i}", 198 + 2 * i, [P, T]) for i in range(2)]
        xo = [at(f"xo{i}", 70 + 4 * i, [P, 2, T]) for i in range(2)]
        ost = [at(f"ost{i}", 78 + 4 * i, [P, TT_N, 256]) for i in range(2)]

        ps = ctx.enter_context(nc.psum_tensor("ps", [P, 8, 512], F32))
        bank = [ps[:, i, :] for i in range(8)]

        u_dram = nc.dram_tensor("u_scratch", (C + T, SSM), F32, kind="Internal").ap()
        kf_dram = nc.dram_tensor("kf_scratch", (NB, P, 15 * GC), F32, kind="Internal").ap()
        gate_dram = nc.dram_tensor("gate_scratch", (16, P, T), F32, kind="Internal").ap()

        def rows(w):
            return w.rearrange("(k p) n -> p k n", p=P)

        w_mod_v = a["w_mod"].rearrange("(p k) n -> p k n", k=KD)
        w_in_v, w_uq_v, w_ukv_v, w_o_v, w_glu_v = (rows(a[n]) for n in ("w_in", "w_uq", "w_ukv", "w_o_attn", "w_glu"))
        w_out_v, w_up_v, w_down_v = (rows(a[n]) for n in ("w_out", "w_up", "w_down"))

        def width(stage, p):
            return {"lat": (2048, 2048, 1280)[p] if stage == "lat" else 0, "uq": 1152,
                    "down": (2048, 2048, 1536)[p % 3]}.get(stage, 2048)

        def parts(stage, p, buf):
            if stage in ("mod1", "mod2"):
                c0 = p * 256 + (2048 if stage == "mod2" else 0)
                return [(buf[:, :].rearrange("p (k n) -> p k n", k=8), w_mod_v[:, :, bass.ds(c0, 256)])]
            if stage == "lat":
                w = width(stage, p) // 8
                return [(buf[:, 0:8 * w].rearrange("p (k n) -> p k n", k=8), w_in_v[:, :, 256 * p:256 * p + w])]
            if stage in ("u", "gate"):
                c0 = (U0 if stage == "u" else GATE0) + p * 256
                return [(buf[:, :].rearrange("p (k n) -> p k n", k=8), w_in_v[:, :, bass.ds(c0, 256)])]
            if stage == "uq":
                return [(buf[:, 0:1152].rearrange("p (k n) -> p k n", k=3), w_uq_v[:, :, 384 * p:384 * p + 384])]
            if stage == "ukv":
                return [(buf[:, :].rearrange("p (k n) -> p k n", k=2), w_ukv_v[:, :, :])]
            if stage == "glu":
                b = buf[:, :].rearrange("p (k v n) -> p k v n", k=4, v=2)
                return [(b[:, :, v, :], w_glu_v[:, :, bass.ds(p * 256 + v * D, 256)]) for v in range(2)]
            if stage == "wo":
                return [(buf[:, :].rearrange("p (k n) -> p k n", k=4), w_o_v[:, :, 512 * p:512 * p + 512])]
            if stage == "wout":
                return [(buf[:, :].rearrange("p (k n) -> p k n", k=8), w_out_v[:, :, bass.ds(p * 256, 256)])]
            if stage == "up":
                b = buf[:, :].rearrange("p (k v n) -> p k v n", k=8, v=2)
                return [(b[:, :, v, :], w_up_v[:, :, bass.ds(p * 128 + v * FF, 128)]) for v in range(2)]
            raise ValueError(stage)

        def down_part(pair, kk, buf):
            n = (8, 8, 6)[kk]
            return buf[:, 0:n * 256].rearrange("p (k n) -> p k n", k=n), w_down_v[:, 8 * kk:8 * kk + n, bass.ds(pair * 256, 256)]

        raw_in = [sem("raw_in0"), sem("raw_in1")]
        hi_ready, lo_ready = sem("hi_ready"), sem("lo_ready")
        tile_done, tile_free = sem("tile_done"), sem("tile_free")
        down_used = sem("down_used")
        params_in, c_in, b_in = sem("params_in"), sem("c_in"), sem("b_in")
        lamv_in, x_in, ctx_in, ccld_in, attn_consts_in = (sem(n) for n in ("lamv_in", "x_in", "ctx_in", "ccld_in", "attn_consts_in"))
        consts_ready, cs_ready, ldt_wide = sem("consts_ready"), sem("cs_ready"), sem("ldt_wide")
        vec_T, vec_ready = sem("vec_T"), sem("vec_ready")
        pool_chain, dve_chain, act_chain = sem("pool_chain"), sem("dve_chain"), sem("act_chain")
        den_ready = sem("den_ready")
        sin_arg, sin_done = sem("sin_arg"), sem("sin_done")
        ssm_scalars = sem("ssm_scalars")
        ct_T, ct_ready = sem("ct_T"), sem("ct_ready")
        sumsq1, diag1_ready, rstd1_mm, rstd1_ready = (sem(n) for n in ("sumsq1", "diag1_ready", "rstd1_mm", "rstd1_ready"))
        xT_mm, xT_ready, xn_ready = sem("xT_mm"), sem("xT_ready"), sem("xn_ready")
        gain1_ready, hf_ready, h_split = sem("gain1_ready"), sem("hf_ready"), sem("h_split")
        latq_evac, latsq, lat_stat, diag2_ready, rstd2_mm, lat_normed = (sem(n) for n in ("latq_evac", "latsq", "lat_stat", "diag2_ready", "rstd2_mm", "lat_normed"))
        u_evac, u_out, utok_in = sem("u_evac"), [sem(f"u_out{i}") for i in range(4)], sem("utok_in")
        bp_ready, cp_ready, e_ready = sem("bp_ready"), sem("cp_ready"), sem("e_ready")
        u_T, u_evacA, u_evacD = sem("u_T"), sem("u_evacA"), sem("u_evacD")
        bp_T, winT_A, winT_D = sem("bp_T"), sem("winT_A"), sem("winT_D")
        t_mm, kf_ready, kf_out, tt_in = sem("t_mm"), sem("kf_ready"), sem("kf_out"), sem("tt_in")
        v_mm, v_read, state_ready, y_mm = sem("v_mm"), sem("v_read"), sem("state_ready"), sem("y_mm")
        y_evac, y_T, ytok_A, ytok_D, y_T2, gelu_done = (sem(n) for n in ("y_evac", "y_T", "ytok_A", "ytok_D", "y_T2", "gelu_done"))
        gate_sig, gate_out = sem("gate_sig"), [sem("gate_out0"), sem("gate_out1")]
        early_in = [sem(f"early_in{i}") for i in range(4)]
        mod1_pe, mod1_dve, mod1_mm = sem("mod1_pe"), sem("mod1_dve"), sem("mod1_mm")
        mod2_used, mod2_acc = sem("mod2_used"), sem("mod2_acc")
        kr_T, kr_ready = sem("kr_T"), sem("kr_ready")
        prep_hi, prep_lo = sem("prep_hi"), sem("prep_lo")
        q_sq, sq_used, v_copy = sem("q_sq"), sem("sq_used"), sem("v_copy")
        q_ready, k_ready, qk_A, qk_D = sem("q_ready"), sem("k_ready"), sem("qk_A"), sem("qk_D")
        yprep_hi, yprep_lo = sem("yprep_hi"), sem("yprep_lo")
        ug_A, ug_D = sem("ug_A"), sem("ug_D")
        gain2_ready, sbd_zero, ct2_ready = sem("gain2_ready"), sem("sbd_zero"), sem("ct2_ready")
        qk_ready, qk_T, qkT_ready = sem("qk_ready"), sem("qk_T"), sem("qkT_ready")
        gload_in = [sem(f"gload_in{i}") for i in range(4)]
        sg_ready, s_ready = sem("sg_ready"), sem("s_ready")
        s_mm, max_ready, exp_ready, p_T, pt_A, pt_D, o_mm, o_evac = (sem(n) for n in ("s_mm", "max_ready", "exp_ready", "p_T", "pt_A", "pt_D", "o_mm", "o_evac"))
        o_T, oT_hi_r, oT_lo_r = sem("o_T"), sem("oT_hi_r"), sem("oT_lo_r")
        mg_f, mg_h, mg_l = sem("mg_f"), sem("mg_h"), sem("mg_l")
        x1_ready, sqx_ready, stat2_mm, diag3_ready, rstd3_mm = (sem(n) for n in ("x1_ready", "sqx_ready", "stat2_mm", "diag3_ready", "rstd3_mm"))
        nx_ready, nh_ready, h2_h, h2_l = sem("nx_ready"), sem("nh_ready"), sem("h2_h"), sem("h2_l")
        cv_a, cv_d, silu_done, act_f, act_h, act_l = (sem(n) for n in ("cv_a", "cv_d", "silu_done", "act_f", "act_h", "act_l"))
        xo_ready, xo_T, ost_ready, out_done = sem("xo_ready"), sem("xo_T"), sem("ost_ready"), [sem("out_done0"), sem("out_done1")]

        def transfers(stage):
            return 2 if stage in ("glu", "up") else 1

        def raw_in_count(n):
            return 16 * sum(transfers(STREAM[m]) for m in range(n % 2, n + 1, 2))

        tiles_through = {}
        for p_, e_ in enumerate((2, 5, 9)):
            tiles_through[N_OF["lat"][p_]] = TILE0["lat"] + e_
        for p_ in range(2):
            tiles_through[N_OF["u"][p_]] = TILE0["u"] + 6 * p_ + 6
            tiles_through[N_OF["uq"][p_]] = TILE0["uq"] + 4 * p_ + 4
            tiles_through[N_OF["wo"][p_]] = TILE0["wo"] + 4 * p_ + 4
        for i_ in range(8):
            tiles_through[N_OF["gate"][i_]] = TILE0["gate"] + 2 * i_ + 2
        tiles_through[N_OF["ukv"][0]] = TILE0["ukv"] + 12
        for p_ in range(4):
            tiles_through[N_OF["glu"][p_]] = TILE0["glu"] + 4 * p_ + 4
            tiles_through[N_OF["wout"][p_]] = TILE0["wout"] + 2 * p_ + 2
        for p_ in range(22):
            tiles_through[N_OF["up"][p_]] = TILE0["up"] + 2 * p_ + 2

        def wait_used(eng, n):
            if STREAM[n] == "mod1":
                return eng.wait_ge(mod1_dve if n % 2 else mod1_pe, 1 if n < 2 else 4)
            if STREAM[n] == "mod2":
                return eng.wait_ge(mod2_used, N_OF["mod2"].index(n) + 1)
            if STREAM[n] == "down":
                p = n - N_OF["down"][0]
                if p % 3 == 2:
                    eng.wait_ge(tile_done, TILE0["down"] + 2 * (p // 3) + 2)
                else:
                    eng.wait_ge(down_used, 2 * (p // 3) + p % 3 + 1)
            else:
                eng.wait_ge(tile_done, tiles_through[n])

        def split_hi(act, s):
            n = N_OF_SPLIT[s]
            w = width(STREAM[n], n - N_OF[STREAM[n]][0])
            act.wait_ge(raw_in[n % 2], raw_in_count(n))
            if s >= 2:
                wait_used(act, N_OF_SPLIT[s - 2])
            else:
                act.wait_ge(mod1_dve if s else mod1_pe, 2)
            act.activation(whi[s % 2][:, 0:w], raw[n % 2][:, 0:w], ACT.Copy).then_inc(hi_ready, 1)

        def split_lo(dve, s):
            n = N_OF_SPLIT[s]
            w = width(STREAM[n], n - N_OF[STREAM[n]][0])
            dve.wait_ge(hi_ready, s + 1)
            if s < 2:
                dve.wait_ge(mod1_dve if s else mod1_pe, 3)
            dve.tensor_tensor(wlo[s % 2][:, 0:w], raw[n % 2][:, 0:w], whi[s % 2][:, 0:w].bitcast(F32),
                              ALU.subtract).then_inc(lo_ready, 1)

        def qk_tile(i):
            if i < H:
                return qT[:, i, :], T
            h, part = (i - H) // 2, (i - H) % 2
            return (kT[:, h, T:], C) if part else (kT[:, h, 0:T], T)

        block = ctx.enter_context(nc.Block())

        @block.sync
        def _(sp):
            def load(n, p=None):
                stage = STREAM[n]
                p = n - N_OF[stage][0] if p is None else p
                if n >= 2:
                    if IS_SPLIT[n - 2]:
                        sp.wait_ge(lo_ready, S_AT[n - 2] + 1)
                    else:
                        wait_used(sp, n - 2)
                for dst, src in parts(stage, p, raw[n % 2]):
                    sp.dma_start(dst, src).then_inc(raw_in[n % 2], 16)

            def load_down(n, pair, kk):
                sp.wait_ge(lo_ready, S_AT[n - 2] + 1)
                dst, src = down_part(pair, kk, raw[n % 2])
                sp.dma_start(dst, src).then_inc(raw_in[n % 2], 16)

            def load_mod1(p, buf, signal):
                for dst, src in parts("mod1", p, buf):
                    sp.dma_start(dst, src).then_inc(signal, 16)

            for p in range(2):
                load_mod1(p, raw[p], raw_in[p])
            sp.dma_start(xtok[:, :, :], a["x"].rearrange("(t p) n -> p t n", p=P)).then_inc(x_in, 16)
            for p in range(2, 4):
                load_mod1(p, early[p - 2], early_in[p - 2])
            sp.dma_start(ctok[:, :, :], a["ctx"].rearrange("(t p) n -> p t n", p=P)).then_inc(ctx_in, 16)
            for p in range(4, 6):
                load_mod1(p, early[p - 2], early_in[p - 2])
            sp.wait_ge(mod1_pe, 1)
            load_mod1(6, raw[0], raw_in[0])
            sp.wait_ge(mod1_dve, 1)
            load_mod1(7, raw[1], raw_in[1])
            for n in N_OF["lat"] + N_OF["u"]:
                load(n)
            gate_p = mod_p = 0
            for n in range(N_OF["gate"][0], N_OF["gate"][-1] + 1):
                if IS_SPLIT[n]:
                    load(n, gate_p)
                    gate_p += 1
                else:
                    load(n, mod_p)
                    mod_p += 1
                if n == N_OF["gate"][0]:
                    for i in range(4):
                        sp.wait_ge(u_out[i], 16 * 3)
                    sp.wait_ge(lat_stat, 1)
                    for j in range(L):
                        sp.dma_start(ustage[0:NK, L - 1 - j, :],
                                     u_dram.rearrange("(k j) c -> j k c", j=L)[j]).then_inc(utok_in, 16)
            for n in N_OF["uq"] + N_OF["ukv"] + N_OF["glu"] + N_OF["wo"] + N_OF["wout"] + N_OF["up"][:2]:
                load(n)
            n0 = N_OF["up"][0]
            with sp.Fori(1, 11) as i:
                for j in range(2):
                    sp.wait_ge(lo_ready, S_AT[n0] + 2 * i + j - 1)
                    for dst, src in parts("up", 2 * i + j, raw[(n0 + j) % 2]):
                        sp.dma_start(dst, src).then_inc(raw_in[(n0 + j) % 2], 16)
            n0 = N_OF["down"][0]
            for j in range(2):
                load_down(n0 + j, 0, j)
            sp.wait_ge(lo_ready, S_AT[n0] + 1)
            dst, src = down_part(0, 2, raw[(n0 + 2) % 2])
            sp.dma_start(dst, src).then_inc(raw_in[(n0 + 2) % 2], 16)
            for j in range(3):
                load_down(n0 + 3 + j, 1, j)
            with sp.Fori(1, 2) as i:
                for j in range(6):
                    sp.wait_ge(lo_ready, S_AT[n0] + 6 * i + j - 1)
                    dst, src = down_part(2 * i + j // 3, j % 3, raw[(n0 + j) % 2])
                    sp.dma_start(dst, src).then_inc(raw_in[(n0 + j) % 2], 16)
            for pair in range(4):
                sp.wait_ge(ost_ready, pair + 1)
                sp.dma_start(out[:, pair * 256:(pair + 1) * 256].rearrange("(t p) n -> p t n", p=P),
                             ost[pair % 2][:, :, :]).then_inc(out_done[pair % 2], 16)
            for i in range(2):
                sp.wait_ge(out_done[i], 32)

        @block.gpsimd
        def _(pool):
            ch = Chain(pool, pool_chain)
            ch(pool.memset(ident[:, :], 0.0))
            ch(pool.memset(bbd[:, :, :, :, :], 0.0))
            ch.wait()
            ch.step(pool.affine_select(out=ident[:, :], in_=ident[:, :], compare_op=ALU.not_equal, fill=1.0, base=0,
                                       pattern=[[-1, P]], channel_multiplier=1))
            pool.memset(ones[:, :], 1.0).then_inc(consts_ready, 1)

            def tt(o_, x_, y_, op):
                return pool.tensor_tensor(o_, x_, y_, op)

            def ts(o_, x_, s1, s2=None, op0=ALU.mult, op1=ALU.add):
                if s2 is None:
                    return pool.tensor_scalar(o_, x_, s1, None, op0)
                return pool.tensor_scalar(o_, x_, s1, s2, op0, op1)

            def stt_(o_, x_, s, y_, op0, op1):
                ch.step(ts(TMP[:, 43, :], x_, s, None, op0))
                return tt(o_, TMP[:, 43, :], y_, op1)

            tmp = [TMP[:, k, :] for k in range(44)]

            def dm(v):
                return v.rearrange("p (d m) -> p d m", d=2)

            def exp(y, x, s):
                xc, n, f, q = s
                ch.step(ts(xc, x, -87.0, 88.0, ALU.max, ALU.min))
                ch.step(ts(n, xc, 1.4426950408889634, 12582912.0, ALU.mult, ALU.add))
                ch.step(ts(n, n, -12582912.0, None, ALU.add))
                ch.step(stt_(f, n, -0.693359375, xc, ALU.mult, ALU.add))
                ch.step(stt_(f, n, 2.12194440e-4, f, ALU.mult, ALU.add))
                ch.step(ts(q, f, 1.0 / 5040))
                for c_ in (1.0 / 720, 1.0 / 120, 1.0 / 24, 1.0 / 6, 0.5, 1.0):
                    ch.step(stt_(q, q, c_, f, ALU.add, ALU.mult))
                ch.step(ts(n.bitcast(I32), n, 8388608.0, 127.0 * 8388608.0))
                ch.step(stt_(y, q, 1.0, n, ALU.add, ALU.mult))
                ch.step(stt_(y, x, -87.0, y, ALU.is_ge, ALU.mult))

            pool.wait_ge(vec_ready, 1)
            lam = VEC[:, V_LAM:V_LAM + 64].rearrange("p (d r m) -> p r d m", d=2, r=2)
            lre, lim = lam[:, 0], lam[:, 1]
            dt, mag, th, n_ = tmp[0], tmp[1], tmp[2], tmp[3]
            exp(dt, VEC[:, V_LDT:V_LDT + 32], tmp[4:8])
            ch.step(tt(dm(th), lim, dm(dt), ALU.mult))
            ch.step(ts(n_, th, 0.15915494309189535, 12582912.0, ALU.mult, ALU.add))
            ch.step(ts(n_, n_, -12582912.0, None, ALU.add))
            ch.step(stt_(th, n_, -6.28125, th, ALU.mult, ALU.add))
            ch.step(stt_(th, n_, -0.0019350051879882812, th, ALU.mult, ALU.add))
            ch.step(stt_(th, n_, -3.0199159819567e-07, th, ALU.mult, ALU.add))
            ch.step(ts(tmp[8], th, 3.1415925, -3.1415925, ALU.min, ALU.max))
            ts(tmp[9], tmp[8], 0.5).then_inc(sin_arg, 1)
            ch.step(tt(dm(tmp[12]), lre, dm(dt), ALU.mult))
            exp(mag, tmp[12], tmp[4:8])
            pool.wait_ge(sin_done, 1)
            c1, s1 = tmp[13], tmp[14]
            ch.step(tt(c1, tmp[11], tmp[11], ALU.mult))
            ch.step(ts(c1, c1, -2.0, 1.0))
            ch.step(pool.tensor_copy(s1, tmp[10]))

            def cmul(o_, x_, y_, t, shape=None):
                b_ = (lambda v: v.to_broadcast(shape)) if shape else (lambda v: v)
                ch(tt(o_[0], x_[0], b_(y_[0]), ALU.mult))
                ch(tt(t[0], x_[1], b_(y_[1]), ALU.mult))
                ch(tt(o_[1], x_[1], b_(y_[0]), ALU.mult))
                ch(tt(t[1], x_[0], b_(y_[1]), ALU.mult))
                ch.wait()
                ch(tt(o_[0], o_[0], t[0], ALU.subtract))
                ch(tt(o_[1], o_[1], t[1], ALU.add))
                ch.wait()

            lp = lambda q: (LP[:, 0, q, :], LP[:, 1, q, :])
            ch(pool.memset(LP[:, 0, 0, :], 1.0))
            ch(pool.memset(LP[:, 1, 0, :], 0.0))
            ch(tt(LP[:, 0, 1, :], mag, c1, ALU.mult))
            ch(tt(LP[:, 1, 1, :], mag, s1, ALU.mult))
            ch.wait()
            tm = (tmp[15], tmp[16])
            cmul(lp(2), lp(1), lp(1), tm)
            cmul(lp(3), lp(2), lp(1), tm)
            cmul(lp(4), lp(2), lp(2), tm)
            for q in range(1, 5):
                cmul(lp(4 + q), lp(4), lp(q), tm)
            ch.step(tt(tmp[17], mag, mag, ALU.mult))
            ch.step(tt(tmp[17], tmp[17], tmp[17], ALU.mult))
            ch.step(tt(r8[:, :], tmp[17], tmp[17], ALU.mult))
            cmul((tmp[18], tmp[19]), (c1, s1), (c1, s1), tm)
            cmul((tmp[20], tmp[21]), (tmp[18], tmp[19]), (tmp[18], tmp[19]), tm)
            z = lambda i: (zp[:, i, 0, :], zp[:, i, 1, :])
            cmul(z(0), (tmp[20], tmp[21]), (tmp[20], tmp[21]), tm)
            for i in range(6):
                cmul(z(i + 1), z(i), z(i), tm)
            nr, _, den, qr, qi = tmp[22:27]
            ch(ts(nr, LP[:, 0, 1, :], -1.0, None, ALU.add))
            ch.wait()
            pool.wait_ge(den_ready, 1)
            ch(tt(dm(qr), dm(nr), lre, ALU.mult))
            ch(tt(dm(tmp[28]), dm(LP[:, 1, 1, :]), lim, ALU.mult))
            ch(tt(dm(qi), dm(LP[:, 1, 1, :]), lre, ALU.mult))
            ch(tt(dm(tmp[29]), dm(nr), lim, ALU.mult))
            ch.wait()
            ch(tt(qr, qr, tmp[28], ALU.add))
            ch(tt(qi, qi, tmp[29], ALU.subtract))
            ch.wait()
            ch(tt(qr, qr, den, ALU.mult))
            ch(tt(qi, qi, den, ALU.mult))
            pool.wait_ge(b_in, 32)
            ch.wait()
            sh = [P, NP, GC]
            for d in range(2):
                re_, im_ = BB[:, 0, d], BB[:, 1, d]
                q0, q1 = dm(qr)[:, d, :, None].to_broadcast(sh), dm(qi)[:, d, :, None].to_broadcast(sh)
                ch(tt(re_, Bld[:, 0], q0, ALU.mult))
                ch(tt(bbt[:, 0], Bld[:, 1], q1, ALU.mult))
                ch(tt(im_, Bld[:, 1], q0, ALU.mult))
                ch(tt(bbt[:, 1], Bld[:, 0], q1, ALU.mult))
                ch.wait()
                ch(tt(re_, re_, bbt[:, 0], ALU.subtract))
                ch.step(tt(im_, im_, bbt[:, 1], ALU.add))
                ins = ts(im_, im_, -1.0)
                ch.step(ins)

            pool.wait_ge(ct_ready, NB)

            def mul(o_, x_, y_, shape):
                ch(pool.tensor_tensor(o_, x_.to_broadcast(shape), y_.to_broadcast(shape), ALU.mult))

            def turn(d, part, pairs, forward):
                v = LP[:, part, 0:9, :].rearrange("p q (d m) -> p d m q", d=2)[:, d, pairs, :]
                return (v if forward else v[:, :, ::-1])

            for b in range(NB):
                pairs = slice(PB * b, PB * b + PB)
                if b >= 1:
                    pool.wait_ge(bp_T, b)
                for d in range(2):
                    sh = [P, PB, 8, GC]
                    br, bi = BB[:, 0, d, pairs, :][:, :, None, :], BB[:, 1, d, pairs, :][:, :, None, :]
                    if d == 0:
                        lr, li = turn(0, 0, pairs, True)[:, :, 0:8], turn(0, 1, pairs, True)[:, :, 0:8]
                    else:
                        lr, li = turn(1, 0, pairs, False)[:, :, 1:9], turn(1, 1, pairs, False)[:, :, 1:9]
                    lr, li = lr[:, :, :, None], li[:, :, :, None]
                    re = BP[:, 0, d].rearrange("p m (q c) -> p m q c", c=GC)
                    im = BP[:, 1, d].rearrange("p m (q c) -> p m q c", c=GC)
                    t1 = pt1[:, :].rearrange("p (m q c) -> p m q c", m=PB, c=GC)
                    mul(re, br, lr, sh)
                    mul(t1, bi, li, sh)
                    ch.wait()
                    ch(pool.tensor_tensor(re, re, t1, ALU.add))
                    ch.wait()
                    mul(im, bi, lr, sh)
                    mul(t1, br, li, sh)
                    ch.wait()
                    pool.tensor_tensor(im, im, t1, ALU.subtract).then_inc(bp_ready, 1)
                    pool.wait_ge(bp_ready, 2 * b + d + 1)
                if b >= 1:
                    pool.wait_ge(t_mm, b)
                    pool.wait_ge(y_mm, b)
                for g2 in range(2):
                    half = slice(64 * g2, 64 * g2 + 64)
                    ch.step(pool.tensor_copy(bbd[half, :, :, :, GC * g2:GC * g2 + GC].rearrange("p r d m c -> p (r d) m c"),
                                        BB[half, :, :, pairs, :].rearrange("p r d m c -> p (r d) m c")))
                for d in range(2):
                    for hp in range(2):
                        sh = [P, 2, 9, GC]
                        two = slice(PB * b + 2 * hp, PB * b + 2 * hp + 2)
                        cr, ci = CT[:, d, 0, two, :][:, :, None, :], CT[:, d, 1, two, :][:, :, None, :]
                        lr, li = turn(d, 0, two, d == 0)[:, :, :, None], turn(d, 1, two, d == 0)[:, :, :, None]
                        re = CP[:, 0, d, 2 * hp:2 * hp + 2].rearrange("p m (q c) -> p m q c", c=GC)
                        im = CP[:, 1, d, 2 * hp:2 * hp + 2].rearrange("p m (q c) -> p m q c", c=GC)
                        t1 = pt1[:, 0:288].rearrange("p (m q c) -> p m q c", m=2, c=GC)
                        mul(re, cr, lr, sh)
                        mul(t1, ci, li, sh)
                        ch.wait()
                        ch(pool.tensor_tensor(re, re, t1, ALU.subtract))
                        ch.wait()
                        mul(im, cr, li, sh)
                        mul(t1, ci, lr, sh)
                        ch.wait()
                        last = pool.tensor_tensor(im, im, t1, ALU.add)
                        if hp == 0:
                            ch.step(last)
                        else:
                            last.then_inc(cp_ready, 1)
                    pool.wait_ge(cp_ready, 2 * b + d + 1)
                pool.wait_ge(cp_ready, 2 * b + 2)
                if b >= 1:
                    pool.wait_ge(state_ready, 2 * b)
                ch(pool.memset(E[:, 0, :, 0:1], 1.0))
                ch(pool.memset(E[:, 1, :, 0:1], 0.0))
                ch.wait()
                at_, i = 1, 0
                while at_ < NK:
                    n = min(at_, NK - at_)
                    z = [zp[:, i, r, :].rearrange("p (d m) -> p d m", d=2)[:, :, pairs] for r in range(2)]
                    sh = [P, 2, PB, n]
                    e = [E[:, r, :, :].rearrange("p (d m) k -> p d m k", d=2) for r in range(2)]
                    t1 = pt1[:, 0:8 * n].rearrange("p (d m k) -> p d m k", d=2, m=PB)
                    new = slice(at_, at_ + n)
                    mul(e[0][:, :, :, new], e[0][:, :, :, 0:n], z[0][:, :, :, None], sh)
                    mul(t1, e[1][:, :, :, 0:n], z[1][:, :, :, None], sh)
                    ch.wait()
                    ch(pool.tensor_tensor(e[0][:, :, :, new], e[0][:, :, :, new], t1, ALU.subtract))
                    ch.wait()
                    mul(e[1][:, :, :, new], e[1][:, :, :, 0:n], z[0][:, :, :, None], sh)
                    mul(t1, e[0][:, :, :, 0:n], z[1][:, :, :, None], sh)
                    ch.wait()
                    last = pool.tensor_tensor(e[1][:, :, :, new], e[1][:, :, :, new], t1, ALU.add)
                    at_ += n
                    i += 1
                    if at_ < NK:
                        ch(last)
                        ch.wait()
                    else:
                        last.then_inc(e_ready, 1)
                        pool.wait_ge(e_ready, b + 1)
            pool.wait_ge(tile_done, TILE0["ukv"] + 12)
            for t in range(16):
                m = 8 + t if t < 8 else t - 8
                if t >= 4:
                    if t < 12:
                        pool.wait_ge(s_ready, t - 3)
                    else:
                        pool.wait_ge(mg_f, t - 11)
                if t == 8:
                    pool.wait_ge(s_ready, 8)
                if t == 0:
                    for i in range(2):
                        pool.wait_ge(gate_out[i], 16 * 8)
                pool.dma_start(gload[t % 4][:, :], gate_dram[m]).then_inc(gload_in[t % 4], 16)

        @block.scalar
        def _(act):
            ch = Chain(act, act_chain)
            for r, name in enumerate(("c", "c_ctx")):
                act.dma_start(ccld[:, r, :], a[name].rearrange("(p k) -> p k", k=KD)).then_inc(ccld_in, 16)
            for r, w, name in ((V_BMOD, 48, "b_mod"), (V_N1, 8, "norm1_g"), (V_N2, 8, "norm2_g"), (V_DSKIP, 4, "d_skip"),
                               (V_QAG, 3, "q_a_g"), (V_KVAG, 2, "kv_a_g")):
                act.dma_start(rowsA[r:r + w, :], a[name].rearrange("(r n) -> r n", n=P)).then_inc(params_in, 16)
            act.dma_start(rowsB[:, :], a["conv_w"][0:2, :].rearrange("w (r n) -> (w r) n", n=P)).then_inc(params_in, 16)
            act.dma_start(rowsC[0:44, :], a["conv_w"][2, :].rearrange("(r n) -> r n", n=P)).then_inc(params_in, 16)
            act.dma_start(rowsC[44:88, :], a["conv_b"].rearrange("(r n) -> r n", n=P)).then_inc(params_in, 16)
            for i, name in enumerate(("lam_re_f", "lam_im_f", "lam_re_b", "lam_im_b")):
                act.dma_start(rowsL[16 * i:16 * i + 16, :], a[name].rearrange("(m g) n -> m (g n)", g=2)).then_inc(params_in, 16)
            for i, name in enumerate(("log_dt_f", "log_dt_b")):
                act.dma_start(ldt[16 * i:16 * i + 16, :], a[name].rearrange("(m g) -> m g", g=2)).then_inc(lamv_in, 16)
            for i, name in enumerate(("b_re", "b_im")):
                act.dma_start(Bld[:, i], a[name].rearrange("(m g) n c -> (g n) m c", g=2)).then_inc(b_in, 16)
            for i, name in enumerate(("c_re_f", "c_im_f", "c_re_b", "c_im_b")):
                for dup in range(2):
                    act.dma_start(ctile[:, i, :, dup, :], a[name].rearrange("(b g) c n -> (g c) b n", b=NB)).then_inc(c_in, 16)

            act.wait_ge(ccld_in, 32)
            act.activation(cs[:, :, :].rearrange("p k r -> p r k"), ccld[:, :, :], ACT.Silu).then_inc(cs_ready, 1)
            def sum_squares(t, src):
                return act.activation(junk[:, :], src, ACT.Square, accum_out=stv[:, t:t + 1])

            act.wait_ge(x_in, 16)
            for t in range(TT_N):
                ch.step(sum_squares(t, xtok[:, t, :]))
            for k in range(KD):
                act.wait_ge(xT_mm, k + 1)
                act.activation(xT[:, k, :], bank[k % 6][:, :], ACT.Copy).then_inc(xT_ready, 1)
            act.wait_ge(vec_T, 1)
            act.activation(VEC[:, :], bank[6][:, 0:V_END], ACT.Copy).then_inc(vec_ready, 1)
            act.wait_ge(ctx_in, 16)
            ch.step(sum_squares(4, ctok[:, 0, :]))
            sum_squares(5, ctok[:, 1, :]).then_inc(sumsq1, 1)
            act.wait_ge(rstd1_mm, 1)
            act.activation(rstdb[:, C:], bank[6][:, :], ACT.Copy).then_inc(rstd1_ready, 1)
            act.activation(rstdb[:, 0:C], bank[0][:, 0:C], ACT.Copy).then_inc(rstd1_ready, 1)
            act.wait_ge(sin_arg, 1)
            act.activation(TMP[:, 10:12, :], TMP[:, 8:10, :], ACT.Sin).then_inc(sin_done, 1)
            for b in range(NB):
                act.wait_ge(ct_T, b + 1)
                for g2 in range(2):
                    half = slice(64 * g2, 64 * g2 + 64)
                    ins = act.activation(CT[half, :, :, PB * b:PB * b + PB, :].rearrange("p d r m c -> p (d r) m c"),
                                         bank[4 + b % 2][half, :].rearrange("p (a m g c) -> p a m g c", a=4, m=PB, g=2)[:, :, :, g2, :],
                                         ACT.Copy)
                    ins.then_inc(ct_ready if g2 else ct2_ready, 1)

            split_hi(act, 0)
            act.wait_ge(gain1_ready, 2)
            act.wait_ge(xn_ready, KD)
            for k in range(KD):
                if k >= 2:
                    act.wait_ge(h_split, k - 1)
                ch(act.activation(hf[k % 2][:, C:], xn[:, k, :], ACT.Identity, scale=gain1[:, 0, k:k + 1], bias=modb[:, k, 0:1]))
                ch(act.activation(h_hi[:, k, :], xn[:, k, :], ACT.Identity, scale=gain1[:, 0, k:k + 1], bias=modb[:, k, 0:1]))
                act.activation(hf[k % 2][:, 0:C], cn[:, k, :], ACT.Identity, scale=gain1[:, 1, k:k + 1],
                               bias=modb[:, k, 1:2]).then_inc(hf_ready, 1)
            split_hi(act, 1)

            def tile_to(dst, src, t, func=ACT.Copy):
                act.wait_ge(tile_done, t + 1)
                act.activation(dst, src, func).then_inc(tile_free, 1)

            t0 = TILE0["lat"]
            lat_tiles = [(cq[:, 0, :], 512), (cq[:, 1, :], 512), (cq[:, 2, :], 512), (ckv[:, 0, C:], 512), (ckv[:, 0, 0:C], C),
                         (ckv[:, 1, C:], 512), (ckv[:, 1, 0:C], C), (krT[:, C:], 512), (krT[:, 0:C], C)]
            for t, (dst, w) in enumerate(lat_tiles):
                if t in (2, 5):
                    split_hi(act, S_OF["lat"][0] + (2 if t == 2 else 3))
                tile_to(dst, bank[(t0 + t) % 2 + 6][0:ROPE if t >= 7 else P, 0:w], t0 + t)
            act.wait_ge(tile_free, t0 + 9)
            act.activation(sqq[:, :, :], cq[:, :, :], ACT.Square).then_inc(latsq, 1)
            act.activation(sqk[:, :, :], ckv[:, :, :], ACT.Square).then_inc(latsq, 1)

            t0 = TILE0["u"]
            for t in range(12):
                if t % 6 == 0:
                    split_hi(act, S_OF["u"][0] + 1 + t // 6)
                if t >= 4:
                    act.wait_ge(u_out[t % 4], 16 * (t // 4))
                act.wait_ge(tile_done, t0 + t + 1)
                act.activation(ust[t % 4][:, :], bank[(t0 + t) % 2 + 6][:, 0:256], ACT.Copy).then_inc(tile_free, 1)
                act.wait_ge(tile_free, t0 + t + 1)
                act.dma_start(u_dram[P * (t % 6):P * (t % 6) + P, 256 * (t // 6):256 * (t // 6) + 256],
                              ust[t % 4][:, :]).then_inc(u_out[t % 4], 16)

            def group_order(b):
                act.activation(utok[0:NK, b, :].rearrange("p (g j c) -> p g j c", g=GB, j=L),
                               ustage[0:NK, :, P * b:P * b + P].rearrange("p j (g c) -> p g j c", c=GC),
                               ACT.Copy).then_inc(ug_A, 1)

            act.wait_ge(kr_T, 1)
            act.activation(kr[:, :, :].rearrange("p t r -> p (t r)"), bank[5][:, 0:6 * ROPE], ACT.Copy).then_inc(kr_ready, 1)
            act.wait_ge(utok_in, 16 * L)
            act.wait_ge(rstd2_mm, 1)
            group_order(1)
            group_order(3)

            def gate_tile(m, t):
                if m >= 2:
                    act.wait_ge(gate_out[m % 2], 16 * (m // 2))
                act.wait_ge(tile_done, t + 1)
                act.activation(gst[m % 2][:, :], bank[6 + t % 2][:, :], ACT.Sigmoid).then_inc(tile_free, 1)
                act.wait_ge(tile_free, t + 1)
                act.dma_start(gate_dram[m], gst[m % 2][:, :]).then_inc(gate_out[m % 2], 16)

            for b in range(NB):
                t = TILE0["gate"] + 4 * b
                for i in range(2):
                    act.wait_ge(u_T, 2 * b + 1 + i)
                    act.activation(U[:, 4 * i:4 * i + 4, :].rearrange("p g k -> p (g k)"), bank[i][:, 0:4 * NK], ACT.Copy).then_inc(u_evacA, 1)
                act.wait_ge(bp_T, b + 1)
                for d in range(2):
                    act.activation(WinT[:, 0, d].rearrange("p m n -> p (m n)"), bank[2 + d][:, :], ACT.Copy).then_inc(winT_A, 1)
                gate_tile(4 * b, t)
                gate_tile(4 * b + 1, t + 1)
                split_hi(act, S_OF["gate"][2 * b] + 1)
                act.wait_ge(kf_ready, b + 1)
                act.dma_start(kf_dram[b], Kf[:, :]).then_inc(kf_out, 16)
                gate_tile(4 * b + 2, t + 2)
                act.wait_ge(kf_out, 16 * b + 16)
                for j in range(L):
                    act.dma_start(TTm[GC * j:GC * j + GC, :, :],
                                  kf_dram[b].rearrange("(g c) m -> c g m", c=GC)[:, :, GC * j:GC * j + P]).then_inc(tt_in, 16)
                gate_tile(4 * b + 3, t + 3)
                split_hi(act, S_OF["gate"][2 * b] + 2)
                act.wait_ge(y_mm, b + 1)
                act.activation(Ysb[:, :, :].rearrange("p g k -> p (g k)"), bank[0][:, :], ACT.Copy).then_inc(y_evac, 1)
                act.wait_ge(y_T, b + 1)
                act.activation(ytok[:, :, 0:64].rearrange("p j (g c) -> p g j c", c=GC),
                               bank[1][0:64, :].rearrange("p (g j c) -> p g j c", g=4, j=L), ACT.Copy).then_inc(ytok_A, 1)
                act.wait_ge(y_T2, b + 1)
                act.activation(utok[:, b, 0:L * CK].rearrange("p (j k) -> p j k", j=L), bank[3][:, :].rearrange("p (j k) -> p j k", j=L),
                               ACT.Gelu_apprx_tanh).then_inc(gelu_done, 1)

            for i in range(2):
                act.wait_ge(gate_out[i], 16 * 8)
            for r, name in enumerate(("q_norm_g", "k_norm_g")):
                act.dma_start(qkg[:, r, :], a[name].rearrange("(o n) -> o n", o=1).to_broadcast([P, QK])).then_inc(attn_consts_in, 16)
            act.dma_start(rope[:, :, :], a["rope"].rearrange("(t p) n -> p t n", p=P)).then_inc(attn_consts_in, 16)
            act.wait_ge(cp_ready, 2 * NB)
            act.wait_ge(e_ready, NB)
            act.activation(cq_hi[:, :, :], cq[:, :, :], ACT.Copy).then_inc(prep_hi, 1)
            act.activation(ckv_hi[:, :, :], ckv[:, :, :], ACT.Copy).then_inc(prep_hi, 1)
            act.wait_ge(gelu_done, NB)
            for b in range(NB):
                act.activation(y_hi[:, b, :].rearrange("p (k j) -> p j k", j=L), utok[:, b, 0:L * CK].rearrange("p (j k) -> p j k", j=L),
                               ACT.Copy).then_inc(yprep_hi, 1)

            t0 = TILE0["uq"]
            for t in range(8):
                if t % 4 == 0:
                    split_hi(act, S_OF["uq"][0] + 1 + t // 4)
                if t >= 2:
                    act.wait_ge(sq_used, t - 1)
                act.wait_ge(tile_done, t0 + t + 1)
                act.activation(sqt[t % 2][:, 0:384], bank[6 + (t0 + t) % 2][:, 0:384], ACT.Square).then_inc(q_sq, 1)
                act.activation(qsb[:, t % 4, 4 * (t // 4):4 * (t // 4) + 4, :].rearrange("p h d -> p (h d)"),
                               bank[6 + (t0 + t) % 2][:, 0:384], ACT.Copy).then_inc(tile_free, 1)
            t0 = TILE0["ukv"]
            split_hi(act, S_OF["glu"][0])
            for t in range(12):
                act.wait_ge(sq_used, 8 + t - 1)
                act.wait_ge(tile_done, t0 + t + 1)
                nope = bank[6 + (t0 + t) % 2][:, :].rearrange("p (h e) -> p h e", h=4)[:, :, 0:NOPE]
                act.activation(sqt[t % 2][:, 0:256].rearrange("p (h e) -> p h e", h=4), nope, ACT.Square).then_inc(q_sq, 1)
                act.activation(ksb[:, t // 2, 4 * (t % 2):4 * (t % 2) + 4, 0:NOPE], nope, ACT.Copy).then_inc(tile_free, 1)

            s0 = S_OF["glu"][0]

            def split_hi_at(s_first, k, i, rounds, wait_sem, wait_value):
                s = s_first + k
                n = N_OF_SPLIT[s]
                act.wait_ge(raw_in[n % 2], raw_in_count(n) + 16 * transfers(STREAM[n]) * (rounds // 2) * i)
                act.wait_ge(wait_sem, wait_value)
                w = width(STREAM[n], n - N_OF[STREAM[n]][0])
                act.activation(whi[s % 2][:, 0:w], raw[n % 2][:, 0:w], ACT.Copy).then_inc(hi_ready, 1)

            t0 = TILE0["glu"]
            for p in range(4):
                split_hi(act, s0 + p + 1)
                for mi in range(2):
                    m = 2 * p + mi
                    act.wait_ge(tile_done, t0 + 2 * m + 2)
                    if m >= 2:
                        act.wait_ge(s_ready, m - 1)
                    act.activation(sg[m % 2][:, :], bank[4 + (2 * m + 1) % 4][:, :], ACT.Sigmoid).then_inc(sg_ready, 1)

            for i in range(0, 24, 2):
                act.wait_ge(qk_T, i + 1)
                dst, w = qk_tile(i)
                act.activation(dst, bank[i % 4][0:QK, 0:w], ACT.Copy).then_inc(qk_A, 1)

            split_hi(act, S_OF["wo"][1])

            def exp(i):
                act.wait_ge(max_ready, i + 1)
                if i >= 2:
                    act.wait_ge(p_T, 2 * (i - 2) + 2)
                act.activation(Pm[i % 2][:, :], ps[:, 2 * (i % 2):2 * (i % 2) + 2, 0:384], ACT.Exp, scale=SCALE,
                               bias=smx[:, i % 4, 1:2], accum_out=smx[:, i % 4, 2:3]).then_inc(exp_ready, 1)

            exp(0)
            for i in range(4 * H):
                act.wait_ge(p_T, 2 * i + 2)
                if i >= 2:
                    act.wait_ge(o_mm, i - 1)
                act.activation(PT[i % 2][:, 3:6, :].rearrange("p a b -> p (a b)"), bank[5][:, 0:384], ACT.Copy).then_inc(pt_A, 1)
                if i + 1 < 4 * H:
                    exp(i + 1)
            for k in range(4):
                act.wait_ge(o_T, k + 1)
                act.activation(oT_hi[:, k, :], bank[k][:, :], ACT.Copy).then_inc(oT_hi_r, 1)
            for m in range(KD):
                if m == 4:
                    split_hi(act, S_OF["wout"][0])
                act.wait_ge(mg_f, m + 1)
                act.activation(mg_hi[:, m, :], mgf[m % 2][:, :], ACT.Copy).then_inc(mg_h, 1)

            for p in range(4):
                split_hi(act, S_OF["wout"][p] + 1)
                for mi in range(2):
                    m = 2 * p + mi
                    act.wait_ge(x1_ready, m + 1)
                    act.activation(sqx[:, m, :], xT[:, m, :], ACT.Square).then_inc(sqx_ready, 1)
            for k in range(KD):
                act.wait_ge(nx_ready, k + 1)
                if k >= 2:
                    act.wait_ge(h2_l, k - 1)
                act.activation(nh[k % 2][:, :], nx[k % 2][:, :], ACT.Identity, scale=gain2[:, k:k + 1],
                               bias=modb[:, 24 + k, 0:1]).then_inc(nh_ready, 1)
                act.wait_ge(nh_ready, k + 1)
                act.activation(h2_hi[:, k, :], nh[k % 2][:, :], ACT.Copy).then_inc(h2_h, 1)

            s0, t0 = S_OF["up"][0], TILE0["up"]

            def up_round(i, j, more):
                f = 2 * i + j
                if more:
                    split_hi_at(s0 + 1, j, i, 2, tile_done, t0 + 4 * i + 2 * j)
                for v in range(2):
                    act.wait_ge(tile_done, t0 + 4 * i + 2 * j + v + 1)
                    act.activation(cv[v][j][:, :], bank[4 + 2 * j + v][:, :], ACT.Identity,
                                   scale=VEC[:, bass.ds(V_W1 + 22 * v + f, 1)],
                                   bias=VEC[:, bass.ds(V_CB + 22 * v + f, 1)]).then_inc(cv_a, 1)
                act.wait_ge(cv_d, 4 * i + 2 * j + 2)
                act.activation(sl[j][:, :], cv[1][j][:, :], ACT.Silu).then_inc(silu_done, 1)
                act.wait_ge(act_f, f + 1)
                act.activation(act_hi[:, bass.ds(f, 1), :], cv[0][j][:, None, :], ACT.Copy).then_inc(act_h, 1)

            up_round(0, 0, True)
            up_round(0, 1, True)
            with act.Fori(1, 10) as i:
                for j in range(2):
                    up_round(i, j, True)
            up_round(10, 0, True)
            split_hi(act, S_OF["down"][0])
            up_round(10, 1, False)

            s0, t0 = S_OF["down"][0], TILE0["down"]

            def rows_out(pair, par):
                for mi in range(2):
                    act.wait_ge(xo_T, 2 * pair + mi + 1)
                    act.activation(ost[par][:, :, P * mi:P * mi + P],
                                   bank[2 * par + mi][:, :].rearrange("p (t n) -> p t n", t=TT_N),
                                   ACT.Copy).then_inc(ost_ready if mi else act_chain, 1)

            for p in range(11):
                split_hi(act, s0 + 1 + p)
                if p in (4, 7, 10):
                    pair = p // 3 - 1
                    if pair >= 2:
                        act.wait_ge(out_done[pair % 2], 16 * (pair // 2))
                    rows_out(pair, pair % 2)
            act.wait_ge(out_done[1], 16)
            rows_out(3, 1)

        @block.vector
        def _(dve):
            ch = Chain(dve, dve_chain)
            V_ = dve

            def tt(o_, x_, y_, op):
                return V_.tensor_tensor(o_, x_, y_, op)

            def ts(o_, x_, s1, s2=None, op0=ALU.mult, op1=ALU.add):
                if s2 is None:
                    return V_.tensor_scalar(o_, x_, s1, None, op0)
                return V_.tensor_scalar(o_, x_, s1, s2, op0, op1)

            def stt_(o_, x_, s, y_, op0, op1):
                return V_.scalar_tensor_tensor(out=o_, in0=x_, scalar=s, in1=y_, op0=op0, op1=op1)

            def rsqrt(y, v, t):
                ch.step(ts(y.bitcast(I32), v.bitcast(I32), -0.5, 1597463007.0))
                for _ in range(3):
                    ch.step(stt_(t, y, -0.5, y, ALU.mult, ALU.mult))
                    ch.step(tt(t, t, v, ALU.mult))
                    ch.step(stt_(y, t, 1.5, y, ALU.add, ALU.mult))

            V_.wait_ge(lamv_in, 32)
            V_.tensor_copy(rowsT[:, :].rearrange("r (g n) -> r g n", g=2),
                           ldt[:, :, None].to_broadcast([32, 2, NS])).then_inc(ldt_wide, 1)
            V_.wait_ge(consts_ready, 1)
            ch.step(V_.tensor_reduce(dmask[:, :], ident[:, :].rearrange("p (g c) -> p c g", c=GC), AX.X, ALU.add))

            def mod_panel(w, acc, r):
                for k in range(KD):
                    if k == 0:
                        ch.step(ts(acc, w[:, k, :], cs[:, k, r:r + 1]))
                    elif k < KD - 1:
                        ch.step(stt_(acc, w[:, k, :], cs[:, k, r:r + 1], acc, ALU.mult, ALU.add))
                    else:
                        return stt_(acc, w[:, k, :], cs[:, k, r:r + 1], acc, ALU.mult, ALU.add)

            def mod1_panel(i, buf, signal, value):
                V_.wait_ge(signal, value)
                w = buf[:, :].rearrange("p (k n) -> p k n", k=KD)
                ch(mod_panel(w, macc1[:, i, 0, :], 0))
                mod_panel(w, macc1[:, i, 1, :], 1).then_inc(mod1_dve, 1)

            V_.wait_ge(cs_ready, 1)
            mod1_panel(0, raw[1], raw_in[1], 16)
            mod1_panel(1, early[1], early_in[1], 16)
            V_.wait_ge(sumsq1, 1)
            ch.step(ts(stv[:, 0:6], stv[:, 0:6], 1.0 / D, EPS))
            rsqrt(sty[:, 0:6], stv[:, 0:6], stt[:, 0:6])
            for t in range(6):
                ts(diag[:, t, :], ident[:, :], sty[:, t:t + 1]).then_inc(diag1_ready, 1)

            V_.wait_ge(vec_ready, 1)
            dm = lambda v: v.rearrange("p (d m) -> p d m", d=2)
            lam = VEC[:, V_LAM:V_LAM + 64].rearrange("p (d r m) -> p r d m", d=2, r=2)
            ch(tt(dm(TMP[:, 24, :]), lam[:, 0], lam[:, 0], ALU.mult))
            ch(tt(dm(TMP[:, 30, :]), lam[:, 1], lam[:, 1], ALU.mult))
            ch.wait()
            ch.step(tt(TMP[:, 24, :], TMP[:, 24, :], TMP[:, 30, :], ALU.add))
            V_.reciprocal(TMP[:, 24, :], TMP[:, 24, :]).then_inc(den_ready, 1)
            mod1_panel(2, early[3], early_in[3], 16)
            mod1_panel(3, raw[1], raw_in[1], 32)

            V_.wait_ge(rstd1_ready, 2)
            for k in range(4):
                V_.wait_ge(xT_mm, KD + k + 1)
                tt(cn[:, 2 * k:2 * k + 2, :], bank[(KD + k) % 6][:, :].rearrange("p (a t) -> p a t", a=2),
                   rstdb[:, None, 0:C].to_broadcast([P, 2, C]), ALU.mult).then_inc(xn_ready, 1)
            for k in range(KD):
                V_.wait_ge(xT_ready, k + 1)
                tt(xn[:, k, :], xT[:, k, :], rstdb[:, C:], ALU.mult).then_inc(xn_ready, 1)
            V_.wait_ge(mod1_mm, 1)
            V_.wait_ge(vec_ready, 1)
            ch.step(tt(modb[:, 0:16, :], bank[7][:, 0:32].rearrange("p (m r) -> p m r", r=2),
                       VEC[:, V_BMOD:V_BMOD + 16, None].to_broadcast([P, 16, 2]), ALU.add))
            for r in range(2):
                stt_(gain1[:, r, :], modb[:, 8:16, r], 1.0, VEC[:, V_N1:V_N1 + 8], ALU.add, ALU.mult).then_inc(gain1_ready, 1)
            split_lo(dve, 0)
            for k in range(KD):
                V_.wait_ge(hf_ready, k + 1)
                ch(V_.tensor_copy(hc_hi[:, k, :], hf[k % 2][:, 0:C]))
                ch.wait()
                ch(tt(h_lo[:, k, :], hf[k % 2][:, C:], h_hi[:, k, :].bitcast(F32), ALU.subtract))
                tt(hc_lo[:, k, :], hf[k % 2][:, 0:C], hc_hi[:, k, :].bitcast(F32), ALU.subtract).then_inc(h_split, 1)
            split_lo(dve, 1)
            split_lo(dve, 2)
            split_lo(dve, 3)
            split_lo(dve, 4)
            V_.wait_ge(lat_stat, 1)
            ch(ts(stv[:, 0:4], bank[0][:, 0:4], 1.0 / QL, EPS))
            ch(ts(stv[:, 4:10], bank[0][:, 4:10], 1.0 / KVL, EPS))
            ch.wait()
            rsqrt(sty[:, 0:10], stv[:, 0:10], stt[:, 0:10])
            for t in range(10):
                ts(diag2[:, t, :], ident[:, :], sty[:, t:t + 1]).then_inc(diag2_ready, 1)
            split_lo(dve, 5)
            V_.wait_ge(rstd2_mm, 1)
            for k in range(3):
                ch(stt_(cq[:, k, :], cq[:, k, :], VEC[:, V_QAG + k:V_QAG + k + 1], bank[1][:, :], ALU.mult, ALU.mult))
            for k in range(2):
                ch(stt_(ckv[:, k, 0:512], ckv[:, k, 0:512], VEC[:, V_KVAG + k:V_KVAG + k + 1], bank[2][:, :], ALU.mult, ALU.mult))
                ins = stt_(ckv[:, k, 512:], ckv[:, k, 512:], VEC[:, V_KVAG + k:V_KVAG + k + 1], bank[3][:, 0:256], ALU.mult, ALU.mult)
                if k == 0:
                    ch(ins)
                else:
                    ins.then_inc(lat_normed, 1)

            V_.wait_ge(tile_done, TILE0["u"] + 12)
            V_.wait_ge(utok_in, 16 * L)
            V_.wait_ge(rstd2_mm, 1)
            for b in (0, 2):
                V_.tensor_copy(utok[0:NK, b, :].rearrange("p (g j c) -> p g j c", g=GB, j=L),
                               ustage[0:NK, :, P * b:P * b + P].rearrange("p j (g c) -> p g j c", c=GC)).then_inc(ug_D, 1)
            V_.wait_ge(ug_A, 2)
            V_.wait_ge(ug_D, 2)
            for r in range(2):
                V_.memset(SBD[r][0:64, :, :, 1, :], 0.0).then_inc(sbd_zero, 1)
                V_.memset(SBD[r][64:128, :, :, 0, :], 0.0).then_inc(sbd_zero, 1)
            for b in range(NB):
                for i in range(2):
                    V_.wait_ge(u_evacA, 2 * b + 1 + i)
                    src = U[:, 4 * i:4 * i + 4, :]
                    ch(V_.tensor_copy(Ub[:, 4 * i:4 * i + 4, 0:CC], src[:, :, CC - 1::-1]))
                    V_.tensor_copy(Ub[:, 4 * i:4 * i + 4, CC:], src[:, :, NK - 1:CC - 1:-1]).then_inc(u_evacD, 1)
                V_.wait_ge(bp_T, b + 1)
                for d in range(2):
                    V_.tensor_copy(WinT[:, 1, d].rearrange("p m n -> p (m n)"), bank[4 + d][:, :]).then_inc(winT_D, 1)
                for q in range(4):
                    n = N_OF["mod2"][4 * b + q]
                    V_.wait_ge(raw_in[n % 2], raw_in_count(n))
                    mod_panel(raw[n % 2][:, :].rearrange("p (k n) -> p k n", k=KD),
                              utok[:, b, 256 * q:256 * q + 256], 0).then_inc(mod2_used, 1)
                split_lo(dve, S_OF["gate"][2 * b] + 1)
                V_.wait_ge(t_mm, b + 1)
                if b:
                    V_.wait_ge(kf_out, 16 * b)
                ch(V_.tensor_copy(Kf[:, 0:P], bank[1][:, 0:P]))
                ch(V_.tensor_copy(Kf[:, P:], bank[0][:, GC:P]))
                ch.wait()
                ch(tt(modb[:, 16 + 8 * b:24 + 8 * b, 0], bank[0][:, 256:264], VEC[:, V_BMOD + 16 + 8 * b:V_BMOD + 24 + 8 * b], ALU.add))
                ch.step(tt(Kf[:, P - GC:P], bank[0][:, 0:GC], Kf[:, P - GC:P], ALU.add))
                stt_(Kf[:, P - GC:P], dmask[:, :], VEC[:, V_DSKIP + b:V_DSKIP + b + 1], Kf[:, P - GC:P],
                     ALU.mult, ALU.add).then_inc(kf_ready, 1)
                V_.wait_ge(e_ready, b + 1)
                if b:
                    V_.wait_ge(y_T2, b)
                for d in range(2):
                    V_.wait_ge(v_mm, 2 * b + 1 + d)
                    if d:
                        V_.wait_ge(kf_out, 16 * b + 16)
                    vr, vi = (bank[2 + 2 * r + d][:, 0:4 * NK].rearrange("p (m k) -> p m k", m=PB) for r in range(2))
                    ec, es = E[:, 0, 4 * d:4 * d + 4, :], E[:, 1, 4 * d:4 * d + 4, :]
                    ch(tt(W[:, 0, d], vr, ec, ALU.mult))
                    ch(tt(tmpA[:, :, :], vi, es, ALU.mult))
                    ch(tt(W[:, 1, d], vi, ec, ALU.mult))
                    tt(tmpB[:, :, :], vr, es, ALU.mult).then_inc(v_read, 1)
                    V_.wait_ge(v_read, 2 * b + 1 + d)
                    ch.wait()
                    ch(tt(W[:, 0, d], W[:, 0, d], tmpA[:, :, :], ALU.subtract))
                    ch(tt(W[:, 1, d], W[:, 1, d], tmpB[:, :, :], ALU.add))
                    ch.wait()
                    for r in range(2):
                        for m in range(PB):
                            col = 16 * d + PB * b + m
                            w = W[:, r, d, m, :]
                            ch(V_.tensor_tensor_scan(w, r8[:, col:col + 1].to_broadcast([P, NK]), w, 0.0, ALU.mult, ALU.add))
                    ch.wait()
                    at_ = slice(CC - 1, NK - 1) if d == 0 else slice(NK - 2, CC - 2, -1)
                    wr, wi, ec, es = W[:, 0, d][:, :, at_], W[:, 1, d][:, :, at_], ec[:, :, at_], es[:, :, at_]
                    for r, (x1_, y1_, op) in enumerate(((wr, wi, ALU.add), (wi, wr, ALU.subtract))):
                        ch(tt(tmpA[:, :, 0:CK], x1_, ec, ALU.mult))
                        ch(tt(tmpB[:, :, 0:CK], y1_, es, ALU.mult))
                        ch.wait()
                        for g2 in range(2):
                            half = slice(64 * g2, 64 * g2 + 64)
                            ins = tt(SBD[r][half, d, :, g2, :], tmpA[half, :, 0:CK], tmpB[half, :, 0:CK], op)
                            if r == 1 and g2 == 1:
                                ins.then_inc(state_ready, 1)
                                V_.wait_ge(state_ready, 2 * b + 1 + d)
                            else:
                                ch(ins)
                        ch.wait()
                split_lo(dve, S_OF["gate"][2 * b] + 2)
                V_.wait_ge(y_T, b + 1)
                V_.tensor_copy(ytok[:, :, 64:128].rearrange("p j (g c) -> p g j c", c=GC),
                               bank[2][0:64, :].rearrange("p (g j c) -> p g j c", g=4, j=L)).then_inc(ytok_D, 1)

            V_.wait_ge(prep_hi, 1)
            tt(cq_lo[:, :, :], cq[:, :, :], cq_hi[:, :, :].bitcast(F32), ALU.subtract).then_inc(prep_lo, 1)
            V_.wait_ge(prep_hi, 2)
            tt(ckv_lo[:, :, :], ckv[:, :, :], ckv_hi[:, :, :].bitcast(F32), ALU.subtract).then_inc(prep_lo, 1)
            for b in range(NB):
                V_.wait_ge(yprep_hi, b + 1)
                tt(y_lo[:, b, :].rearrange("p (k j) -> p j k", j=L), utok[:, b, 0:L * CK].rearrange("p (j k) -> p j k", j=L),
                   y_hi[:, b, :].rearrange("p (k j) -> p j k", j=L).bitcast(F32), ALU.subtract).then_inc(yprep_lo, 1)
            ch.wait()
            stt_(gain2[:, :], modb[:, 32:40, 0], 1.0, VEC[:, V_N2:V_N2 + 8], ALU.add, ALU.mult).then_inc(gain2_ready, 1)

            V_.wait_ge(attn_consts_in, 48)
            for t in range(8):
                if t % 4 == 0:
                    split_lo(dve, S_OF["uq"][0] + 1 + t // 4)
                V_.wait_ge(q_sq, t + 1)
                c0 = 8 * (t % 4) + 4 * (t // 4)
                V_.tensor_reduce(stq[:, 0, c0:c0 + 4], sqt[t % 2][:, 0:384].rearrange("p (h d) -> p h d", h=4),
                                 AX.X, ALU.add).then_inc(sq_used, 1)
            split_lo(dve, S_OF["glu"][0])
            t0 = TILE0["ukv"]
            for t in range(12):
                V_.wait_ge(tile_free, t0 + t + 1)
                V_.tensor_copy(V[:, t // 2, 256 * (t % 2):256 * (t % 2) + 256].rearrange("p (h e) -> p h e", h=4),
                               bank[6 + (t0 + t) % 2][:, :].rearrange("p (h e) -> p h e", h=4)[:, :, NOPE:]).then_inc(v_copy, 1)
                V_.wait_ge(q_sq, 8 + t + 1)
                c0 = 32 + 8 * (t // 2) + 4 * (t % 2)
                V_.tensor_reduce(stq[:, 0, c0:c0 + 4], sqt[t % 2][:, 0:256].rearrange("p (h d) -> p h d", h=4),
                                 AX.X, ALU.add).then_inc(sq_used, 1)

            yprep = None
            qg, kg = qkg[:, 0, :], qkg[:, 1, :]
            rq = stq[:, 1, 0:32].rearrange("p (t h) -> p t h", t=TT_N)[:, :, :, None]
            rk = stq[:, 1, 32:80].rearrange("p (t h) -> p t h", t=6)[:, :, :, None]
            tq_ = [tq[:, i, :].rearrange("p (t h c) -> p t h c", t=TT_N, h=H) for i in range(4)]

            def qk_norm_part(m):
                if m == 0:
                    V_.wait_ge(sq_used, 20)
                    V_.wait_ge(kr_ready, 1)
                    V_.wait_ge(tile_free, TILE0["glu"])
                    ch.step(tt(sqt[0][:, 0:192].rearrange("p (t r) -> p t r", t=6), kr[:, :, :], kr[:, :, :], ALU.mult))
                    ch.step(V_.tensor_reduce(stq3[:, :], sqt[0][:, 0:192].rearrange("p (t r) -> p t r", t=6), AX.X, ALU.add))
                    ks = stq[:, 0, 32:80].rearrange("p (t h) -> p t h", t=6)
                    ch.step(tt(ks, ks, stq3[:, :, None].to_broadcast([P, 6, H]), ALU.add))
                    ch.step(ts(stq[:, 0, :], stq[:, 0, :], 1.0 / QK, EPS))
                    rsqrt(stq[:, 1, :], stq[:, 0, :], sqt[1][:, 0:80])
                elif m == 1:
                    ch.step(tt(qsb[:, :, :, :], qsb[:, :, :, :], rq.to_broadcast([P, TT_N, H, QK]), ALU.mult))
                elif m == 2:
                    ch.step(tt(qsb[:, :, :, :], qsb[:, :, :, :], qg[:, None, None, :].to_broadcast([P, TT_N, H, QK]), ALU.mult))
                elif m == 3:
                    r1, r2 = qsb[:, :, :, 64:80], qsb[:, :, :, 80:96]
                    sh4 = [P, TT_N, H, 16]
                    co, si = rope[:, :, None, 0:16].to_broadcast(sh4), rope[:, :, None, 16:32].to_broadcast(sh4)
                    ch(tt(tq_[0], r1, co, ALU.mult))
                    ch(tt(tq_[1], r2, si, ALU.mult))
                    ch(tt(tq_[2], r1, si, ALU.mult))
                    ch(tt(tq_[3], r2, co, ALU.mult))
                    ch.wait()
                    ch(tt(r1, tq_[0], tq_[1], ALU.subtract))
                    tt(r2, tq_[2], tq_[3], ALU.add).then_inc(q_ready, 1)
                elif m == 4:
                    kn = ksb[:, :, :, 0:NOPE]
                    ch.step(tt(kn, kn, rk.to_broadcast([P, 6, H, NOPE]), ALU.mult))
                elif m == 5:
                    kn = ksb[:, :, :, 0:NOPE]
                    ch(tt(kn, kn, kg[:, None, None, 0:NOPE].to_broadcast([P, 6, H, NOPE]), ALU.mult))
                elif m == 6:
                    V_.wait_ge(q_ready, 1)
                    ch.step(tt(kr[:, :, :], kr[:, :, :], kg[:, None, NOPE:].to_broadcast([P, 6, ROPE]), ALU.mult))
                    r1, r2 = kr[:, CT_N:, 0:16], kr[:, CT_N:, 16:32]
                    co, si = rope[:, :, 0:16], rope[:, :, 16:32]
                    tk = [tq[:, i, 0:64].rearrange("p (t c) -> p t c", t=TT_N) for i in range(4)]
                    ch(tt(tk[0], r1, co, ALU.mult))
                    ch(tt(tk[1], r2, si, ALU.mult))
                    ch(tt(tk[2], r1, si, ALU.mult))
                    ch(tt(tk[3], r2, co, ALU.mult))
                    ch.wait()
                    ch(tt(r1, tk[0], tk[1], ALU.subtract))
                    ch.step(tt(r2, tk[2], tk[3], ALU.add))
                    tt(ksb[:, :, :, NOPE:], kr[:, :, None, :].to_broadcast([P, 6, H, ROPE]),
                       rk.to_broadcast([P, 6, H, ROPE]), ALU.mult).then_inc(k_ready, 1)

            t0 = TILE0["glu"]
            for m in range(KD):
                if m % 2 == 0:
                    split_lo(dve, S_OF["glu"][m // 2] + 1)
                qk_norm_part(m)
                V_.wait_ge(sg_ready, m + 1)
                V_.wait_ge(gload_in[m % 4], 16 * (m // 4 + 1))
                ch.step(tt(sg[m % 2][:, :], sg[m % 2][:, :], gload[m % 4][:, :], ALU.mult))
                V_.wait_ge(tile_done, t0 + 2 * m + 1)
                tt(sT[:, m, :], bank[4 + (2 * m) % 4][:, :], sg[m % 2][:, :], ALU.mult).then_inc(s_ready, 1)

            for i in range(1, 24, 2):
                V_.wait_ge(qk_T, i + 1)
                dst, w = qk_tile(i)
                V_.tensor_copy(dst, bank[i % 4][0:QK, 0:w]).then_inc(qk_D, 1)
            split_lo(dve, S_OF["wo"][1])

            def row_max(i):
                V_.wait_ge(s_mm, i + 1)
                if i >= 4:
                    V_.wait_ge(exp_ready, i - 3)
                ch.step(V_.tensor_reduce(smx[:, i % 4, 0:1], ps[:, 2 * (i % 2):2 * (i % 2) + 2, 0:384], AX.XY, ALU.max))
                ts(smx[:, i % 4, 1:2], smx[:, i % 4, 0:1], -SCALE).then_inc(max_ready, 1)

            def o_out(i):
                h, q = i // 4, i % 4
                V_.wait_ge(exp_ready, i + 1)
                ch.step(V_.reciprocal(smx[:, i % 4, 3:4], smx[:, i % 4, 2:3]))
                V_.wait_ge(o_mm, i + 1)
                ts(otok[:, q, VD * h:VD * h + VD], bank[6 + i % 2][:, 0:VD], smx[:, i % 4, 3:4]).then_inc(o_evac, 1)

            row_max(0)
            for i in range(4 * H):
                if i + 1 < 4 * H:
                    row_max(i + 1)
                V_.wait_ge(p_T, 2 * i + 1)
                if i >= 2:
                    V_.wait_ge(o_mm, i - 1)
                V_.tensor_copy(PT[i % 2][:, 0:3, :].rearrange("p a b -> p (a b)"), bank[4][:, 0:384]).then_inc(pt_D, 1)
                if i >= 1:
                    o_out(i - 1)
            o_out(4 * H - 1)
            for k in range(4):
                V_.wait_ge(oT_hi_r, k + 1)
                tt(oT_lo[:, k, :], bank[k][:, :], oT_hi[:, k, :].bitcast(F32), ALU.subtract).then_inc(oT_lo_r, 1)

            def merged_lo(m):
                V_.wait_ge(mg_h, m + 1)
                tt(mg_lo[:, m, :], mgf[m % 2][:, :], mg_hi[:, m, :].bitcast(F32), ALU.subtract).then_inc(mg_l, 1)

            t0 = TILE0["wo"]
            for m in range(KD):
                V_.wait_ge(tile_done, t0 + m + 1)
                V_.wait_ge(gload_in[m % 4], 16 * (2 + m // 4 + 1))
                if m >= 2:
                    V_.wait_ge(mg_l, m - 1)
                ch.step(tt(mgf[m % 2][:, :], bank[6 + m % 2][:, :], gload[m % 4][:, :], ALU.mult))
                tt(mgf[m % 2][:, :], mgf[m % 2][:, :], sT[:, m, :], ALU.add).then_inc(mg_f, 1)
                if m >= 1:
                    merged_lo(m - 1)
                if m == 5:
                    split_lo(dve, S_OF["wout"][0])
            merged_lo(KD - 1)

            t0 = TILE0["wout"]
            for p in range(4):
                split_lo(dve, S_OF["wout"][p] + 1)
                for mi in range(2):
                    m = 2 * p + mi
                    V_.wait_ge(tile_done, t0 + m + 1)
                    stt_(xT[:, m, :], bank[6 + m % 2][:, :], modb[:, 16 + m, 0:1], xT[:, m, :], ALU.mult, ALU.add).then_inc(x1_ready, 1)
            V_.wait_ge(stat2_mm, 1)
            ch.step(ts(stv[:, 0:4], ps[:, 0:4, 0:1].rearrange("p a b -> p (a b)"), 1.0 / D, EPS))
            rsqrt(sty[:, 0:4], stv[:, 0:4], stt[:, 0:4])
            for t in range(TT_N):
                ts(diag3[:, t, :], ident[:, :], sty[:, t:t + 1]).then_inc(diag3_ready, 1)
            V_.wait_ge(rstd3_mm, 1)
            for k in range(KD + 1):
                if k < KD:
                    if k >= 2:
                        V_.wait_ge(nh_ready, k - 1)
                    tt(nx[k % 2][:, :], xT[:, k, :], bank[4][:, :], ALU.mult).then_inc(nx_ready, 1)
                if k >= 1:
                    V_.wait_ge(h2_h, k)
                    tt(h2_lo[:, k - 1, :], nh[(k - 1) % 2][:, :], h2_hi[:, k - 1, :].bitcast(F32), ALU.subtract).then_inc(h2_l, 1)

            s0, t0 = S_OF["up"][0], TILE0["up"]

            def up_round(i, j, more):
                f = 2 * i + j
                if more:
                    s = s0 + 1 + j
                    V_.wait_ge(hi_ready, s + 1 + 2 * i)
                    V_.tensor_tensor(wlo[s % 2][:, :], raw[N_OF_SPLIT[s] % 2][:, :], whi[s % 2][:, :].bitcast(F32),
                                     ALU.subtract).then_inc(lo_ready, 1)
                for v in range(2):
                    u_ = bank[4 + 2 * j + v]
                    V_.wait_ge(cv_a, 4 * i + 2 * j + v + 1)
                    ch.step(stt_(cv[v][j][:, 1:], u_[:, 0:T - 1], VEC[:, bass.ds(V_W0 + 22 * v + f, 1)], cv[v][j][:, 1:],
                                 ALU.mult, ALU.add))
                    stt_(cv[v][j][:, 0:T - 1], u_[:, 1:], VEC[:, bass.ds(V_W2 + 22 * v + f, 1)], cv[v][j][:, 0:T - 1],
                         ALU.mult, ALU.add).then_inc(cv_d, 1)
                V_.wait_ge(silu_done, f + 1)
                tt(cv[0][j][:, :], cv[0][j][:, :], sl[j][:, :], ALU.mult).then_inc(act_f, 1)
                V_.wait_ge(act_h, f + 1)
                tt(act_lo[:, bass.ds(f, 1), :], cv[0][j][:, None, :], act_hi[:, bass.ds(f, 1), :].bitcast(F32),
                   ALU.subtract).then_inc(act_l, 1)

            up_round(0, 0, True)
            up_round(0, 1, True)
            with dve.Fori(1, 10) as i:
                ch.enter(i - 1, 4)
                for j in range(2):
                    up_round(i, j, True)
                ch.leave(9)
            up_round(10, 0, True)
            split_lo(dve, S_OF["down"][0])
            up_round(10, 1, False)

            s0, t0 = S_OF["down"][0], TILE0["down"]
            for p in range(12):
                if p < 11:
                    split_lo(dve, s0 + p + 1)
                if p % 3 == 2:
                    pair = p // 3
                    if pair >= 2:
                        V_.wait_ge(xo_T, 2 * (pair - 2) + 2)
                    for mi in range(2):
                        m = 2 * pair + mi
                        V_.wait_ge(tile_done, t0 + m + 1)
                        stt_(xo[pair % 2][:, mi, :], bank[4 + m % 4][:, :], modb[:, 40 + m, 0:1], xT[:, m, :],
                             ALU.mult, ALU.add).then_inc(xo_ready, 1)

        @block.tensor
        def _(pe):
            def product(out_, wx, last=True, first=True):
                ins = None
                for i, (w_, x_) in enumerate(wx):
                    ins = pe.matmul(out_, w_, x_, start=(first and i == 0), stop=(last and i == len(wx) - 1))
                return ins

            def three(s_hi, s_lo, m_hi, m_lo):
                return [(s_hi, m_hi), (s_hi, m_lo), (s_lo, m_hi)]

            def tok(k, t):
                if t < CT_N:
                    return hc_hi[:, k, P * t:P * t + P], hc_lo[:, k, P * t:P * t + P]
                return h_hi[:, k, P * (t - CT_N):P * (t - CT_N) + P], h_lo[:, k, P * (t - CT_N):P * (t - CT_N) + P]

            def panel(s, k_tiles, w):
                pe.wait_ge(lo_ready, s + 1)
                return [b_[s % 2][:, 0:k_tiles * w].rearrange("p (k n) -> p k n", k=k_tiles) for b_ in (whi, wlo)]

            def mod1_products(p, buf, signal, value):
                pe.wait_ge(signal, value)
                w = buf[:, :].rearrange("p (k n) -> p k n", k=KD)
                for mi in range(2):
                    c0 = 2 * (2 * p + mi)
                    ins = product(bank[7][:, c0:c0 + 2], [(w[:, k, P * mi:P * mi + P], cs[:, k, :]) for k in range(KD)])
                ins.then_inc(mod1_pe, 1)

            pe.wait_ge(cs_ready, 1)
            mod1_products(0, raw[0], raw_in[0], 16)

            pe.wait_ge(consts_ready, 1)
            pe.wait_ge(x_in, 16)
            for k in range(KD):
                if k >= 6:
                    pe.wait_ge(xT_ready, k - 5)
                for t in range(TT_N):
                    ins = pe.transpose(bank[k % 6][:, P * t:P * t + P], xtok[:, t, P * k:P * k + P], ident[:, :])
                ins.then_inc(xT_mm, 1)

            pe.wait_ge(params_in, 16 * 13)
            pe.transpose(bank[6][:, 0:73], rowsA[:, :], ident[0:73, 0:73])
            pe.transpose(bank[6][:, 73:161], rowsB[:, :], ident[0:88, 0:88])
            pe.transpose(bank[6][:, 161:249], rowsC[:, :], ident[0:88, 0:88])
            pe.transpose(bank[6][:, 249:313], rowsL[:, :], ident[0:64, 0:64])
            pe.wait_ge(ldt_wide, 1)
            pe.transpose(bank[6][:, 313:345], rowsT[:, :], ident[0:32, 0:32]).then_inc(vec_T, 1)
            mod1_products(2, early[0], early_in[0], 16)

            pe.wait_ge(ctx_in, 16)
            for k2 in range(KD // 2):
                pe.wait_ge(xT_ready, k2 + 3)
                for a_ in range(2):
                    for t in range(CT_N):
                        ins = pe.transpose(bank[(KD + k2) % 6][:, C * a_ + P * t:C * a_ + P * t + P],
                                           ctok[:, t, P * (2 * k2 + a_):P * (2 * k2 + a_) + P], ident[:, :])
                ins.then_inc(xT_mm, 1)
            mod1_products(4, early[2], early_in[2], 16)

            pe.wait_ge(diag1_ready, TT_N + CT_N)
            pe.wait_ge(vec_ready, 1)
            pe.wait_ge(xT_ready, KD)
            for t in range(TT_N + CT_N):
                ins = pe.matmul(bank[0 if t >= TT_N else 6][:, P * (t % TT_N):P * (t % TT_N) + P], ones[:, :], diag[:, t, :], start=True, stop=True)
            ins.then_inc(rstd1_mm, 1)
            mod1_products(6, raw[0], raw_in[0], 32)

            pe.wait_ge(c_in, 16 * 8)
            pe.wait_ge(xn_ready, 4)
            for b in range(NB):
                if b >= 2:
                    pe.wait_ge(ct_ready, b - 1)
                    pe.wait_ge(ct2_ready, b - 1)
                for i in range(4):
                    ins = pe.transpose(bank[4 + b % 2][:, P * i:P * i + P], ctile[:, i, b].rearrange("p g n -> p (g n)"), ident[:, :])
                ins.then_inc(ct_T, 1)

            pe.wait_ge(mod1_dve, 4)
            for i in range(4):
                for mi in range(2):
                    for r in range(2):
                        c0 = 2 * (2 * (2 * i + 1) + mi) + r
                        ins = pe.matmul(bank[7][:, c0:c0 + 1], macc1[:, i, r, P * mi:P * mi + P], ones[:, 0:1], start=True, stop=True)
            ins.then_inc(mod1_mm, 1)

            def next_tile(t):
                if t >= 2:
                    pe.wait_ge(tile_free, t - 1)
                return bank[6 + t % 2]

            def lat_products(t, out_, wh, wl, cols, x, ks):
                xh, xl = x
                for k in ks:
                    ins = product(out_, three(wh[:, k, cols], wl[:, k, cols], xh[:, k, :], xl[:, k, :]),
                                  first=k == 0, last=k == KD - 1)
                if KD - 1 in ks:
                    ins.then_inc(tile_done, 1)

            low, high, of_x, of_ctx = slice(0, P), slice(P, 2 * P), (h_hi, h_lo), (hc_hi, hc_lo)
            pe.wait_ge(rstd1_ready, 2)
            pe.wait_ge(gain1_ready, 2)
            wh, wl = panel(S_OF["lat"][0], KD, 256)
            for k in range(KD):
                pe.wait_ge(h_split, k + 1)
                lat_products(0, bank[6], wh, wl, low, of_x, [k])
                lat_products(1, bank[7], wh, wl, high, of_x, [k])
            t = 2
            wh, wl = panel(S_OF["lat"][1], KD, 256)
            for cols, x in ((low, of_x), (high, of_x), (high, of_ctx)):
                lat_products(t, next_tile(t)[:, 0:C if x is of_ctx else T], wh, wl, cols, x, range(KD))
                t += 1
            wh, wl = panel(S_OF["lat"][2], KD, 160)
            for cols, x in ((low, of_x), (low, of_ctx), (slice(P, P + ROPE), of_x), (slice(P, P + ROPE), of_ctx)):
                rows_ = cols.stop - cols.start
                lat_products(t, next_tile(t)[0:rows_, 0:C if x is of_ctx else T], wh, wl, cols, x, range(KD))
                t += 1

            for p in range(2):
                wh, wl = panel(S_OF["u"][p], KD, 256)
                for tt_ in range(CT_N + TT_N):
                    product(next_tile(t)[:, 0:256],
                            [q_ for k in range(KD) for q_ in three(*tok(k, tt_), wh[:, k, :], wl[:, k, :])]).then_inc(tile_done, 1)
                    t += 1
                if p == 0:
                    for tt_ in range(CT_N + TT_N):
                        ins = pe.transpose(bank[5][:, ROPE * tt_:ROPE * tt_ + ROPE], krT[:, P * tt_:P * tt_ + P], ident[0:ROPE, 0:ROPE])
                    ins.then_inc(kr_T, 1)
                    pe.wait_ge(latsq, 2)
                    for tt_ in range(TT_N):
                        product(bank[0][:, tt_:tt_ + 1], [(sqq[:, k, P * tt_:P * tt_ + P], ones[:, 0:1]) for k in range(3)])
                    for tt_ in range(CT_N + TT_N):
                        ins = product(bank[0][:, 4 + tt_:5 + tt_], [(sqk[:, k, P * tt_:P * tt_ + P], ones[:, 0:1]) for k in range(2)])
                    ins.then_inc(lat_stat, 1)
            pe.wait_ge(diag2_ready, 10)
            for tt_ in range(10):
                b_, c_ = (1, tt_) if tt_ < 4 else (2 + (tt_ - 4) // 4, (tt_ - 4) % 4)
                ins = pe.matmul(bank[b_][:, P * c_:P * c_ + P], ones[:, :], diag2[:, tt_, :], start=True, stop=True)
            ins.then_inc(rstd2_mm, 1)

            def gate_panel(i, t):
                wh, wl = panel(S_OF["gate"][i], KD, 256)
                for mi in range(2):
                    col = P * mi
                    product(next_tile(t + mi), [q_ for k in range(KD) for q_ in three(
                        wh[:, k, col:col + P], wl[:, k, col:col + P], h_hi[:, k, :], h_lo[:, k, :])]).then_inc(tile_done, 1)

            pe.wait_ge(kr_ready, 1)
            pe.wait_ge(lat_normed, 1)
            pe.wait_ge(ug_A, 2)
            pe.wait_ge(ug_D, 2)
            for b in range(NB):
                t = TILE0["gate"] + 4 * b
                for g in range(GB):
                    if b >= 1 and g == 0:
                        pe.wait_ge(y_evac, b)
                    if b >= 1 and g == 4:
                        pe.wait_ge(ytok_A, b)
                    ins = pe.transpose(bank[g // 4][:, NK * (g % 4):NK * (g % 4) + NK],
                                       utok[0:NK, b, P * g:P * g + P], ident[0:NK, 0:NK])
                    if g % 4 == 3:
                        ins.then_inc(u_T, 1)
                pe.wait_ge(bp_ready, 2 * b + 2)
                if b >= 1:
                    pe.wait_ge(v_read, 2 * b)
                    pe.wait_ge(ytok_D, b)
                    pe.wait_ge(gelu_done, b)
                for r in range(2):
                    for d in range(2):
                        for m in range(PB):
                            ins = pe.transpose(bank[2 + 2 * r + d][:, P * m:P * m + P], BP[:, r, d, m, :], ident[:, :])
                ins.then_inc(bp_T, 1)
                gate_panel(2 * b, t)
                pe.wait_ge(cp_ready, 2 * b + 2)
                pe.wait_ge(u_evacA, 2 * b + 2)
                pe.wait_ge(u_evacD, 2 * b + 2)
                pe.wait_ge(mod2_used, 4 * b + 4)
                for q in range(8):
                    pe.matmul(bank[0][:, 256 + q:257 + q], utok[:, b, P * q:P * q + P], ones[:, 0:1], start=True, stop=True)
                for m in range(PB):
                    for d in range(2):
                        c0 = GC * d
                        ins = product(bank[d][32 * m:32 * m + 32, 0:P],
                                      [(bbd[:, r, d, m, :], CP[:, r, d, m, c0:c0 + P]) for r in range(2)])
                ins.then_inc(t_mm, 1)
                pe.wait_ge(winT_A, 2 * b + 2)
                pe.wait_ge(winT_D, 2 * b + 2)
                for d in range(2):
                    u_ = Ub if d else U
                    for r in range(2):
                        for m in range(PB):
                            for g2 in range(2):
                                ins = pe.matmul(bank[2 + 2 * r + d][64 * g2:64 * g2 + 64, NK * m:NK * m + NK],
                                                WinT[:, r, d, m, 64 * g2:64 * g2 + 64], u_[:, 2 * m + g2, :], start=True, stop=True)
                    ins.then_inc(v_mm, 1)
                gate_panel(2 * b + 1, t + 2)
                pe.wait_ge(kf_ready, b + 1)
                pe.wait_ge(state_ready, 2 * b + 2)
                pe.wait_ge(sbd_zero, 4)
                pe.wait_ge(tt_in, 16 * L * (b + 1))
                for m in range(PB):
                    product(bank[0][:, P * m:P * m + P],
                            [(CP[:, r, d, m, GC * (1 - d):GC * (1 - d) + P], SBD[r][:, d, m].rearrange("p g k -> p (g k)"))
                             for d in range(2) for r in range(2)], last=False)
                    for g2 in range(2):
                        g = 2 * m + g2
                        ins = pe.matmul(bank[0][:, CK * g:CK * g + CK], TTm[:, g, :], U[:, g, CC:], start=False, stop=g2 == 1)
                ins.then_inc(y_mm, 1)
                pe.wait_ge(y_evac, b + 1)
                for g in range(GB):
                    ins = pe.transpose(bank[1 + g // 4][0:CK, P * (g % 4):P * (g % 4) + P], Ysb[:, g, :], ident[:, :])
                ins.then_inc(y_T, 1)
                pe.wait_ge(ytok_A, b + 1)
                pe.wait_ge(ytok_D, b + 1)
                for j in range(L):
                    ins = pe.transpose(bank[3][:, CK * j:CK * j + CK], ytok[:, j, :], ident[0:CK, 0:CK])
                ins.then_inc(y_T2, 1)

            t = TILE0["uq"]
            pe.wait_ge(prep_lo, 1)
            for p in range(2):
                wh, wl = panel(S_OF["uq"][p], 3, 384)
                for tt_ in range(TT_N):
                    product(next_tile(t)[:, 0:384], [q_ for k in range(3) for q_ in three(
                        cq_hi[:, k, P * tt_:P * tt_ + P], cq_lo[:, k, P * tt_:P * tt_ + P], wh[:, k, :], wl[:, k, :])]).then_inc(tile_done, 1)
                    t += 1
            pe.wait_ge(prep_lo, 2)
            wh, wl = panel(S_OF["ukv"][0], 2, 1024)
            for tt_ in range(CT_N + TT_N):
                for half in range(2):
                    n_ = 2 * tt_ + half
                    if n_ >= 2:
                        pe.wait_ge(v_copy, n_ - 1)
                    product(next_tile(t), [q_ for k in range(2) for q_ in three(
                        ckv_hi[:, k, P * tt_:P * tt_ + P], ckv_lo[:, k, P * tt_:P * tt_ + P],
                        wh[:, k, 512 * half:512 * half + 512], wl[:, k, 512 * half:512 * half + 512])]).then_inc(tile_done, 1)
                    t += 1

            pe.wait_ge(yprep_lo, NB)
            for p in range(4):
                wh, wl = panel(S_OF["glu"][p], 4, 512)
                for mi in range(2):
                    m = 2 * p + mi
                    if m == 1:
                        pe.wait_ge(tile_free, TILE0["glu"])
                        pe.wait_ge(v_copy, 12)
                    if m >= 2:
                        pe.wait_ge(s_ready, m - 1)
                        pe.wait_ge(sg_ready, m - 1)
                    for v in range(2):
                        col = 256 * v + P * mi
                        product(bank[4 + (2 * m + v) % 4], [q_ for k in range(4) for q_ in three(
                            wh[:, k, col:col + P], wl[:, k, col:col + P], y_hi[:, k, :], y_lo[:, k, :])]).then_inc(tile_done, 1)

            pe.wait_ge(q_ready, 1)
            for i in range(24):
                if i == H:
                    pe.wait_ge(k_ready, 1)
                if i >= 4:
                    pe.wait_ge(qk_D if i % 2 else qk_A, (i - 4) // 2 + 1)
                if i < H:
                    src = [qsb[:, tt_, i, :] for tt_ in range(TT_N)]
                else:
                    h, part = (i - H) // 2, (i - H) % 2
                    src = [ksb[:, tt_, h, :] for tt_ in ((4, 5) if part else (0, 1, 2, 3))]
                for j, s_ in enumerate(src):
                    ins = pe.transpose(bank[i % 4][0:QK, P * j:P * j + P], s_, ident[:, :])
                ins.then_inc(qk_T, 1)

            def scores(i):
                h, q = i // 4, i % 4
                if i >= 2:
                    pe.wait_ge(exp_ready, i - 1)
                for j in range(2):
                    ins = pe.matmul(bank[2 * (i % 2) + j][:, 0:384], qT[:, h, P * q:P * q + P],
                                    kT[:, h, 384 * j:384 * j + 384], start=True, stop=True)
                ins.then_inc(s_mm, 1)

            def turn_probs(i):
                pe.wait_ge(exp_ready, i + 1)
                for half in range(2):
                    if i >= 1:
                        pe.wait_ge(pt_A if half else pt_D, i)
                    for j in range(3):
                        ins = pe.transpose(bank[4 + half][:, P * j:P * j + P],
                                           Pm[i % 2][:, P * (3 * half + j):P * (3 * half + j) + P], ident[:, :])
                    ins.then_inc(p_T, 1)

            def weigh_values(i):
                h = i // 4
                pe.wait_ge(pt_D, i + 1)
                pe.wait_ge(pt_A, i + 1)
                if i >= 2:
                    pe.wait_ge(o_evac, i - 1)
                product(bank[6 + i % 2][:, 0:VD], [(PT[i % 2][:, kt, :], V[:, kt, VD * h:VD * h + VD]) for kt in range(6)]).then_inc(o_mm, 1)

            pe.wait_ge(qk_A, 12)
            pe.wait_ge(qk_D, 12)
            pe.wait_ge(s_ready, KD)
            scores(0)
            for i in range(4 * H):
                if i + 1 < 4 * H:
                    scores(i + 1)
                turn_probs(i)
                if i >= 1:
                    weigh_values(i - 1)
            weigh_values(4 * H - 1)

            pe.wait_ge(o_evac, 4 * H)
            for k in range(4):
                for q in range(TT_N):
                    ins = pe.transpose(bank[k][:, P * q:P * q + P], otok[:, q, P * k:P * k + P], ident[:, :])
                ins.then_inc(o_T, 1)
            for p in range(2):
                wh, wl = panel(S_OF["wo"][p], 4, 512)
                for mi in range(4):
                    m = 4 * p + mi
                    if m >= 2:
                        pe.wait_ge(mg_f, m - 1)
                    for k in range(4):
                        if m == 0:
                            pe.wait_ge(oT_lo_r, k + 1)
                        ins = product(bank[6 + m % 2], three(wh[:, k, P * mi:P * mi + P], wl[:, k, P * mi:P * mi + P],
                                                             oT_hi[:, k, :], oT_lo[:, k, :]), first=k == 0, last=k == 3)
                    ins.then_inc(tile_done, 1)
            for p in range(4):
                wh, wl = panel(S_OF["wout"][p], KD, 256)
                for mi in range(2):
                    m = 2 * p + mi
                    if m == 0:
                        pe.wait_ge(mg_f, KD)
                    if m >= 2:
                        pe.wait_ge(x1_ready, m - 1)
                    for k in range(KD):
                        if m == 0:
                            pe.wait_ge(mg_l, k + 1)
                        ins = product(bank[6 + m % 2], three(wh[:, k, P * mi:P * mi + P], wl[:, k, P * mi:P * mi + P],
                                                             mg_hi[:, k, :], mg_lo[:, k, :]), first=k == 0, last=k == KD - 1)
                    ins.then_inc(tile_done, 1)

            pe.wait_ge(sqx_ready, KD)
            for q in range(TT_N):
                ins = product(bank[q][:, 0:1], [(sqx[:, k, P * q:P * q + P], ones[:, 0:1]) for k in range(KD)])
            ins.then_inc(stat2_mm, 1)
            pe.wait_ge(diag3_ready, TT_N)
            for q in range(TT_N):
                ins = pe.matmul(bank[4][:, P * q:P * q + P], ones[:, :], diag3[:, q, :], start=True, stop=True)
            ins.then_inc(rstd3_mm, 1)

            s0 = S_OF["up"][0]
            pe.wait_ge(nx_ready, KD)
            pe.wait_ge(x1_ready, KD)

            def up_products(i, j, first):
                s = s0 + j
                pe.wait_ge(lo_ready, s + 1 + 2 * i)
                wh, wl = (b_[s % 2][:, :].rearrange("p (k v n) -> p k v n", k=KD, v=2) for b_ in (whi, wlo))
                if not first:
                    pe.wait_ge(cv_d, 4 * i + 2 * j - 2)
                for v in range(2):
                    for k in range(KD):
                        if first and j == 0 and v == 0:
                            pe.wait_ge(h2_l, k + 1)
                        ins = product(bank[4 + 2 * j + v], three(wh[:, k, v, :], wl[:, k, v, :], h2_hi[:, k, :], h2_lo[:, k, :]),
                                      first=k == 0, last=k == KD - 1)
                    ins.then_inc(tile_done, 1)

            for j in range(2):
                up_products(0, j, True)
            with pe.Fori(1, 11) as i:
                for j in range(2):
                    up_products(i, j, False)

            s0 = S_OF["down"][0]
            pe.wait_ge(cv_d, 2 * KF)

            def turn_out(pair):
                for mi in range(2):
                    pe.wait_ge(xo_ready, 2 * pair + mi + 1)
                    if pair >= 2 and mi == 0:
                        pe.wait_ge(ost_ready, pair - 1)
                    for tt_ in range(TT_N):
                        ins = pe.transpose(bank[2 * (pair % 2) + mi][:, P * tt_:P * tt_ + P],
                                           xo[pair % 2][:, mi, P * tt_:P * tt_ + P], ident[:, :])
                    ins.then_inc(xo_T, 1)

            for pair in range(4):
                for kk in range(3):
                    n_k = (8, 8, 6)[kk]
                    wh, wl = panel(s0 + 3 * pair + kk, n_k, 256)
                    pe.wait_ge(act_l, 8 * kk + n_k)
                    for mi in range(2):
                        m = 2 * pair + mi
                        if kk == 0 and m >= 4:
                            pe.wait_ge(xo_ready, m - 3)
                        ins = product(bank[4 + m % 4], [q_ for k in range(n_k) for q_ in three(
                            wh[:, k, P * mi:P * mi + P], wl[:, k, P * mi:P * mi + P],
                            act_hi[:, 8 * kk + k, :], act_lo[:, 8 * kk + k, :])], first=kk == 0, last=kk == 2)
                        if kk == 2:
                            ins.then_inc(tile_done, 1)
                    if kk < 2:
                        ins.then_inc(down_used, 1)
                    if kk == 0 and pair >= 1:
                        turn_out(pair - 1)
            turn_out(3)


NAMES = ["x", "ctx", "c", "c_ctx", "w_mod", "b_mod", "norm1_g", "norm2_g", "w_in", "q_a_g", "w_uq", "kv_a_g", "w_ukv",
         "q_norm_g", "k_norm_g", "w_o_attn", "lam_re_f", "lam_im_f", "log_dt_f", "c_re_f", "c_im_f",
         "lam_re_b", "lam_im_b", "log_dt_b", "c_re_b", "c_im_b", "b_re", "b_im", "d_skip", "w_glu", "w_out", "w_up",
         "conv_w", "conv_b", "w_down"]


def kernel(**inputs):
    import concourse.bacc as bacc
    from concourse.bass_utils import run_bass_kernel_spmd

    nc = bacc.Bacc("TRN2", target_bir_lowering=False, num_devices=1)
    arrays = {}
    for name in NAMES:
        v = np.asarray(inputs[name])
        arrays["in_" + name] = np.ascontiguousarray(v if name == "c_ctx" else v[0])
    arrays["in_rope"] = rope_tables()
    a = {name[3:]: nc.dram_tensor(name, v.shape, F32, kind="ExternalInput").ap() for name, v in arrays.items()}
    out = nc.dram_tensor("out_x", (T, D), F32, kind="ExternalOutput").ap()
    build(nc, a, out)
    result = run_bass_kernel_spmd(nc, [arrays], core_ids=[0])
    return result.results[0]["out_x"].reshape(1, T, D)
```

```python
from contextlib import ExitStack

import numpy as np

import concourse.bass as bass
from concourse import mybir
from concourse.alu_op_type import AluOpType as ALU

F32 = mybir.dt.float32
F32R = mybir.dt.float32r
I32 = mybir.dt.int32
ACT = mybir.ActivationFunctionType
AX = mybir.AxisListType

P = 128
D = 1024
KD = D // P
T = 512
C = 256
TT_N, CT_N = T // P, C // P
H, NOPE, ROPE, VD = 8, 64, 32, 64
QK = NOPE + ROPE
QL, KVL = 384, 256
SSM = 512
G, GC, NS = 32, 16, 64
NP = G // 2
L = 8
CK, CC = T // L, C // L
NK = CC + CK
NB, GB, PB = 4, 8, 4
FF = 2816
KF = FF // P
IN_W = QL + KVL + ROPE + SSM + 2 * D
U0 = QL + KVL + ROPE
GATE0 = U0 + SSM
PW = 2048
EPS = 1e-6
SCALE = QK ** -0.5

V_BMOD, V_N1, V_N2, V_DSKIP, V_QAG, V_KVAG = 0, 48, 56, 64, 68, 71
V_W0, V_W1, V_W2, V_CB = 73, 117, 161, 205
V_LAM, V_LDT, V_C, V_END = 249, 313, 345, 361

GATE_ORDER = ("gate", "mod2", "mod2", "mod2", "gate", "mod2") * 4
STREAM = ["mod1"] * 2 + ["lat"] * 2 + ["u"] * 2 + ["lat"] + list(GATE_ORDER) + ["uq"] * 2 + ["ukv"] + ["glu"] * 4 \
    + ["wo"] * 2 + ["wout"] * 4 + ["up"] * 22 + ["down"] * 12


def positions():
    n_of, s_of, s_at, is_split = {}, {}, [], []
    s = 0
    for n, stage in enumerate(STREAM):
        n_of.setdefault(stage, []).append(n)
        split = not stage.startswith("mod")
        is_split.append(split)
        s_at.append(s)
        if split:
            s_of.setdefault(stage, []).append(s)
            s += 1
    return n_of, s_of, s_at, is_split


N_OF, S_OF, S_AT, IS_SPLIT = positions()
N_OF_SPLIT = [n for n in range(len(STREAM)) if IS_SPLIT[n]]

TILES = {"lat": 5, "u": 12, "lat2": 4, "gate": 16, "uq": 8, "ukv": 12, "glu": 16, "wo": 8, "wout": 8,
         "up": 44, "down": 8}
TILE0 = {}
_t = 0
for _name, _n in TILES.items():
    TILE0[_name] = _t
    _t += _n


class Chain:

    def __init__(self, eng, sem):
        self.eng, self.sem, self.base, self.local = eng, sem, 0, 0

    def __call__(self, ins):
        ins.then_inc(self.sem, 1)
        self.local += 1

    def wait(self):
        self.eng.wait_ge(self.sem, self.base + self.local)

    def step(self, ins):
        self(ins)
        self.wait()

    def enter(self, i, per_round):
        self.outer = self.base + self.local
        self.per_round = per_round
        self.base, self.local = self.outer + i * per_round, 0

    def leave(self, rounds):
        assert self.local == self.per_round, (self.local, self.per_round)
        self.base, self.local = self.outer + rounds * self.per_round, 0


def rope_tables():
    pos = np.arange(T)
    freqs = (10000.0 ** (-np.arange(ROPE // 4, dtype=np.float32) / (ROPE // 4))).astype(np.float32)
    row = (pos // 64).astype(np.float32)[:, None] * freqs
    col = (pos % 64).astype(np.float32)[:, None] * freqs
    ang = np.concatenate([row, col], axis=-1).astype(np.float64)
    return np.concatenate([np.cos(ang), np.sin(ang)], axis=-1).astype(np.float32)


def build(nc, a, out):
    ctx = ExitStack()
    with ctx:
        def sem(name):
            return ctx.enter_context(nc.semaphore(name))

        ORIGIN = 16512

        def at(name, kb, shape, dt=F32):
            return nc.alloc_sbuf_tensor_at(name, shape, dt, offset=ORIGIN + int(kb * 1024))

        raw = [at(f"raw{i}", 8 * i, [P, PW]) for i in range(2)]
        whi = [at(f"w_hi{i}", 16 + 8 * i, [P, PW], F32R) for i in range(2)]
        wlo = [at(f"w_lo{i}", 32 + 8 * i, [P, PW], F32R) for i in range(2)]
        early = [at(f"early{i}", kb, [P, PW]) for i, kb in enumerate((16, 24, 32, 40, 130, 114))]
        xT = at("xT", 48, [P, KD, T])
        o = [64.0]

        def small(name, shape, dt=F32):
            t = at(name, o[0], shape, dt)
            n = 1
            for d in shape[1:]:
                n *= d
            o[0] += ((n * 4 + 31) // 32 * 32) / 1024
            assert o[0] <= 70.01, (name, o[0])
            return t

        ident = small("ident", [P, P])
        ones = small("ones", [P, P])
        VEC = small("VEC", [P, V_END])
        modb = small("modb", [P, 48, 2])
        gain1 = small("gain1", [P, 2, KD])
        gain2 = small("gain2", [P, KD])
        LP = small("LP", [P, 2, 9, 32])
        r8 = small("r8", [P, 32])
        cs = small("cs", [P, KD, 2])
        dmask = small("dmask", [P, GC])
        rl = small("rl", [P, 10])
        stv = small("stv", [P, 10])
        sty = small("sty", [P, 10])
        stt = small("stt", [P, 10])
        smx = small("smx", [P, 4, 4])

        h_hi = at("h_hi", 70, [P, KD, T], F32R)
        h_lo = at("h_lo", 86, [P, KD, T], F32R)
        cq = at("cq", 102, [P, 3, T])
        ckv = at("ckv", 108, [P, 2, C + T])
        hc_hi = at("hc_hi", 114, [P, KD, C], F32R)
        hc_lo = at("hc_lo", 122, [P, KD, C], F32R)
        utok = at("utok", 130, [P, NB, GB * L * GC])
        ustage = at("ustage", 179, [P, L, SSM])
        CP_ = [at("CP0", 146, [P, 2, 2, PB, 9 * GC]), at("CP1", 54, [P, 2, 2, PB, 9 * GC])]
        BP = at("BP", 155, [P, 2, 2, PB, P])
        bbd = at("bbd", 163, [P, 2, 2, PB, 32])
        E_ = [at("E0", 165, [P, 2, 8, NK]), at("E1", 48, [P, 2, 8, NK])]
        CT = at("CT", 171, [P, 2, 2, NP, GC])
        BB = at("BB", 175, [P, 2, 2, NP, GC])
        xtok = at("xtok", 70, [P, TT_N, D])
        ctok = at("ctok", 86, [P, CT_N, D])
        junk = at("junk", 122, [P, D])
        diag = at("diag", 126, [P, 6, P])
        Bld = at("Bld", 152, [P, 2, NP, GC])
        TMP = at("TMP", 146, [P, 44, 32])
        bbt = at("bbt", 154, [P, 2, NP, GC])
        mrow = at("mrow", 102, [2, 2 * D])
        xn = at("xn", 179, [P, KD, T])
        cn = at("cn", 94, [P, KD, C])
        rstdb = at("rstdb", 203, [P, C + T])
        hf = [at(f"hf{i}", 130 + 3 * i, [P, C + T]) for i in range(2)]
        krT = at("krT", 197, [ROPE, C + T])
        ust = [at(f"ust{i}", 191 + i, [P, 256]) for i in range(4)]
        WinT = at("WinT", 114, [P, 2, 2, PB, P])
        TTm = at("TTm", 122, [P, GB, P])
        SBD = [at("SBD0", 126, [P, 2, PB, 2, CK]), at("SBD1", 191, [P, 2, PB, 2, CK])]
        U = at("U", 179, [P, GB, NK])
        Ub = at("Ub", 182, [P, GB, NK])
        W = at("W", 185, [P, 2, 2, PB, NK])
        Ysb = at("Ysb", 185, [P, GB, CK])
        zp = at("zp", 200, [P, 7, 2, 32])
        pt1 = at("pt1", 195, [P, 512])
        ytok = at("ytok", 187, [64, L, P])
        tmpA = at("tmpA", 197, [P, PB, NK])
        tmpB = at("tmpB", 198.5, [P, PB, NK])
        Kf = at("Kf", 190, [P, 15 * GC])
        gst = [at(f"gst{i}", 202 + 2 * i, [P, T]) for i in range(2)]
        kr = at("kr", 206, [P, 6, ROPE])
        y_hi = at("y_hi", 70, [P, 4, T], F32R)
        y_lo = at("y_lo", 78, [P, 4, T], F32R)
        sT = at("sT", 86, [P, KD, T])
        qT = at("qT", 102, [QK, H, T])
        V = at("V", 118, [P, 6, H * VD])
        kT = at("kT", 130, [QK, H, C + T])
        cq_hi = at("cq_hi", 86, [P, 3, T], F32R)
        cq_lo = at("cq_lo", 92, [P, 3, T], F32R)
        ckv_hi = at("ckv_hi", 158, [P, 2, C + T], F32R)
        ckv_lo = at("ckv_lo", 164, [P, 2, C + T], F32R)
        gload = [at(f"gload{i}", 154 + 2 * i, [P, T]) for i in range(4)]
        sg = [at(f"sg{i}", 162 + 2 * i, [P, T]) for i in range(2)]
        qsb = at("qsb", 170, [P, TT_N, H, QK])
        ksb = at("ksb", 182, [P, 6, H, QK])
        sqt = [at(f"sqt{i}", 200 + 2 * i, [P, T]) for i in range(2)]
        tq = at("tq", 130, [P, 4, 512])
        qkg = at("qkg", 204, [P, 2, QK])
        rope = at("rope", 204.75, [P, TT_N, 32])
        stq = at("stq", 205.25, [P, 2, 80])
        stq3 = at("stq3", 206.75, [P, 6])
        Pm = [at(f"Pm{i}", 170 + 3 * i, [P, C + T]) for i in range(2)]
        PT = [at(f"PT{i}", 176 + 3 * i, [P, 6, P]) for i in range(2)]
        otok = at("otok", 182, [P, TT_N, H * VD])
        oT_hi = at("oT_hi", 190, [P, 4, T], F32R)
        oT_lo = at("oT_lo", 198, [P, 4, T], F32R)
        mg_hi = at("mg_hi", 102, [P, KD, T], F32R)
        mg_lo = at("mg_lo", 118, [P, KD, T], F32R)
        mgf = [at(f"mgf{i}", 162 + 2 * i, [P, T]) for i in range(2)]
        sqx = at("sqx", 134, [P, KD, T])
        h2_hi = at("h2_hi", 70, [P, KD, T], F32R)
        h2_lo = at("h2_lo", 86, [P, KD, T], F32R)
        nx = [at(f"nx{i}", 190 + 2 * i, [P, T]) for i in range(2)]
        nh = [at(f"nh{i}", 194 + 2 * i, [P, T]) for i in range(2)]
        diag3 = at("diag3", 198, [P, TT_N, P])
        act_hi = at("act_hi", 102, [P, KF, T], F32R)
        act_lo = at("act_lo", 146, [P, KF, T], F32R)
        cv = [[at(f"cv{v}{i}", 190 + 4 * v + 2 * i, [P, T]) for i in range(2)] for v in range(2)]
        sl = [at(f"sl{i}", 198 + 2 * i, [P, T]) for i in range(2)]
        xo = [at(f"xo{i}", 70 + 4 * i, [P, 2, T]) for i in range(2)]
        ost = [at(f"ost{i}", 78 + 4 * i, [P, TT_N, 256]) for i in range(2)]

        ps = ctx.enter_context(nc.psum_tensor("ps", [P, 8, 512], F32))
        bank = [ps[:, i, :] for i in range(8)]

        u_dram = nc.dram_tensor("u_scratch", (C + T, SSM), F32, kind="Internal").ap()
        kf_dram = nc.dram_tensor("kf_scratch", (NB, P, 15 * GC), F32, kind="Internal").ap()
        xT_dram = nc.dram_tensor("xT_scratch", (P, KD, T), F32, kind="Internal").ap()
        gate_dram = nc.dram_tensor("gate_scratch", (16, P, T), F32, kind="Internal").ap()

        def rows(w):
            return w.rearrange("(k p) n -> p k n", p=P)

        w_mod_v = a["w_mod"].rearrange("(p k) n -> p k n", k=KD)
        w_in_v, w_uq_v, w_ukv_v, w_o_v, w_glu_v = (rows(a[n]) for n in ("w_in", "w_uq", "w_ukv", "w_o_attn", "w_glu"))
        w_out_v, w_up_v, w_down_v = (rows(a[n]) for n in ("w_out", "w_up", "w_down"))

        def width(stage, p):
            return {"lat": (2048, 2048, 1280)[p] if stage == "lat" else 0, "uq": 1152,
                    "down": (2048, 2048, 1536)[p % 3]}.get(stage, 2048)

        def parts(stage, p, buf):
            if stage in ("mod1", "mod2"):
                c0 = p * 256 + (2048 if stage == "mod2" else 0)
                return [(buf[:, :].rearrange("p (k n) -> p k n", k=8), w_mod_v[:, :, bass.ds(c0, 256)])]
            if stage == "lat":
                w = width(stage, p) // 8
                return [(buf[:, 0:8 * w].rearrange("p (k n) -> p k n", k=8), w_in_v[:, :, 256 * p:256 * p + w])]
            if stage in ("u", "gate"):
                c0 = (U0 if stage == "u" else GATE0) + p * 256
                return [(buf[:, :].rearrange("p (k n) -> p k n", k=8), w_in_v[:, :, bass.ds(c0, 256)])]
            if stage == "uq":
                return [(buf[:, 0:1152].rearrange("p (k n) -> p k n", k=3), w_uq_v[:, :, 384 * p:384 * p + 384])]
            if stage == "ukv":
                return [(buf[:, :].rearrange("p (k n) -> p k n", k=2), w_ukv_v[:, :, :])]
            if stage == "glu":
                b = buf[:, :].rearrange("p (k v n) -> p k v n", k=4, v=2)
                return [(b[:, :, v, :], w_glu_v[:, :, bass.ds(p * 256 + v * D, 256)]) for v in range(2)]
            if stage == "wo":
                return [(buf[:, :].rearrange("p (k n) -> p k n", k=4), w_o_v[:, :, 512 * p:512 * p + 512])]
            if stage == "wout":
                return [(buf[:, :].rearrange("p (k n) -> p k n", k=8), w_out_v[:, :, bass.ds(p * 256, 256)])]
            if stage == "up":
                b = buf[:, :].rearrange("p (k v n) -> p k v n", k=8, v=2)
                return [(b[:, :, v, :], w_up_v[:, :, bass.ds(p * 128 + v * FF, 128)]) for v in range(2)]
            raise ValueError(stage)

        def down_part(pair, kk, buf):
            n = (8, 8, 6)[kk]
            return buf[:, 0:n * 256].rearrange("p (k n) -> p k n", k=n), w_down_v[:, 8 * kk:8 * kk + n, bass.ds(pair * 256, 256)]

        raw_in = [sem("raw_in0"), sem("raw_in1")]
        hi_ready, lo_ready = sem("hi_ready"), sem("lo_ready")
        tile_done, tile_free = sem("tile_done"), sem("tile_free")
        down_used = sem("down_used")
        params_in, c_in, b_in = sem("params_in"), sem("c_in"), sem("b_in")
        lamv_in, x_in, ctx_in, ccld_in, attn_consts_in = (sem(n) for n in ("lamv_in", "x_in", "ctx_in", "ccld_in", "attn_consts_in"))
        consts_ready, cs_ready, ldt_wide = sem("consts_ready"), sem("cs_ready"), sem("ldt_wide")
        vec_T, vec_ready = sem("vec_T"), sem("vec_ready")
        pool_chain, dve_chain, act_chain = sem("pool_chain"), sem("dve_chain"), sem("act_chain")
        den_ready = sem("den_ready")
        sin_arg, sin_done = sem("sin_arg"), sem("sin_done")
        ssm_scalars = sem("ssm_scalars")
        ct_T, ct_ready = sem("ct_T"), sem("ct_ready")
        sumsq1, diag1_ready, rstd1_mm, rstd1_ready = (sem(n) for n in ("sumsq1", "diag1_ready", "rstd1_mm", "rstd1_ready"))
        xT_mm, xT_ready, xn_ready = sem("xT_mm"), sem("xT_ready"), sem("xn_ready")
        gain1_ready, hf_ready, h_split = sem("gain1_ready"), sem("hf_ready"), sem("h_split")
        latq_evac, latsq, lat_stat, diag2_ready, rstd2_mm, lat_normed = (sem(n) for n in ("latq_evac", "latsq", "lat_stat", "diag2_ready", "rstd2_mm", "lat_normed"))
        u_evac, u_out, utok_in = sem("u_evac"), [sem(f"u_out{i}") for i in range(4)], sem("utok_in")
        bp_ready, cp_ready, e_ready = sem("bp_ready"), sem("cp_ready"), sem("e_ready")
        u_T, u_evacA, u_evacD = sem("u_T"), sem("u_evacA"), sem("u_evacD")
        bp_T, winT_A, winT_D = sem("bp_T"), sem("winT_A"), sem("winT_D")
        t_mm, kf_ready, kf_out, tt_in = sem("t_mm"), sem("kf_ready"), sem("kf_out"), sem("tt_in")
        v_mm, v_read, state_ready, y_mm = sem("v_mm"), sem("v_read"), sem("state_ready"), sem("y_mm")
        y_evac, y_T, ytok_A, ytok_D, y_T2, gelu_done = (sem(n) for n in ("y_evac", "y_T", "ytok_A", "ytok_D", "y_T2", "gelu_done"))
        gate_sig, gate_out = sem("gate_sig"), [sem("gate_out0"), sem("gate_out1")]
        early_in = [sem(f"early_in{i}") for i in range(6)]
        mod1_pe, mrow_ready, mod1_T = sem("mod1_pe"), sem("mrow_ready"), sem("mod1_T")
        mod2_used, mod2_acc = sem("mod2_used"), sem("mod2_acc")
        cn_ready, xT_out, xT_back = sem("cn_ready"), sem("xT_out"), sem("xT_back")
        sq_lat, stat_mm, stat_read, mod2_mm = sem("sq_lat"), sem("stat_mm"), sem("stat_read"), sem("mod2_mm")
        kr_T, kr_ready = sem("kr_T"), sem("kr_ready")
        prep_hi, prep_lo = sem("prep_hi"), sem("prep_lo")
        q_sq, sq_used, v_copy = sem("q_sq"), sem("sq_used"), sem("v_copy")
        q_ready, k_ready, qk_A, qk_D = sem("q_ready"), sem("k_ready"), sem("qk_A"), sem("qk_D")
        yprep_hi, yprep_lo = sem("yprep_hi"), sem("yprep_lo")
        ug_A, ug_D = sem("ug_A"), sem("ug_D")
        gain2_ready, sbd_zero, ct2_ready = sem("gain2_ready"), sem("sbd_zero"), sem("ct2_ready")
        qk_ready, qk_T, qkT_ready = sem("qk_ready"), sem("qk_T"), sem("qkT_ready")
        gload_in = [sem(f"gload_in{i}") for i in range(4)]
        sg_ready, s_ready = sem("sg_ready"), sem("s_ready")
        s_mm, max_ready, exp_ready, p_T, pt_A, pt_D, o_mm, o_evac = (sem(n) for n in ("s_mm", "max_ready", "exp_ready", "p_T", "pt_A", "pt_D", "o_mm", "o_evac"))
        o_T, oT_hi_r, oT_lo_r = sem("o_T"), sem("oT_hi_r"), sem("oT_lo_r")
        mg_f, mg_h, mg_l = sem("mg_f"), sem("mg_h"), sem("mg_l")
        x1_ready, sqx_ready, stat2_mm, diag3_ready, rstd3_mm = (sem(n) for n in ("x1_ready", "sqx_ready", "stat2_mm", "diag3_ready", "rstd3_mm"))
        nx_ready, nh_ready, h2_h, h2_l = sem("nx_ready"), sem("nh_ready"), sem("h2_h"), sem("h2_l")
        cv_a, cv_d, silu_done, act_f, act_h, act_l = (sem(n) for n in ("cv_a", "cv_d", "silu_done", "act_f", "act_h", "act_l"))
        xo_ready, xo_T, ost_ready, out_done = sem("xo_ready"), sem("xo_T"), sem("ost_ready"), [sem("out_done0"), sem("out_done1")]

        def transfers(stage):
            return 2 if stage in ("glu", "up") else 1

        def raw_in_count(n):
            return 16 * sum(transfers(STREAM[m]) for m in range(n % 2, n + 1, 2))

        tiles_through = {}
        for p_, e_ in enumerate((2, 5, TILE0["lat2"] + 4 - TILE0["lat"])):
            tiles_through[N_OF["lat"][p_]] = TILE0["lat"] + e_
        for p_ in range(2):
            tiles_through[N_OF["u"][p_]] = TILE0["u"] + 6 * p_ + 6
            tiles_through[N_OF["uq"][p_]] = TILE0["uq"] + 4 * p_ + 4
            tiles_through[N_OF["wo"][p_]] = TILE0["wo"] + 4 * p_ + 4
        for i_ in range(8):
            tiles_through[N_OF["gate"][i_]] = TILE0["gate"] + 2 * i_ + 2
        tiles_through[N_OF["ukv"][0]] = TILE0["ukv"] + 12
        for p_ in range(4):
            tiles_through[N_OF["glu"][p_]] = TILE0["glu"] + 4 * p_ + 4
            tiles_through[N_OF["wout"][p_]] = TILE0["wout"] + 2 * p_ + 2
        for p_ in range(22):
            tiles_through[N_OF["up"][p_]] = TILE0["up"] + 2 * p_ + 2

        def wait_used(eng, n):
            if STREAM[n] == "mod1":
                return eng.wait_ge(mod1_pe, n + 1)
            if STREAM[n] == "mod2":
                return eng.wait_ge(mod2_used, N_OF["mod2"].index(n) + 1)
            if STREAM[n] == "down":
                p = n - N_OF["down"][0]
                if p % 3 == 2:
                    eng.wait_ge(tile_done, TILE0["down"] + 2 * (p // 3) + 2)
                else:
                    eng.wait_ge(down_used, 2 * (p // 3) + p % 3 + 1)
            else:
                eng.wait_ge(tile_done, tiles_through[n])

        def split_hi(act, s):
            n = N_OF_SPLIT[s]
            w = width(STREAM[n], N_OF[STREAM[n]].index(n))
            act.wait_ge(raw_in[n % 2], raw_in_count(n))
            if s >= 2:
                wait_used(act, N_OF_SPLIT[s - 2])
            else:
                act.wait_ge(mod1_pe, 3 + s)
            act.activation(whi[s % 2][:, 0:w], raw[n % 2][:, 0:w], ACT.Copy).then_inc(hi_ready, 1)

        def split_lo(dve, s):
            n = N_OF_SPLIT[s]
            w = width(STREAM[n], N_OF[STREAM[n]].index(n))
            dve.wait_ge(hi_ready, s + 1)
            if s < 2:
                dve.wait_ge(mod1_pe, 5 + s)
            dve.tensor_tensor(wlo[s % 2][:, 0:w], raw[n % 2][:, 0:w], whi[s % 2][:, 0:w].bitcast(F32),
                              ALU.subtract).then_inc(lo_ready, 1)

        def qk_tile(i):
            if i < H:
                return qT[:, i, :], T
            h, part = (i - H) // 2, (i - H) % 2
            return (kT[:, h, T:], C) if part else (kT[:, h, 0:T], T)

        block = ctx.enter_context(nc.Block())

        @block.sync
        def _(sp):
            def load(n, p=None):
                stage = STREAM[n]
                p = N_OF[stage].index(n) if p is None else p
                if n >= 2:
                    if IS_SPLIT[n - 2]:
                        sp.wait_ge(lo_ready, S_AT[n - 2] + 1)
                    else:
                        wait_used(sp, n - 2)
                for dst, src in parts(stage, p, raw[n % 2]):
                    sp.dma_start(dst, src).then_inc(raw_in[n % 2], 16)

            def load_down(n, pair, kk):
                sp.wait_ge(lo_ready, S_AT[n - 2] + 1)
                dst, src = down_part(pair, kk, raw[n % 2])
                sp.dma_start(dst, src).then_inc(raw_in[n % 2], 16)

            def load_mod1(p, buf, signal):
                for dst, src in parts("mod1", p, buf):
                    sp.dma_start(dst, src).then_inc(signal, 16)

            sp.dma_start(VEC[:, :], a["vectors"]).then_inc(vec_ready, 16)
            load_mod1(0, raw[0], raw_in[0])
            load_mod1(1, raw[1], raw_in[1])
            sp.dma_start(xtok[:, :, :], a["x"].rearrange("(t p) n -> p t n", p=P)).then_inc(x_in, 16)
            sp.dma_start(ctok[:, :, :], a["ctx"].rearrange("(t p) n -> p t n", p=P)).then_inc(ctx_in, 16)
            for p in range(2, 8):
                load_mod1(p, early[p - 2], early_in[p - 2])
            sp.dma_start(Bld[:, :, :, :], a["b"]).then_inc(b_in, 16)
            sp.dma_start(CT[:, :, :, :, :], a["c_states"]).then_inc(c_in, 16)
            for n in range(N_OF["lat"][0], N_OF["lat"][-1] + 1):
                load(n)
                if n == N_OF["lat"][1]:
                    sp.wait_ge(xT_ready, KD)
                    sp.dma_start(xT_dram, xT[:, :, :]).then_inc(xT_out, 16)
            for i in range(4):
                sp.wait_ge(u_out[i], 16 * 3)
            for j in range(L):
                sp.dma_start(ustage[0:NK, L - 1 - j, :],
                             u_dram.rearrange("(k j) c -> j k c", j=L)[j]).then_inc(utok_in, 16)
            gate_p = mod_p = 0
            for n in range(N_OF["gate"][0], N_OF["uq"][0]):
                if IS_SPLIT[n]:
                    load(n, gate_p)
                    gate_p += 1
                else:
                    load(n, mod_p)
                    mod_p += 1
            for n in N_OF["uq"] + N_OF["ukv"]:
                load(n)
            sp.wait_ge(y_mm, NB)
            sp.wait_ge(state_ready, 2 * NB)
            sp.wait_ge(xT_out, 16)
            sp.dma_start(xT[:, :, :], xT_dram).then_inc(xT_back, 16)
            for n in N_OF["glu"] + N_OF["wo"] + N_OF["wout"] + N_OF["up"][:2]:
                load(n)
            n0 = N_OF["up"][0]
            with sp.Fori(1, 11) as i:
                for j in range(2):
                    sp.wait_ge(lo_ready, S_AT[n0] + 2 * i + j - 1)
                    for dst, src in parts("up", 2 * i + j, raw[(n0 + j) % 2]):
                        sp.dma_start(dst, src).then_inc(raw_in[(n0 + j) % 2], 16)
            n0 = N_OF["down"][0]
            for j in range(2):
                load_down(n0 + j, 0, j)
            sp.wait_ge(lo_ready, S_AT[n0] + 1)
            dst, src = down_part(0, 2, raw[(n0 + 2) % 2])
            sp.dma_start(dst, src).then_inc(raw_in[(n0 + 2) % 2], 16)
            for j in range(3):
                load_down(n0 + 3 + j, 1, j)
            with sp.Fori(1, 2) as i:
                for j in range(6):
                    sp.wait_ge(lo_ready, S_AT[n0] + 6 * i + j - 1)
                    dst, src = down_part(2 * i + j // 3, j % 3, raw[(n0 + j) % 2])
                    sp.dma_start(dst, src).then_inc(raw_in[(n0 + j) % 2], 16)
            for pair in range(4):
                sp.wait_ge(ost_ready, pair + 1)
                sp.dma_start(out[:, pair * 256:(pair + 1) * 256].rearrange("(t p) n -> p t n", p=P),
                             ost[pair % 2][:, :, :]).then_inc(out_done[pair % 2], 16)
            for i in range(2):
                sp.wait_ge(out_done[i], 32)

        @block.gpsimd
        def _(pool):
            ch = Chain(pool, pool_chain)
            ch(pool.memset(ident[:, :], 0.0))
            ch(pool.memset(bbd[:, :, :, :, :], 0.0))
            ch.wait()
            ch.step(pool.affine_select(out=ident[:, :], in_=ident[:, :], compare_op=ALU.not_equal, fill=1.0, base=0,
                                       pattern=[[-1, P]], channel_multiplier=1))
            pool.memset(ones[:, :], 1.0).then_inc(consts_ready, 1)

            def tt(o_, x_, y_, op):
                return pool.tensor_tensor(o_, x_, y_, op)

            def ts(o_, x_, s1, s2=None, op0=ALU.mult, op1=ALU.add):
                if s2 is None:
                    return pool.tensor_scalar(o_, x_, s1, None, op0)
                return pool.tensor_scalar(o_, x_, s1, s2, op0, op1)

            def stt_(o_, x_, s, y_, op0, op1):
                ch.step(ts(TMP[:, 43, :], x_, s, None, op0))
                return tt(o_, TMP[:, 43, :], y_, op1)

            pool.wait_ge(vec_ready, 16)
            tmp = [TMP[:, k, :] for k in range(44)]

            def dm(v):
                return v.rearrange("p (d m) -> p d m", d=2)

            def exp(y, x, s):
                xc, n, f, q = s
                ch.step(ts(xc, x, -87.0, 88.0, ALU.max, ALU.min))
                ch.step(ts(n, xc, 1.4426950408889634, 12582912.0, ALU.mult, ALU.add))
                ch.step(ts(n, n, -12582912.0, None, ALU.add))
                ch.step(stt_(f, n, -0.693359375, xc, ALU.mult, ALU.add))
                ch.step(stt_(f, n, 2.12194440e-4, f, ALU.mult, ALU.add))
                ch.step(ts(q, f, 1.0 / 5040))
                for c_ in (1.0 / 720, 1.0 / 120, 1.0 / 24, 1.0 / 6, 0.5, 1.0):
                    ch.step(stt_(q, q, c_, f, ALU.add, ALU.mult))
                ch.step(ts(n.bitcast(I32), n, 8388608.0, 127.0 * 8388608.0))
                ch.step(stt_(y, q, 1.0, n, ALU.add, ALU.mult))
                ch.step(stt_(y, x, -87.0, y, ALU.is_ge, ALU.mult))

            lam = VEC[:, V_LAM:V_LAM + 64].rearrange("p (d r m) -> p r d m", d=2, r=2)
            lre, lim = lam[:, 0], lam[:, 1]
            dt, mag, th, n_ = tmp[0], tmp[1], tmp[2], tmp[3]
            exp(dt, VEC[:, V_LDT:V_LDT + 32], tmp[4:8])
            ch.step(tt(dm(th), lim, dm(dt), ALU.mult))
            ch.step(ts(n_, th, 0.15915494309189535, 12582912.0, ALU.mult, ALU.add))
            ch.step(ts(n_, n_, -12582912.0, None, ALU.add))
            ch.step(stt_(th, n_, -6.28125, th, ALU.mult, ALU.add))
            ch.step(stt_(th, n_, -0.0019350051879882812, th, ALU.mult, ALU.add))
            ch.step(stt_(th, n_, -3.0199159819567e-07, th, ALU.mult, ALU.add))
            ch.step(ts(tmp[8], th, 3.1415925, -3.1415925, ALU.min, ALU.max))
            ts(tmp[9], tmp[8], 0.5).then_inc(sin_arg, 1)
            pool.wait_ge(rstd1_ready, 2)
            for k in range(KD):
                tt(xn[:, k, :], xT[:, k, :], rstdb[:, C:], ALU.mult).then_inc(xn_ready, 1)

            ch.step(tt(dm(tmp[12]), lre, dm(dt), ALU.mult))
            exp(mag, tmp[12], tmp[4:8])
            pool.wait_ge(sin_done, 1)
            c1, s1 = tmp[13], tmp[14]
            ch.step(tt(c1, tmp[11], tmp[11], ALU.mult))
            ch.step(ts(c1, c1, -2.0, 1.0))
            ch.step(pool.tensor_copy(s1, tmp[10]))

            def cmul(o_, x_, y_, t, shape=None):
                b_ = (lambda v: v.to_broadcast(shape)) if shape else (lambda v: v)
                ch(tt(o_[0], x_[0], b_(y_[0]), ALU.mult))
                ch(tt(t[0], x_[1], b_(y_[1]), ALU.mult))
                ch(tt(o_[1], x_[1], b_(y_[0]), ALU.mult))
                ch(tt(t[1], x_[0], b_(y_[1]), ALU.mult))
                ch.wait()
                ch(tt(o_[0], o_[0], t[0], ALU.subtract))
                ch(tt(o_[1], o_[1], t[1], ALU.add))
                ch.wait()

            lp = lambda q: (LP[:, 0, q, :], LP[:, 1, q, :])
            ch(pool.memset(LP[:, 0, 0, :], 1.0))
            ch(pool.memset(LP[:, 1, 0, :], 0.0))
            ch(tt(LP[:, 0, 1, :], mag, c1, ALU.mult))
            ch(tt(LP[:, 1, 1, :], mag, s1, ALU.mult))
            ch.wait()
            tm = (tmp[15], tmp[16])
            cmul(lp(2), lp(1), lp(1), tm)
            cmul(lp(3), lp(2), lp(1), tm)
            cmul(lp(4), lp(2), lp(2), tm)
            for q in range(1, 5):
                cmul(lp(4 + q), lp(4), lp(q), tm)
            ch.step(tt(tmp[17], mag, mag, ALU.mult))
            ch.step(tt(tmp[17], tmp[17], tmp[17], ALU.mult))
            ch.step(tt(r8[:, :], tmp[17], tmp[17], ALU.mult))
            cmul((tmp[18], tmp[19]), (c1, s1), (c1, s1), tm)
            cmul((tmp[20], tmp[21]), (tmp[18], tmp[19]), (tmp[18], tmp[19]), tm)
            z = lambda i: (zp[:, i, 0, :], zp[:, i, 1, :])
            cmul(z(0), (tmp[20], tmp[21]), (tmp[20], tmp[21]), tm)
            for i in range(6):
                cmul(z(i + 1), z(i), z(i), tm)
            nr, _, den, qr, qi = tmp[22:27]
            ch(ts(nr, LP[:, 0, 1, :], -1.0, None, ALU.add))
            ch.wait()
            pool.wait_ge(den_ready, 1)
            ch(tt(dm(qr), dm(nr), lre, ALU.mult))
            ch(tt(dm(tmp[28]), dm(LP[:, 1, 1, :]), lim, ALU.mult))
            ch(tt(dm(qi), dm(LP[:, 1, 1, :]), lre, ALU.mult))
            ch(tt(dm(tmp[29]), dm(nr), lim, ALU.mult))
            ch.wait()
            ch(tt(qr, qr, tmp[28], ALU.add))
            ch(tt(qi, qi, tmp[29], ALU.subtract))
            ch.wait()
            ch(tt(qr, qr, den, ALU.mult))
            ch(tt(qi, qi, den, ALU.mult))
            pool.wait_ge(b_in, 16)
            ch.wait()
            sh = [P, NP, GC]
            for d in range(2):
                re_, im_ = BB[:, 0, d], BB[:, 1, d]
                q0, q1 = dm(qr)[:, d, :, None].to_broadcast(sh), dm(qi)[:, d, :, None].to_broadcast(sh)
                ch(tt(re_, Bld[:, 0], q0, ALU.mult))
                ch(tt(bbt[:, 0], Bld[:, 1], q1, ALU.mult))
                ch(tt(im_, Bld[:, 1], q0, ALU.mult))
                ch(tt(bbt[:, 1], Bld[:, 0], q1, ALU.mult))
                ch.wait()
                ch(tt(re_, re_, bbt[:, 0], ALU.subtract))
                ch.step(tt(im_, im_, bbt[:, 1], ALU.add))
                ins = ts(im_, im_, -1.0)
                ch.step(ins)

            pool.wait_ge(c_in, 16)

            def mul(o_, x_, y_, shape):
                ch(pool.tensor_tensor(o_, x_.to_broadcast(shape), y_.to_broadcast(shape), ALU.mult))

            def turn(d, part, pairs, forward):
                v = LP[:, part, 0:9, :].rearrange("p q (d m) -> p d m q", d=2)[:, d, pairs, :]
                return (v if forward else v[:, :, ::-1])

            for b in range(NB):
                pairs = slice(PB * b, PB * b + PB)
                if b >= 1:
                    pool.wait_ge(bp_T, b)
                for d in range(2):
                    sh = [P, PB, 8, GC]
                    br, bi = BB[:, 0, d, pairs, :][:, :, None, :], BB[:, 1, d, pairs, :][:, :, None, :]
                    if d == 0:
                        lr, li = turn(0, 0, pairs, True)[:, :, 0:8], turn(0, 1, pairs, True)[:, :, 0:8]
                    else:
                        lr, li = turn(1, 0, pairs, False)[:, :, 1:9], turn(1, 1, pairs, False)[:, :, 1:9]
                    lr, li = lr[:, :, :, None], li[:, :, :, None]
                    re = BP[:, 0, d].rearrange("p m (q c) -> p m q c", c=GC)
                    im = BP[:, 1, d].rearrange("p m (q c) -> p m q c", c=GC)
                    t1 = pt1[:, :].rearrange("p (m q c) -> p m q c", m=PB, c=GC)
                    mul(re, br, lr, sh)
                    mul(t1, bi, li, sh)
                    ch.wait()
                    ch(pool.tensor_tensor(re, re, t1, ALU.add))
                    ch.wait()
                    mul(im, bi, lr, sh)
                    mul(t1, br, li, sh)
                    ch.wait()
                    pool.tensor_tensor(im, im, t1, ALU.subtract).then_inc(bp_ready, 1)
                    pool.wait_ge(bp_ready, 2 * b + d + 1)
                CP, E = CP_[b % 2], E_[b % 2]
                if b >= 1:
                    pool.wait_ge(t_mm, b)
                if b == 1:
                    pool.wait_ge(xT_out, 16)
                if b >= 2:
                    pool.wait_ge(y_mm, b - 1)
                for g2 in range(2):
                    half = slice(64 * g2, 64 * g2 + 64)
                    ch.step(pool.tensor_copy(bbd[half, :, :, :, GC * g2:GC * g2 + GC].rearrange("p r d m c -> p (r d) m c"),
                                        BB[half, :, :, pairs, :].rearrange("p r d m c -> p (r d) m c")))
                for d in range(2):
                    for hp in range(2):
                        sh = [P, 2, 9, GC]
                        two = slice(PB * b + 2 * hp, PB * b + 2 * hp + 2)
                        cr, ci = CT[:, d, 0, two, :][:, :, None, :], CT[:, d, 1, two, :][:, :, None, :]
                        lr, li = turn(d, 0, two, d == 0)[:, :, :, None], turn(d, 1, two, d == 0)[:, :, :, None]
                        re = CP[:, 0, d, 2 * hp:2 * hp + 2].rearrange("p m (q c) -> p m q c", c=GC)
                        im = CP[:, 1, d, 2 * hp:2 * hp + 2].rearrange("p m (q c) -> p m q c", c=GC)
                        t1 = pt1[:, 0:288].rearrange("p (m q c) -> p m q c", m=2, c=GC)
                        mul(re, cr, lr, sh)
                        mul(t1, ci, li, sh)
                        ch.wait()
                        ch(pool.tensor_tensor(re, re, t1, ALU.subtract))
                        ch.wait()
                        mul(im, cr, li, sh)
                        mul(t1, ci, lr, sh)
                        ch.wait()
                        last = pool.tensor_tensor(im, im, t1, ALU.add)
                        if hp == 0:
                            ch.step(last)
                        else:
                            last.then_inc(cp_ready, 1)
                    pool.wait_ge(cp_ready, 2 * b + d + 1)
                pool.wait_ge(cp_ready, 2 * b + 2)
                if b >= 2:
                    pool.wait_ge(state_ready, 2 * b - 2)
                ch(pool.memset(E[:, 0, :, 0:1], 1.0))
                ch(pool.memset(E[:, 1, :, 0:1], 0.0))
                ch.wait()
                at_, i = 1, 0
                while at_ < NK:
                    n = min(at_, NK - at_)
                    z = [zp[:, i, r, :].rearrange("p (d m) -> p d m", d=2)[:, :, pairs] for r in range(2)]
                    sh = [P, 2, PB, n]
                    e = [E[:, r, :, :].rearrange("p (d m) k -> p d m k", d=2) for r in range(2)]
                    t1 = pt1[:, 0:8 * n].rearrange("p (d m k) -> p d m k", d=2, m=PB)
                    new = slice(at_, at_ + n)
                    mul(e[0][:, :, :, new], e[0][:, :, :, 0:n], z[0][:, :, :, None], sh)
                    mul(t1, e[1][:, :, :, 0:n], z[1][:, :, :, None], sh)
                    ch.wait()
                    ch(pool.tensor_tensor(e[0][:, :, :, new], e[0][:, :, :, new], t1, ALU.subtract))
                    ch.wait()
                    mul(e[1][:, :, :, new], e[1][:, :, :, 0:n], z[0][:, :, :, None], sh)
                    mul(t1, e[0][:, :, :, 0:n], z[1][:, :, :, None], sh)
                    ch.wait()
                    last = pool.tensor_tensor(e[1][:, :, :, new], e[1][:, :, :, new], t1, ALU.add)
                    at_ += n
                    i += 1
                    if at_ < NK:
                        ch(last)
                        ch.wait()
                    else:
                        last.then_inc(e_ready, 1)
                        pool.wait_ge(e_ready, b + 1)
            pool.wait_ge(tile_done, TILE0["ukv"] + 12)
            for t in range(16):
                m = 8 + t if t < 8 else t - 8
                if t >= 4:
                    if t < 12:
                        pool.wait_ge(s_ready, t - 3)
                    else:
                        pool.wait_ge(mg_f, t - 11)
                if t == 8:
                    pool.wait_ge(s_ready, 8)
                if t == 0:
                    for i in range(2):
                        pool.wait_ge(gate_out[i], 16 * 8)
                pool.dma_start(gload[t % 4][:, :], gate_dram[m]).then_inc(gload_in[t % 4], 16)

        @block.scalar
        def _(act):
            ch = Chain(act, act_chain)
            act.wait_ge(vec_ready, 16)
            act.activation(cs[:, :, :].rearrange("p k r -> p r k"), VEC[:, V_C:V_END].rearrange("p (r k) -> p r k", r=2),
                           ACT.Silu).then_inc(cs_ready, 1)
            def sum_squares(t, src):
                return act.activation(junk[:, :], src, ACT.Square, accum_out=stv[:, t:t + 1])

            def mod1_row(p):
                act.wait_ge(mod1_pe, p + 1)
                act.activation(mrow[:, 256 * p:256 * p + 256], bank[6 + p % 2][0:2, 0:256], ACT.Copy).then_inc(mrow_ready, 1)

            mod1_row(0)
            mod1_row(1)
            act.wait_ge(x_in, 16)
            for k in range(KD):
                act.wait_ge(xT_mm, k + 1)
                act.activation(xT[:, k, :], bank[k % 6][:, :], ACT.Copy).then_inc(xT_ready, 1)
                if k % 2:
                    ch.step(sum_squares(k // 2, xtok[:, k // 2, :]))
            mod1_row(2)
            act.wait_ge(ctx_in, 16)
            ch.step(sum_squares(4, ctok[:, 0, :]))
            sum_squares(5, ctok[:, 1, :]).then_inc(sumsq1, 1)
            for p in range(3, 6):
                mod1_row(p)
            act.wait_ge(rstd1_mm, 1)
            act.activation(rstdb[:, C:], bank[1][:, :], ACT.Copy).then_inc(rstd1_ready, 1)
            act.activation(rstdb[:, 0:C], bank[0][:, 0:C], ACT.Copy).then_inc(rstd1_ready, 1)
            for p in range(6, 8):
                mod1_row(p)
            act.wait_ge(sin_arg, 1)
            act.activation(TMP[:, 10:12, :], TMP[:, 8:10, :], ACT.Sin).then_inc(sin_done, 1)
            split_hi(act, 0)
            act.wait_ge(gain1_ready, 2)
            for k in range(KD):
                act.wait_ge(xn_ready, k + 1)
                if k >= 2:
                    act.wait_ge(h_split, k - 1)
                ch(act.activation(hf[k % 2][:, C:], xn[:, k, :], ACT.Identity, scale=gain1[:, 0, k:k + 1], bias=modb[:, k, 0:1]))
                ch(act.activation(h_hi[:, k, :], xn[:, k, :], ACT.Identity, scale=gain1[:, 0, k:k + 1], bias=modb[:, k, 0:1]))
                act.activation(hf[k % 2][:, 0:C], cn[:, k, :], ACT.Identity, scale=gain1[:, 1, k:k + 1],
                               bias=modb[:, k, 1:2]).then_inc(hf_ready, 1)
            split_hi(act, 1)

            def lat_tile(t, i, dst, width_, gain):
                act.wait_ge(tile_done, t + 1)
                if i >= 2:
                    act.wait_ge(stat_mm, i - 1)
                src = bank[6 + t % 2][:, 0:width_]
                act.activation(gst[i % 2][:, 0:width_], src, ACT.Square).then_inc(sq_lat, 1)
                act.activation(dst, src, ACT.Identity, scale=VEC[:, gain:gain + 1]).then_inc(tile_free, 1)

            lat_tiles = [(cq[:, 0, :], T, V_QAG), (cq[:, 1, :], T, V_QAG + 1), (cq[:, 2, :], T, V_QAG + 2),
                         (ckv[:, 0, C:], T, V_KVAG), (ckv[:, 0, 0:C], C, V_KVAG),
                         (ckv[:, 1, C:], T, V_KVAG + 1), (ckv[:, 1, 0:C], C, V_KVAG + 1)]
            for t in range(5):
                if t == 2:
                    split_hi(act, 2)
                lat_tile(t, t, *lat_tiles[t])
            t0 = TILE0["u"]
            for t in range(12):
                if t % 6 == 0:
                    split_hi(act, 3 + t // 6)
                if t >= 4:
                    act.wait_ge(u_out[t % 4], 16 * (t // 4))
                act.wait_ge(tile_done, t0 + t + 1)
                act.activation(ust[t % 4][:, :], bank[(t0 + t) % 2 + 6][:, 0:256], ACT.Copy).then_inc(tile_free, 1)
                act.wait_ge(tile_free, t0 + t + 1)
                act.dma_start(u_dram[P * (t % 6):P * (t % 6) + P, 256 * (t // 6):256 * (t // 6) + 256],
                              ust[t % 4][:, :]).then_inc(u_out[t % 4], 16)
            t0 = TILE0["lat2"]
            for i, (dst, width_) in enumerate(((krT[:, C:], T), (krT[:, 0:C], C))):
                act.wait_ge(tile_done, t0 + i + 1)
                act.activation(dst, bank[6 + (t0 + i) % 2][0:ROPE, 0:width_], ACT.Copy).then_inc(tile_free, 1)
            for i in range(2):
                lat_tile(t0 + 2 + i, 5 + i, *lat_tiles[5 + i])
                if i == 0:
                    split_hi(act, S_OF["gate"][0])

            def group_order(b):
                act.activation(utok[0:NK, b, :].rearrange("p (g j c) -> p g j c", g=GB, j=L),
                               ustage[0:NK, :, P * b:P * b + P].rearrange("p j (g c) -> p g j c", c=GC),
                               ACT.Copy).then_inc(ug_A, 1)

            act.wait_ge(kr_T, 1)
            act.activation(kr[:, :, :].rearrange("p t r -> p (t r)"), bank[5][:, 0:6 * ROPE], ACT.Copy).then_inc(kr_ready, 1)
            act.wait_ge(utok_in, 16 * L)
            group_order(1)
            group_order(3)

            def gate_tile(m, t):
                if m >= 2:
                    act.wait_ge(gate_out[m % 2], 16 * (m // 2))
                act.wait_ge(tile_done, t + 1)
                act.activation(gst[m % 2][:, :], bank[6 + t % 2][:, :], ACT.Sigmoid).then_inc(tile_free, 1)
                act.wait_ge(tile_free, t + 1)
                act.dma_start(gate_dram[m], gst[m % 2][:, :]).then_inc(gate_out[m % 2], 16)

            for b in range(NB):
                t = TILE0["gate"] + 4 * b
                for i in range(2):
                    act.wait_ge(u_T, 2 * b + 1 + i)
                    act.activation(U[:, 4 * i:4 * i + 4, :].rearrange("p g k -> p (g k)"), bank[i][:, 0:4 * NK], ACT.Copy).then_inc(u_evacA, 1)
                act.wait_ge(bp_T, b + 1)
                for d in range(2):
                    act.activation(WinT[:, 0, d].rearrange("p m n -> p (m n)"), bank[2 + d][:, :], ACT.Copy).then_inc(winT_A, 1)
                if b == 0:
                    act.wait_ge(stat_mm, 7)
                gate_tile(4 * b, t)
                gate_tile(4 * b + 1, t + 1)
                split_hi(act, S_OF["gate"][2 * b] + 1)
                act.wait_ge(kf_ready, b + 1)
                act.dma_start(kf_dram[b], Kf[:, :]).then_inc(kf_out, 16)
                gate_tile(4 * b + 2, t + 2)
                act.wait_ge(kf_out, 16 * b + 16)
                for j in range(L):
                    act.dma_start(TTm[GC * j:GC * j + GC, :, :],
                                  kf_dram[b].rearrange("(g c) m -> c g m", c=GC)[:, :, GC * j:GC * j + P]).then_inc(tt_in, 16)
                gate_tile(4 * b + 3, t + 3)
                split_hi(act, S_OF["gate"][2 * b] + 2)
                if b == NB - 1:
                    act.wait_ge(cp_ready, 2 * NB)
                    act.activation(cq_hi[:, :, :], cq[:, :, :], ACT.Copy).then_inc(prep_hi, 1)
                    act.wait_ge(state_ready, 2 * NB)
                    act.activation(ckv_hi[:, :, :], ckv[:, :, :], ACT.Copy).then_inc(prep_hi, 1)
                act.wait_ge(y_mm, b + 1)
                act.activation(Ysb[:, :, :].rearrange("p g k -> p (g k)"), bank[0][:, :], ACT.Copy).then_inc(y_evac, 1)
                act.wait_ge(y_T, b + 1)
                act.activation(ytok[:, :, 0:64].rearrange("p j (g c) -> p g j c", c=GC),
                               bank[1][0:64, :].rearrange("p (g j c) -> p g j c", g=4, j=L), ACT.Copy).then_inc(ytok_A, 1)
                act.wait_ge(y_T2, b + 1)
                act.activation(utok[:, b, 0:L * CK].rearrange("p (j k) -> p j k", j=L), bank[3][:, :].rearrange("p (j k) -> p j k", j=L),
                               ACT.Gelu_apprx_tanh).then_inc(gelu_done, 1)

            for i in range(2):
                act.wait_ge(gate_out[i], 16 * 8)
            for r, name in enumerate(("q_norm_g", "k_norm_g")):
                act.dma_start(qkg[:, r, :], a[name].rearrange("(o n) -> o n", o=1).to_broadcast([P, QK])).then_inc(attn_consts_in, 16)
            act.dma_start(rope[:, :, :], a["rope"].rearrange("(t p) n -> p t n", p=P)).then_inc(attn_consts_in, 16)
            t0 = TILE0["uq"]
            for t in range(8):
                if t % 4 == 0:
                    split_hi(act, S_OF["uq"][0] + 1 + t // 4)
                if t >= 2:
                    act.wait_ge(sq_used, t - 1)
                act.wait_ge(tile_done, t0 + t + 1)
                act.activation(sqt[t % 2][:, 0:384], bank[6 + (t0 + t) % 2][:, 0:384], ACT.Square).then_inc(q_sq, 1)
                act.activation(qsb[:, t % 4, 4 * (t // 4):4 * (t // 4) + 4, :].rearrange("p h d -> p (h d)"),
                               bank[6 + (t0 + t) % 2][:, 0:384], ACT.Copy).then_inc(tile_free, 1)
                if t >= 4:
                    b = t - 4
                    act.activation(y_hi[:, b, :].rearrange("p (k j) -> p j k", j=L), utok[:, b, 0:L * CK].rearrange("p (j k) -> p j k", j=L),
                                   ACT.Copy).then_inc(yprep_hi, 1)
            t0 = TILE0["ukv"]
            split_hi(act, S_OF["glu"][0])
            for t in range(12):
                act.wait_ge(sq_used, 8 + t - 1)
                act.wait_ge(tile_done, t0 + t + 1)
                nope = bank[6 + (t0 + t) % 2][:, :].rearrange("p (h e) -> p h e", h=4)[:, :, 0:NOPE]
                act.activation(sqt[t % 2][:, 0:256].rearrange("p (h e) -> p h e", h=4), nope, ACT.Square).then_inc(q_sq, 1)
                act.activation(ksb[:, t // 2, 4 * (t % 2):4 * (t % 2) + 4, 0:NOPE], nope, ACT.Copy).then_inc(tile_free, 1)

            s0 = S_OF["glu"][0]

            def split_hi_at(s_first, k, i, rounds, wait_sem, wait_value):
                s = s_first + k
                n = N_OF_SPLIT[s]
                act.wait_ge(raw_in[n % 2], raw_in_count(n) + 16 * transfers(STREAM[n]) * (rounds // 2) * i)
                act.wait_ge(wait_sem, wait_value)
                w = width(STREAM[n], N_OF[STREAM[n]].index(n))
                act.activation(whi[s % 2][:, 0:w], raw[n % 2][:, 0:w], ACT.Copy).then_inc(hi_ready, 1)

            t0 = TILE0["glu"]
            for p in range(4):
                split_hi(act, s0 + p + 1)
                for mi in range(2):
                    m = 2 * p + mi
                    act.wait_ge(tile_done, t0 + 2 * m + 2)
                    if m >= 2:
                        act.wait_ge(s_ready, m - 1)
                    act.activation(sg[m % 2][:, :], bank[4 + (2 * m + 1) % 4][:, :], ACT.Sigmoid).then_inc(sg_ready, 1)

            for i in range(0, 24, 2):
                act.wait_ge(qk_T, i + 1)
                dst, w = qk_tile(i)
                act.activation(dst, bank[i % 4][0:QK, 0:w], ACT.Copy).then_inc(qk_A, 1)

            split_hi(act, S_OF["wo"][1])

            def exp(i):
                act.wait_ge(max_ready, i + 1)
                if i >= 2:
                    act.wait_ge(p_T, 2 * (i - 2) + 2)
                act.activation(Pm[i % 2][:, :], ps[:, 2 * (i % 2):2 * (i % 2) + 2, 0:384], ACT.Exp, scale=SCALE,
                               bias=smx[:, i % 4, 1:2], accum_out=smx[:, i % 4, 2:3]).then_inc(exp_ready, 1)

            exp(0)
            for i in range(4 * H):
                act.wait_ge(p_T, 2 * i + 2)
                if i >= 2:
                    act.wait_ge(o_mm, i - 1)
                act.activation(PT[i % 2][:, 3:6, :].rearrange("p a b -> p (a b)"), bank[5][:, 0:384], ACT.Copy).then_inc(pt_A, 1)
                if i + 1 < 4 * H:
                    exp(i + 1)
            for k in range(4):
                act.wait_ge(o_T, k + 1)
                act.activation(oT_hi[:, k, :], bank[k][:, :], ACT.Copy).then_inc(oT_hi_r, 1)
            for m in range(KD):
                if m == 4:
                    split_hi(act, S_OF["wout"][0])
                act.wait_ge(mg_f, m + 1)
                act.activation(mg_hi[:, m, :], mgf[m % 2][:, :], ACT.Copy).then_inc(mg_h, 1)

            for p in range(4):
                split_hi(act, S_OF["wout"][p] + 1)
                for mi in range(2):
                    m = 2 * p + mi
                    act.wait_ge(x1_ready, m + 1)
                    act.activation(sqx[:, m, :], xT[:, m, :], ACT.Square).then_inc(sqx_ready, 1)
            for k in range(KD):
                act.wait_ge(nx_ready, k + 1)
                if k >= 2:
                    act.wait_ge(h2_l, k - 1)
                act.activation(nh[k % 2][:, :], nx[k % 2][:, :], ACT.Identity, scale=gain2[:, k:k + 1],
                               bias=modb[:, 24 + k, 0:1]).then_inc(nh_ready, 1)
                act.activation(h2_hi[:, k, :], nx[k % 2][:, :], ACT.Identity, scale=gain2[:, k:k + 1],
                               bias=modb[:, 24 + k, 0:1]).then_inc(h2_h, 1)

            s0, t0 = S_OF["up"][0], TILE0["up"]

            def up_round(i, j, more):
                f = 2 * i + j
                if more:
                    split_hi_at(s0 + 1, j, i, 2, tile_done, t0 + 4 * i + 2 * j)
                for v in range(2):
                    act.wait_ge(tile_done, t0 + 4 * i + 2 * j + v + 1)
                    act.activation(cv[v][j][:, :], bank[4 + 2 * j + v][:, :], ACT.Identity,
                                   scale=VEC[:, bass.ds(V_W1 + 22 * v + f, 1)],
                                   bias=VEC[:, bass.ds(V_CB + 22 * v + f, 1)]).then_inc(cv_a, 1)
                act.wait_ge(cv_d, 4 * i + 2 * j + 2)
                act.activation(sl[j][:, :], cv[1][j][:, :], ACT.Silu).then_inc(silu_done, 1)
                act.wait_ge(act_f, f + 1)
                act.activation(act_hi[:, bass.ds(f, 1), :], cv[0][j][:, None, :], ACT.Copy).then_inc(act_h, 1)

            up_round(0, 0, True)
            up_round(0, 1, True)
            with act.Fori(1, 10) as i:
                for j in range(2):
                    up_round(i, j, True)
            up_round(10, 0, True)
            split_hi(act, S_OF["down"][0])
            up_round(10, 1, False)

            s0, t0 = S_OF["down"][0], TILE0["down"]

            def rows_out(pair, par):
                for mi in range(2):
                    act.wait_ge(xo_T, 2 * pair + mi + 1)
                    act.activation(ost[par][:, :, P * mi:P * mi + P],
                                   bank[2 * par + mi][:, :].rearrange("p (t n) -> p t n", t=TT_N),
                                   ACT.Copy).then_inc(ost_ready if mi else act_chain, 1)

            for p in range(11):
                split_hi(act, s0 + 1 + p)
                if p in (4, 7, 10):
                    pair = p // 3 - 1
                    if pair >= 2:
                        act.wait_ge(out_done[pair % 2], 16 * (pair // 2))
                    rows_out(pair, pair % 2)
            act.wait_ge(out_done[1], 16)
            rows_out(3, 1)

        @block.vector
        def _(dve):
            ch = Chain(dve, dve_chain)
            V_ = dve

            def tt(o_, x_, y_, op):
                return V_.tensor_tensor(o_, x_, y_, op)

            def ts(o_, x_, s1, s2=None, op0=ALU.mult, op1=ALU.add):
                if s2 is None:
                    return V_.tensor_scalar(o_, x_, s1, None, op0)
                return V_.tensor_scalar(o_, x_, s1, s2, op0, op1)

            def stt_(o_, x_, s, y_, op0, op1):
                return V_.scalar_tensor_tensor(out=o_, in0=x_, scalar=s, in1=y_, op0=op0, op1=op1)

            def rsqrt(y, v, t):
                ch.step(ts(y.bitcast(I32), v.bitcast(I32), -0.5, 1597463007.0))
                for _ in range(3):
                    ch.step(stt_(t, y, -0.5, y, ALU.mult, ALU.mult))
                    ch.step(tt(t, t, v, ALU.mult))
                    ch.step(stt_(y, t, 1.5, y, ALU.add, ALU.mult))

            V_.wait_ge(consts_ready, 1)
            ch.step(V_.tensor_reduce(dmask[:, :], ident[:, :].rearrange("p (g c) -> p c g", c=GC), AX.X, ALU.add))

            def mod_panel(w, acc, r):
                for k in range(KD):
                    if k == 0:
                        ch.step(ts(acc, w[:, k, :], cs[:, k, r:r + 1]))
                    elif k < KD - 1:
                        ch.step(stt_(acc, w[:, k, :], cs[:, k, r:r + 1], acc, ALU.mult, ALU.add))
                    else:
                        return stt_(acc, w[:, k, :], cs[:, k, r:r + 1], acc, ALU.mult, ALU.add)

            V_.wait_ge(cs_ready, 1)
            V_.wait_ge(sumsq1, 1)
            ch.step(ts(stv[:, 0:6], stv[:, 0:6], 1.0 / D, EPS))
            rsqrt(sty[:, 0:6], stv[:, 0:6], stt[:, 0:6])
            for t in range(6):
                ts(diag[:, t, :], ident[:, :], sty[:, t:t + 1]).then_inc(diag1_ready, 1)

            dm = lambda v: v.rearrange("p (d m) -> p d m", d=2)
            lam = VEC[:, V_LAM:V_LAM + 64].rearrange("p (d r m) -> p r d m", d=2, r=2)
            ch(tt(dm(TMP[:, 24, :]), lam[:, 0], lam[:, 0], ALU.mult))
            ch(tt(dm(TMP[:, 30, :]), lam[:, 1], lam[:, 1], ALU.mult))
            ch.wait()
            ch.step(tt(TMP[:, 24, :], TMP[:, 24, :], TMP[:, 30, :], ALU.add))
            V_.reciprocal(TMP[:, 24, :], TMP[:, 24, :]).then_inc(den_ready, 1)

            V_.wait_ge(rstd1_ready, 2)
            for k in range(4):
                V_.wait_ge(xT_mm, KD + k + 1)
                tt(cn[:, 2 * k:2 * k + 2, :], bank[(KD + k) % 6][:, :].rearrange("p (a t) -> p a t", a=2),
                   rstdb[:, None, 0:C].to_broadcast([P, 2, C]), ALU.mult).then_inc(cn_ready, 1)
            V_.wait_ge(mod1_T, 1)
            ch.step(tt(modb[:, 0:16, :], bank[0][:, 0:32].rearrange("p (m r) -> p m r", r=2),
                       VEC[:, V_BMOD:V_BMOD + 16, None].to_broadcast([P, 16, 2]), ALU.add))
            for r in range(2):
                stt_(gain1[:, r, :], modb[:, 8:16, r], 1.0, VEC[:, V_N1:V_N1 + 8], ALU.add, ALU.mult).then_inc(gain1_ready, 1)
            split_lo(dve, 0)
            for k in range(KD):
                V_.wait_ge(hf_ready, k + 1)
                ch(V_.tensor_copy(hc_hi[:, k, :], hf[k % 2][:, 0:C]))
                ch.wait()
                ch(tt(h_lo[:, k, :], hf[k % 2][:, C:], h_hi[:, k, :].bitcast(F32), ALU.subtract))
                tt(hc_lo[:, k, :], hf[k % 2][:, 0:C], hc_hi[:, k, :].bitcast(F32), ALU.subtract).then_inc(h_split, 1)
            split_lo(dve, 1)
            split_lo(dve, 2)
            split_lo(dve, 3)
            split_lo(dve, 4)
            split_lo(dve, 5)

            V_.wait_ge(tile_done, TILE0["u"] + 12)
            V_.wait_ge(utok_in, 16 * L)
            for b in (0, 2):
                V_.tensor_copy(utok[0:NK, b, :].rearrange("p (g j c) -> p g j c", g=GB, j=L),
                               ustage[0:NK, :, P * b:P * b + P].rearrange("p j (g c) -> p g j c", c=GC)).then_inc(ug_D, 1)
            V_.wait_ge(ug_A, 2)
            V_.wait_ge(ug_D, 2)
            for r in range(2):
                V_.memset(SBD[r][0:64, :, :, 1, :], 0.0).then_inc(sbd_zero, 1)
                V_.memset(SBD[r][64:128, :, :, 0, :], 0.0).then_inc(sbd_zero, 1)
            V_.wait_ge(stat_mm, 7)
            ch(V_.tensor_reduce(stv[:, 0:4], bank[4][:, 0:12].rearrange("p (k t) -> p t k", t=TT_N), AX.X, ALU.add))
            V_.tensor_reduce(stv[:, 4:10], bank[4][:, 12:24].rearrange("p (k t) -> p t k", t=CT_N + TT_N), AX.X, ALU.add).then_inc(stat_read, 1)

            def mod2_panel(q):
                n = N_OF["mod2"][q]
                V_.wait_ge(raw_in[n % 2], raw_in_count(n))
                mod_panel(raw[n % 2][:, :].rearrange("p (k n) -> p k n", k=KD),
                          utok[:, q // 4, 256 * (q % 4):256 * (q % 4) + 256], 0).then_inc(mod2_used, 1)

            for b in range(NB):
                V_.wait_ge(u_T, 2 * b + 2)
                mod2_panel(4 * b)
                for i in range(2):
                    V_.wait_ge(u_evacA, 2 * b + 1 + i)
                    src = U[:, 4 * i:4 * i + 4, :]
                    ch(V_.tensor_copy(Ub[:, 4 * i:4 * i + 4, 0:CC], src[:, :, CC - 1::-1]))
                    V_.tensor_copy(Ub[:, 4 * i:4 * i + 4, CC:], src[:, :, NK - 1:CC - 1:-1]).then_inc(u_evacD, 1)
                V_.wait_ge(bp_T, b + 1)
                for d in range(2):
                    V_.tensor_copy(WinT[:, 1, d].rearrange("p m n -> p (m n)"), bank[4 + d][:, :]).then_inc(winT_D, 1)
                for q in range(1, 3):
                    mod2_panel(4 * b + q)
                split_lo(dve, S_OF["gate"][2 * b] + 1)
                V_.wait_ge(t_mm, b + 1)
                if b:
                    V_.wait_ge(kf_out, 16 * b)
                ch(V_.tensor_copy(Kf[:, 0:P], bank[1][:, 0:P]))
                ch(V_.tensor_copy(Kf[:, P:], bank[0][:, GC:P]))
                ch.wait()
                m0, m1 = 16 + 8 * b - (4 if b else 0), 20 + 8 * b
                ch(tt(modb[:, m0:m1, 0], bank[0][:, 264 - (m1 - m0):264], VEC[:, V_BMOD + m0:V_BMOD + m1], ALU.add))
                ch.step(tt(Kf[:, P - GC:P], bank[0][:, 0:GC], Kf[:, P - GC:P], ALU.add))
                stt_(Kf[:, P - GC:P], dmask[:, :], VEC[:, V_DSKIP + b:V_DSKIP + b + 1], Kf[:, P - GC:P],
                     ALU.mult, ALU.add).then_inc(kf_ready, 1)
                V_.wait_ge(e_ready, b + 1)
                if b:
                    V_.wait_ge(y_T2, b)
                for d in range(2):
                    V_.wait_ge(v_mm, 2 * b + 1 + d)
                    if d:
                        V_.wait_ge(kf_out, 16 * b + 16)
                    vr, vi = (bank[2 + 2 * r + d][:, 0:4 * NK].rearrange("p (m k) -> p m k", m=PB) for r in range(2))
                    E = E_[b % 2]
                    ec, es = E[:, 0, 4 * d:4 * d + 4, :], E[:, 1, 4 * d:4 * d + 4, :]
                    ch(tt(W[:, 0, d], vr, ec, ALU.mult))
                    ch(tt(tmpA[:, :, :], vi, es, ALU.mult))
                    ch(tt(W[:, 1, d], vi, ec, ALU.mult))
                    tt(tmpB[:, :, :], vr, es, ALU.mult).then_inc(v_read, 1)
                    V_.wait_ge(v_read, 2 * b + 1 + d)
                    ch.wait()
                    ch(tt(W[:, 0, d], W[:, 0, d], tmpA[:, :, :], ALU.subtract))
                    ch(tt(W[:, 1, d], W[:, 1, d], tmpB[:, :, :], ALU.add))
                    ch.wait()
                    for r in range(2):
                        for m in range(PB):
                            col = 16 * d + PB * b + m
                            w = W[:, r, d, m, :]
                            ch(V_.tensor_tensor_scan(w, r8[:, col:col + 1].to_broadcast([P, NK]), w, 0.0, ALU.mult, ALU.add))
                    ch.wait()
                    at_ = slice(CC - 1, NK - 1) if d == 0 else slice(NK - 2, CC - 2, -1)
                    wr, wi, ec, es = W[:, 0, d][:, :, at_], W[:, 1, d][:, :, at_], ec[:, :, at_], es[:, :, at_]
                    for r, (x1_, y1_, op) in enumerate(((wr, wi, ALU.add), (wi, wr, ALU.subtract))):
                        ch(tt(tmpA[:, :, 0:CK], x1_, ec, ALU.mult))
                        ch(tt(tmpB[:, :, 0:CK], y1_, es, ALU.mult))
                        ch.wait()
                        for g2 in range(2):
                            half = slice(64 * g2, 64 * g2 + 64)
                            ins = tt(SBD[r][half, d, :, g2, :], tmpA[half, :, 0:CK], tmpB[half, :, 0:CK], op)
                            if r == 1 and g2 == 1:
                                ins.then_inc(state_ready, 1)
                                V_.wait_ge(state_ready, 2 * b + 1 + d)
                            else:
                                ch(ins)
                        ch.wait()
                split_lo(dve, S_OF["gate"][2 * b] + 2)
                mod2_panel(4 * b + 3)
                if b == NB - 1:
                    for i, (full, hi, lo) in enumerate(((cq, cq_hi, cq_lo), (ckv, ckv_hi, ckv_lo))):
                        V_.wait_ge(prep_hi, i + 1)
                        tt(lo[:, :, :], full[:, :, :], hi[:, :, :].bitcast(F32), ALU.subtract).then_inc(prep_lo, 1)
                V_.wait_ge(y_T, b + 1)
                V_.tensor_copy(ytok[:, :, 64:128].rearrange("p j (g c) -> p g j c", c=GC),
                               bank[2][0:64, :].rearrange("p (g j c) -> p g j c", g=4, j=L)).then_inc(ytok_D, 1)

            ch(ts(stv[:, 0:4], stv[:, 0:4], 1.0 / QL, EPS))
            ch(ts(stv[:, 4:10], stv[:, 4:10], 1.0 / KVL, EPS))
            ch.wait()
            rsqrt(rl[:, :], stv[:, :], stt[:, :])
            stt_(gain2[:, :], modb[:, 32:40, 0], 1.0, VEC[:, V_N2:V_N2 + 8], ALU.add, ALU.mult).then_inc(gain2_ready, 1)

            V_.wait_ge(attn_consts_in, 48)
            for t in range(8):
                if t % 4 == 0:
                    split_lo(dve, S_OF["uq"][0] + 1 + t // 4)
                V_.wait_ge(q_sq, t + 1)
                c0 = 8 * (t % 4) + 4 * (t // 4)
                V_.tensor_reduce(stq[:, 0, c0:c0 + 4], sqt[t % 2][:, 0:384].rearrange("p (h d) -> p h d", h=4),
                                 AX.X, ALU.add).then_inc(sq_used, 1)
                if t >= 4:
                    b = t - 4
                    V_.wait_ge(yprep_hi, b + 1)
                    tt(y_lo[:, b, :].rearrange("p (k j) -> p j k", j=L), utok[:, b, 0:L * CK].rearrange("p (j k) -> p j k", j=L),
                       y_hi[:, b, :].rearrange("p (k j) -> p j k", j=L).bitcast(F32), ALU.subtract).then_inc(yprep_lo, 1)
            split_lo(dve, S_OF["glu"][0])
            t0 = TILE0["ukv"]
            for t in range(12):
                V_.wait_ge(tile_free, t0 + t + 1)
                ts(V[:, t // 2, 256 * (t % 2):256 * (t % 2) + 256].rearrange("p (h e) -> p h e", h=4),
                   bank[6 + (t0 + t) % 2][:, :].rearrange("p (h e) -> p h e", h=4)[:, :, NOPE:],
                   rl[:, 4 + t // 2:5 + t // 2]).then_inc(v_copy, 1)
                V_.wait_ge(q_sq, 8 + t + 1)
                c0 = 32 + 8 * (t // 2) + 4 * (t % 2)
                V_.tensor_reduce(stq[:, 0, c0:c0 + 4], sqt[t % 2][:, 0:256].rearrange("p (h d) -> p h d", h=4),
                                 AX.X, ALU.add).then_inc(sq_used, 1)

            yprep = None
            qg, kg = qkg[:, 0, :], qkg[:, 1, :]
            rq = stq[:, 0, 0:32].rearrange("p (t h) -> p t h", t=TT_N)[:, :, :, None]
            rk = stq[:, 1, 32:80].rearrange("p (t h) -> p t h", t=6)[:, :, :, None]
            V_.wait_ge(mod2_mm, 1)
            ch(tt(modb[:, 44:48, 0], bank[0][:, 0:4], VEC[:, V_BMOD + 44:V_BMOD + 48], ALU.add))
            rkn = stq[:, 0, 32:80].rearrange("p (t h) -> p t h", t=6)[:, :, :, None]
            tq_ = [tq[:, i, :].rearrange("p (t h c) -> p t h c", t=TT_N, h=H) for i in range(4)]

            def qk_norm_part(m):
                if m == 0:
                    V_.wait_ge(sq_used, 20)
                    V_.wait_ge(kr_ready, 1)
                    V_.wait_ge(tile_free, TILE0["glu"])
                    ch.step(tt(sqt[0][:, 0:192].rearrange("p (t r) -> p t r", t=6), kr[:, :, :], kr[:, :, :], ALU.mult))
                    ch.step(V_.tensor_reduce(stq3[:, :], sqt[0][:, 0:192].rearrange("p (t r) -> p t r", t=6), AX.X, ALU.add))
                    ks = stq[:, 0, 32:80].rearrange("p (t h) -> p t h", t=6)
                    qs, r_q = stq[:, 0, 0:32].rearrange("p (t h) -> p t h", t=TT_N), rl[:, 0:4, None].to_broadcast([P, TT_N, H])
                    r_k = rl[:, 4:10, None].to_broadcast([P, 6, H])
                    for _ in range(2):
                        ch(tt(qs, qs, r_q, ALU.mult))
                        ch.step(tt(ks, ks, r_k, ALU.mult))
                    ch.step(tt(ks, ks, stq3[:, :, None].to_broadcast([P, 6, H]), ALU.add))
                    ch.step(ts(stq[:, 0, :], stq[:, 0, :], 1.0 / QK, EPS))
                    rsqrt(stq[:, 1, :], stq[:, 0, :], sqt[1][:, 0:80])
                    ch(tt(qs, stq[:, 1, 0:32].rearrange("p (t h) -> p t h", t=TT_N), r_q, ALU.mult))
                    ch.step(tt(ks, stq[:, 1, 32:80].rearrange("p (t h) -> p t h", t=6), r_k, ALU.mult))
                elif m == 1:
                    ch.step(tt(qsb[:, :, :, :], qsb[:, :, :, :], rq.to_broadcast([P, TT_N, H, QK]), ALU.mult))
                elif m == 2:
                    ch.step(tt(qsb[:, :, :, :], qsb[:, :, :, :], qg[:, None, None, :].to_broadcast([P, TT_N, H, QK]), ALU.mult))
                elif m == 3:
                    r1, r2 = qsb[:, :, :, 64:80], qsb[:, :, :, 80:96]
                    sh4 = [P, TT_N, H, 16]
                    co, si = rope[:, :, None, 0:16].to_broadcast(sh4), rope[:, :, None, 16:32].to_broadcast(sh4)
                    ch(tt(tq_[0], r1, co, ALU.mult))
                    ch(tt(tq_[1], r2, si, ALU.mult))
                    ch(tt(tq_[2], r1, si, ALU.mult))
                    ch(tt(tq_[3], r2, co, ALU.mult))
                    ch.wait()
                    ch(tt(r1, tq_[0], tq_[1], ALU.subtract))
                    tt(r2, tq_[2], tq_[3], ALU.add).then_inc(q_ready, 1)
                elif m == 4:
                    kn = ksb[:, :, :, 0:NOPE]
                    ch.step(tt(kn, kn, rkn.to_broadcast([P, 6, H, NOPE]), ALU.mult))
                elif m == 5:
                    kn = ksb[:, :, :, 0:NOPE]
                    ch(tt(kn, kn, kg[:, None, None, 0:NOPE].to_broadcast([P, 6, H, NOPE]), ALU.mult))
                elif m == 6:
                    V_.wait_ge(q_ready, 1)
                    ch.step(tt(kr[:, :, :], kr[:, :, :], kg[:, None, NOPE:].to_broadcast([P, 6, ROPE]), ALU.mult))
                    r1, r2 = kr[:, CT_N:, 0:16], kr[:, CT_N:, 16:32]
                    co, si = rope[:, :, 0:16], rope[:, :, 16:32]
                    tk = [tq[:, i, 0:64].rearrange("p (t c) -> p t c", t=TT_N) for i in range(4)]
                    ch(tt(tk[0], r1, co, ALU.mult))
                    ch(tt(tk[1], r2, si, ALU.mult))
                    ch(tt(tk[2], r1, si, ALU.mult))
                    ch(tt(tk[3], r2, co, ALU.mult))
                    ch.wait()
                    ch(tt(r1, tk[0], tk[1], ALU.subtract))
                    ch.step(tt(r2, tk[2], tk[3], ALU.add))
                    tt(ksb[:, :, :, NOPE:], kr[:, :, None, :].to_broadcast([P, 6, H, ROPE]),
                       rk.to_broadcast([P, 6, H, ROPE]), ALU.mult).then_inc(k_ready, 1)

            t0 = TILE0["glu"]
            for m in range(KD):
                if m % 2 == 0:
                    split_lo(dve, S_OF["glu"][m // 2] + 1)
                qk_norm_part(m)
                V_.wait_ge(sg_ready, m + 1)
                V_.wait_ge(gload_in[m % 4], 16 * (m // 4 + 1))
                ch.step(tt(sg[m % 2][:, :], sg[m % 2][:, :], gload[m % 4][:, :], ALU.mult))
                V_.wait_ge(tile_done, t0 + 2 * m + 1)
                tt(sT[:, m, :], bank[4 + (2 * m) % 4][:, :], sg[m % 2][:, :], ALU.mult).then_inc(s_ready, 1)

            for i in range(1, 24, 2):
                V_.wait_ge(qk_T, i + 1)
                dst, w = qk_tile(i)
                V_.tensor_copy(dst, bank[i % 4][0:QK, 0:w]).then_inc(qk_D, 1)
            split_lo(dve, S_OF["wo"][1])

            def row_max(i):
                V_.wait_ge(s_mm, i + 1)
                if i >= 4:
                    V_.wait_ge(exp_ready, i - 3)
                ch.step(V_.tensor_reduce(smx[:, i % 4, 0:1], ps[:, 2 * (i % 2):2 * (i % 2) + 2, 0:384], AX.XY, ALU.max))
                ts(smx[:, i % 4, 1:2], smx[:, i % 4, 0:1], -SCALE).then_inc(max_ready, 1)

            def o_out(i):
                h, q = i // 4, i % 4
                V_.wait_ge(exp_ready, i + 1)
                ch.step(V_.reciprocal(smx[:, i % 4, 3:4], smx[:, i % 4, 2:3]))
                V_.wait_ge(o_mm, i + 1)
                ts(otok[:, q, VD * h:VD * h + VD], bank[6 + i % 2][:, 0:VD], smx[:, i % 4, 3:4]).then_inc(o_evac, 1)

            row_max(0)
            for i in range(4 * H):
                if i + 1 < 4 * H:
                    row_max(i + 1)
                V_.wait_ge(p_T, 2 * i + 1)
                if i >= 2:
                    V_.wait_ge(o_mm, i - 1)
                V_.tensor_copy(PT[i % 2][:, 0:3, :].rearrange("p a b -> p (a b)"), bank[4][:, 0:384]).then_inc(pt_D, 1)
                if i >= 1:
                    o_out(i - 1)
            o_out(4 * H - 1)
            for k in range(4):
                V_.wait_ge(oT_hi_r, k + 1)
                tt(oT_lo[:, k, :], bank[k][:, :], oT_hi[:, k, :].bitcast(F32), ALU.subtract).then_inc(oT_lo_r, 1)

            def merged_lo(m):
                V_.wait_ge(mg_h, m + 1)
                tt(mg_lo[:, m, :], mgf[m % 2][:, :], mg_hi[:, m, :].bitcast(F32), ALU.subtract).then_inc(mg_l, 1)

            t0 = TILE0["wo"]
            for m in range(KD):
                V_.wait_ge(tile_done, t0 + m + 1)
                V_.wait_ge(gload_in[m % 4], 16 * (2 + m // 4 + 1))
                if m >= 2:
                    V_.wait_ge(mg_l, m - 1)
                ch.step(tt(mgf[m % 2][:, :], bank[6 + m % 2][:, :], gload[m % 4][:, :], ALU.mult))
                tt(mgf[m % 2][:, :], mgf[m % 2][:, :], sT[:, m, :], ALU.add).then_inc(mg_f, 1)
                if m >= 1:
                    merged_lo(m - 1)
                if m == 5:
                    split_lo(dve, S_OF["wout"][0])
            merged_lo(KD - 1)

            t0 = TILE0["wout"]
            V_.wait_ge(xT_back, 16)
            for p in range(4):
                split_lo(dve, S_OF["wout"][p] + 1)
                for mi in range(2):
                    m = 2 * p + mi
                    V_.wait_ge(tile_done, t0 + m + 1)
                    stt_(xT[:, m, :], bank[6 + m % 2][:, :], modb[:, 16 + m, 0:1], xT[:, m, :], ALU.mult, ALU.add).then_inc(x1_ready, 1)
            V_.wait_ge(stat2_mm, 1)
            ch.step(V_.tensor_reduce(stv[:, 0:4], bank[0][:, 0:32].rearrange("p (m q) -> p q m", q=TT_N), AX.X, ALU.add))
            ch.step(ts(stv[:, 0:4], stv[:, 0:4], 1.0 / D, EPS))
            rsqrt(sty[:, 0:4], stv[:, 0:4], stt[:, 0:4])
            for t in range(TT_N):
                ts(diag3[:, t, :], ident[:, :], sty[:, t:t + 1]).then_inc(diag3_ready, 1)
            V_.wait_ge(rstd3_mm, 1)
            for k in range(KD + 1):
                if k < KD:
                    if k >= 2:
                        V_.wait_ge(nh_ready, k - 1)
                    tt(nx[k % 2][:, :], xT[:, k, :], bank[1][:, :], ALU.mult).then_inc(nx_ready, 1)
                if k >= 1:
                    V_.wait_ge(h2_h, k)
                    tt(h2_lo[:, k - 1, :], nh[(k - 1) % 2][:, :], h2_hi[:, k - 1, :].bitcast(F32), ALU.subtract).then_inc(h2_l, 1)

            s0, t0 = S_OF["up"][0], TILE0["up"]

            def up_round(i, j, more):
                f = 2 * i + j
                if more:
                    s = s0 + 1 + j
                    V_.wait_ge(hi_ready, s + 1 + 2 * i)
                    V_.tensor_tensor(wlo[s % 2][:, :], raw[N_OF_SPLIT[s] % 2][:, :], whi[s % 2][:, :].bitcast(F32),
                                     ALU.subtract).then_inc(lo_ready, 1)
                for v in range(2):
                    u_ = bank[4 + 2 * j + v]
                    V_.wait_ge(cv_a, 4 * i + 2 * j + v + 1)
                    ch.step(stt_(cv[v][j][:, 1:], u_[:, 0:T - 1], VEC[:, bass.ds(V_W0 + 22 * v + f, 1)], cv[v][j][:, 1:],
                                 ALU.mult, ALU.add))
                    stt_(cv[v][j][:, 0:T - 1], u_[:, 1:], VEC[:, bass.ds(V_W2 + 22 * v + f, 1)], cv[v][j][:, 0:T - 1],
                         ALU.mult, ALU.add).then_inc(cv_d, 1)
                V_.wait_ge(silu_done, f + 1)
                tt(cv[0][j][:, :], cv[0][j][:, :], sl[j][:, :], ALU.mult).then_inc(act_f, 1)
                V_.wait_ge(act_h, f + 1)
                tt(act_lo[:, bass.ds(f, 1), :], cv[0][j][:, None, :], act_hi[:, bass.ds(f, 1), :].bitcast(F32),
                   ALU.subtract).then_inc(act_l, 1)

            up_round(0, 0, True)
            up_round(0, 1, True)
            with dve.Fori(1, 10) as i:
                ch.enter(i - 1, 4)
                for j in range(2):
                    up_round(i, j, True)
                ch.leave(9)
            up_round(10, 0, True)
            split_lo(dve, S_OF["down"][0])
            up_round(10, 1, False)

            s0, t0 = S_OF["down"][0], TILE0["down"]
            for p in range(12):
                if p < 11:
                    split_lo(dve, s0 + p + 1)
                if p % 3 == 2:
                    pair = p // 3
                    if pair >= 2:
                        V_.wait_ge(xo_T, 2 * (pair - 2) + 2)
                    for mi in range(2):
                        m = 2 * pair + mi
                        V_.wait_ge(tile_done, t0 + m + 1)
                        stt_(xo[pair % 2][:, mi, :], bank[4 + m % 4][:, :], modb[:, 40 + m, 0:1], xT[:, m, :],
                             ALU.mult, ALU.add).then_inc(xo_ready, 1)

        @block.tensor
        def _(pe):
            def product(out_, wx, last=True, first=True):
                ins = None
                for i, (w_, x_) in enumerate(wx):
                    ins = pe.matmul(out_, w_, x_, start=(first and i == 0), stop=(last and i == len(wx) - 1))
                return ins

            def three(s_hi, s_lo, m_hi, m_lo):
                return [(s_hi, m_hi), (s_hi, m_lo), (s_lo, m_hi)]

            def tok(k, t):
                if t < CT_N:
                    return hc_hi[:, k, P * t:P * t + P], hc_lo[:, k, P * t:P * t + P]
                return h_hi[:, k, P * (t - CT_N):P * (t - CT_N) + P], h_lo[:, k, P * (t - CT_N):P * (t - CT_N) + P]

            def panel(s, k_tiles, w):
                pe.wait_ge(lo_ready, s + 1)
                return [b_[s % 2][:, 0:k_tiles * w].rearrange("p (k n) -> p k n", k=k_tiles) for b_ in (whi, wlo)]

            def mod1_products(p, buf, signal, value):
                pe.wait_ge(signal, value)
                if p >= 2:
                    pe.wait_ge(mrow_ready, p - 1)
                w = buf[:, :].rearrange("p (k n) -> p k n", k=KD)
                product(bank[6 + p % 2][0:2, 0:256], [(cs[:, k, :], w[:, k, :]) for k in range(KD)]).then_inc(mod1_pe, 1)

            pe.wait_ge(cs_ready, 1)
            for p in range(2):
                mod1_products(p, raw[p], raw_in[p], 16)

            pe.wait_ge(consts_ready, 1)
            pe.wait_ge(x_in, 16)
            for k in range(KD):
                if k >= 6:
                    pe.wait_ge(xT_ready, k - 5)
                for t in range(TT_N):
                    ins = pe.transpose(bank[k % 6][:, P * t:P * t + P], xtok[:, t, P * k:P * k + P], ident[:, :])
                ins.then_inc(xT_mm, 1)


            pe.wait_ge(ctx_in, 16)
            for k2 in range(KD // 2):
                pe.wait_ge(xT_ready, k2 + 3)
                for a_ in range(2):
                    for t in range(CT_N):
                        ins = pe.transpose(bank[(KD + k2) % 6][:, C * a_ + P * t:C * a_ + P * t + P],
                                           ctok[:, t, P * (2 * k2 + a_):P * (2 * k2 + a_) + P], ident[:, :])
                ins.then_inc(xT_mm, 1)
            for p in range(2, 6):
                mod1_products(p, early[p - 2], early_in[p - 2], 16)

            pe.wait_ge(diag1_ready, TT_N + CT_N)
            pe.wait_ge(xT_ready, KD)
            for t in range(TT_N + CT_N):
                ins = pe.matmul(bank[0 if t >= TT_N else 1][:, P * (t % TT_N):P * (t % TT_N) + P], ones[:, :], diag[:, t, :], start=True, stop=True)
            ins.then_inc(rstd1_mm, 1)
            for p in range(6, 8):
                mod1_products(p, early[p - 2], early_in[p - 2], 16)

            pe.wait_ge(mrow_ready, 8)
            pe.wait_ge(rstd1_ready, 2)
            for m in range(16):
                ins = pe.transpose(bank[0][:, 2 * m:2 * m + 2], mrow[:, P * m:P * m + P], ident[0:2, 0:2])
            ins.then_inc(mod1_T, 1)

            def next_tile(t):
                if t >= 2:
                    pe.wait_ge(tile_free, t - 1)
                return bank[6 + t % 2]

            def lat_products(t, out_, wh, wl, cols, x, ks):
                xh, xl = x
                for k in ks:
                    ins = product(out_, three(wh[:, k, cols], wl[:, k, cols], xh[:, k, :], xl[:, k, :]),
                                  first=k == 0, last=k == KD - 1)
                if KD - 1 in ks:
                    ins.then_inc(tile_done, 1)

            low, high, of_x, of_ctx = slice(0, P), slice(P, 2 * P), (h_hi, h_lo), (hc_hi, hc_lo)
            wh, wl = panel(S_OF["lat"][0], KD, 256)
            for k in range(KD):
                pe.wait_ge(h_split, k + 1)
                lat_products(0, bank[6], wh, wl, low, of_x, [k])
                lat_products(1, bank[7], wh, wl, high, of_x, [k])
            def stat_job(i):
                pe.wait_ge(sq_lat, i + 1)
                if i < 3:
                    tiles, c0 = TT_N, TT_N * i
                else:
                    k, of_c = (i - 3) // 2, (i - 3) % 2
                    tiles, c0 = (CT_N, 12 + 6 * k) if of_c else (TT_N, 12 + 6 * k + CT_N)
                for tt_ in range(tiles):
                    ins = pe.matmul(bank[4][:, c0 + tt_:c0 + tt_ + 1], gst[i % 2][:, P * tt_:P * tt_ + P], ones[:, 0:1], start=True, stop=True)
                ins.then_inc(stat_mm, 1)

            t = 2
            wh, wl = panel(S_OF["lat"][1], KD, 256)
            pe.wait_ge(cn_ready, 4)
            for i, (cols, x) in enumerate(((low, of_x), (high, of_x), (high, of_ctx))):
                lat_products(t, next_tile(t)[:, 0:C if x is of_ctx else T], wh, wl, cols, x, range(KD))
                stat_job(i)
                t += 1

            for p in range(2):
                wh, wl = panel(S_OF["u"][p], KD, 256)
                for tt_ in range(CT_N + TT_N):
                    product(next_tile(t)[:, 0:256],
                            [q_ for k in range(KD) for q_ in three(*tok(k, tt_), wh[:, k, :], wl[:, k, :])]).then_inc(tile_done, 1)
                    t += 1
                    if p == 0 and tt_ < 2:
                        stat_job(3 + tt_)

            wh, wl = panel(S_OF["lat"][2], KD, 160)
            for cols, x in ((slice(P, P + ROPE), of_x), (slice(P, P + ROPE), of_ctx), (low, of_x), (low, of_ctx)):
                rows_ = cols.stop - cols.start
                lat_products(t, next_tile(t)[0:rows_, 0:C if x is of_ctx else T], wh, wl, cols, x, range(KD))
                t += 1
            for tt_ in range(CT_N + TT_N):
                ins = pe.transpose(bank[5][:, ROPE * tt_:ROPE * tt_ + ROPE], krT[:, P * tt_:P * tt_ + P], ident[0:ROPE, 0:ROPE])
            ins.then_inc(kr_T, 1)

            def gate_panel(i, t):
                wh, wl = panel(S_OF["gate"][i], KD, 256)
                for mi in range(2):
                    col = P * mi
                    product(next_tile(t + mi), [q_ for k in range(KD) for q_ in three(
                        wh[:, k, col:col + P], wl[:, k, col:col + P], h_hi[:, k, :], h_lo[:, k, :])]).then_inc(tile_done, 1)

            pe.wait_ge(ug_A, 2)
            pe.wait_ge(ug_D, 2)
            for b in range(NB):
                t = TILE0["gate"] + 4 * b
                for g in range(GB):
                    if b >= 1 and g == 0:
                        pe.wait_ge(y_evac, b)
                    if b >= 1 and g == 4:
                        pe.wait_ge(ytok_A, b)
                    ins = pe.transpose(bank[g // 4][:, NK * (g % 4):NK * (g % 4) + NK],
                                       utok[0:NK, b, P * g:P * g + P], ident[0:NK, 0:NK])
                    if g % 4 == 3:
                        ins.then_inc(u_T, 1)
                if b == 0:
                    stat_job(5)
                    stat_job(6)
                    pe.wait_ge(stat_read, 1)
                    pe.wait_ge(kr_ready, 1)
                pe.wait_ge(bp_ready, 2 * b + 2)
                if b >= 1:
                    pe.wait_ge(v_read, 2 * b)
                    pe.wait_ge(ytok_D, b)
                    pe.wait_ge(gelu_done, b)
                for r in range(2):
                    for d in range(2):
                        for m in range(PB):
                            ins = pe.transpose(bank[2 + 2 * r + d][:, P * m:P * m + P], BP[:, r, d, m, :], ident[:, :])
                ins.then_inc(bp_T, 1)
                gate_panel(2 * b, t)
                pe.wait_ge(cp_ready, 2 * b + 2)
                pe.wait_ge(u_evacA, 2 * b + 2)
                pe.wait_ge(u_evacD, 2 * b + 2)
                pe.wait_ge(mod2_used, 4 * b + 2)
                for q in range(0 if b else 4, 8):
                    pb, c0 = (b, P * (q - 4)) if q >= 4 else (b - 1, P * (q + 4))
                    pe.matmul(bank[0][:, 256 + q:257 + q], utok[:, pb, c0:c0 + P], ones[:, 0:1], start=True, stop=True)
                for m in range(PB):
                    for d in range(2):
                        c0 = GC * d
                        ins = product(bank[d][32 * m:32 * m + 32, 0:P],
                                      [(bbd[:, r, d, m, :], CP_[b % 2][:, r, d, m, c0:c0 + P]) for r in range(2)])
                ins.then_inc(t_mm, 1)
                pe.wait_ge(winT_A, 2 * b + 2)
                pe.wait_ge(winT_D, 2 * b + 2)
                for d in range(2):
                    u_ = Ub if d else U
                    for r in range(2):
                        for m in range(PB):
                            for g2 in range(2):
                                ins = pe.matmul(bank[2 + 2 * r + d][64 * g2:64 * g2 + 64, NK * m:NK * m + NK],
                                                WinT[:, r, d, m, 64 * g2:64 * g2 + 64], u_[:, 2 * m + g2, :], start=True, stop=True)
                    ins.then_inc(v_mm, 1)
                gate_panel(2 * b + 1, t + 2)
                pe.wait_ge(kf_ready, b + 1)
                pe.wait_ge(state_ready, 2 * b + 2)
                pe.wait_ge(sbd_zero, 4)
                pe.wait_ge(tt_in, 16 * L * (b + 1))
                for m in range(PB):
                    product(bank[0][:, P * m:P * m + P],
                            [(CP_[b % 2][:, r, d, m, GC * (1 - d):GC * (1 - d) + P], SBD[r][:, d, m].rearrange("p g k -> p (g k)"))
                             for d in range(2) for r in range(2)], last=False)
                    for g2 in range(2):
                        g = 2 * m + g2
                        ins = pe.matmul(bank[0][:, CK * g:CK * g + CK], TTm[:, g, :], U[:, g, CC:], start=False, stop=g2 == 1)
                ins.then_inc(y_mm, 1)
                pe.wait_ge(y_evac, b + 1)
                for g in range(GB):
                    ins = pe.transpose(bank[1 + g // 4][0:CK, P * (g % 4):P * (g % 4) + P], Ysb[:, g, :], ident[:, :])
                ins.then_inc(y_T, 1)
                pe.wait_ge(ytok_A, b + 1)
                pe.wait_ge(ytok_D, b + 1)
                for j in range(L):
                    ins = pe.transpose(bank[3][:, CK * j:CK * j + CK], ytok[:, j, :], ident[0:CK, 0:CK])
                ins.then_inc(y_T2, 1)

            t = TILE0["uq"]
            pe.wait_ge(prep_lo, 1)
            for p in range(2):
                wh, wl = panel(S_OF["uq"][p], 3, 384)
                for tt_ in range(TT_N):
                    product(next_tile(t)[:, 0:384], [q_ for k in range(3) for q_ in three(
                        cq_hi[:, k, P * tt_:P * tt_ + P], cq_lo[:, k, P * tt_:P * tt_ + P], wh[:, k, :], wl[:, k, :])]).then_inc(tile_done, 1)
                    t += 1
            pe.wait_ge(prep_lo, 2)
            wh, wl = panel(S_OF["ukv"][0], 2, 1024)
            for tt_ in range(CT_N + TT_N):
                for half in range(2):
                    n_ = 2 * tt_ + half
                    if n_ >= 2:
                        pe.wait_ge(v_copy, n_ - 1)
                    product(next_tile(t), [q_ for k in range(2) for q_ in three(
                        ckv_hi[:, k, P * tt_:P * tt_ + P], ckv_lo[:, k, P * tt_:P * tt_ + P],
                        wh[:, k, 512 * half:512 * half + 512], wl[:, k, 512 * half:512 * half + 512])]).then_inc(tile_done, 1)
                    t += 1

            pe.wait_ge(mod2_used, 4 * NB)
            for q in range(4):
                ins = pe.matmul(bank[0][:, q:q + 1], utok[:, NB - 1, P * (q + 4):P * (q + 5)], ones[:, 0:1], start=True, stop=True)
            ins.then_inc(mod2_mm, 1)

            pe.wait_ge(yprep_lo, NB)
            for p in range(4):
                wh, wl = panel(S_OF["glu"][p], 4, 512)
                for mi in range(2):
                    m = 2 * p + mi
                    if m == 1:
                        pe.wait_ge(tile_free, TILE0["glu"])
                        pe.wait_ge(v_copy, 12)
                    if m >= 2:
                        pe.wait_ge(s_ready, m - 1)
                        pe.wait_ge(sg_ready, m - 1)
                    for v in range(2):
                        col = 256 * v + P * mi
                        product(bank[4 + (2 * m + v) % 4], [q_ for k in range(4) for q_ in three(
                            wh[:, k, col:col + P], wl[:, k, col:col + P], y_hi[:, k, :], y_lo[:, k, :])]).then_inc(tile_done, 1)

            pe.wait_ge(q_ready, 1)
            for i in range(24):
                if i == H:
                    pe.wait_ge(k_ready, 1)
                if i >= 4:
                    pe.wait_ge(qk_D if i % 2 else qk_A, (i - 4) // 2 + 1)
                if i < H:
                    src = [qsb[:, tt_, i, :] for tt_ in range(TT_N)]
                else:
                    h, part = (i - H) // 2, (i - H) % 2
                    src = [ksb[:, tt_, h, :] for tt_ in ((4, 5) if part else (0, 1, 2, 3))]
                for j, s_ in enumerate(src):
                    ins = pe.transpose(bank[i % 4][0:QK, P * j:P * j + P], s_, ident[:, :])
                ins.then_inc(qk_T, 1)

            def scores(i):
                h, q = i // 4, i % 4
                if i >= 2:
                    pe.wait_ge(exp_ready, i - 1)
                for j in range(2):
                    ins = pe.matmul(bank[2 * (i % 2) + j][:, 0:384], qT[:, h, P * q:P * q + P],
                                    kT[:, h, 384 * j:384 * j + 384], start=True, stop=True)
                ins.then_inc(s_mm, 1)

            def turn_probs(i):
                pe.wait_ge(exp_ready, i + 1)
                for half in range(2):
                    if i >= 1:
                        pe.wait_ge(pt_A if half else pt_D, i)
                    for j in range(3):
                        ins = pe.transpose(bank[4 + half][:, P * j:P * j + P],
                                           Pm[i % 2][:, P * (3 * half + j):P * (3 * half + j) + P], ident[:, :])
                    ins.then_inc(p_T, 1)

            def weigh_values(i):
                h = i // 4
                pe.wait_ge(pt_D, i + 1)
                pe.wait_ge(pt_A, i + 1)
                if i >= 2:
                    pe.wait_ge(o_evac, i - 1)
                product(bank[6 + i % 2][:, 0:VD], [(PT[i % 2][:, kt, :], V[:, kt, VD * h:VD * h + VD]) for kt in range(6)]).then_inc(o_mm, 1)

            pe.wait_ge(qk_A, 12)
            pe.wait_ge(qk_D, 12)
            pe.wait_ge(s_ready, KD)
            scores(0)
            for i in range(4 * H):
                if i + 1 < 4 * H:
                    scores(i + 1)
                turn_probs(i)
                if i >= 1:
                    weigh_values(i - 1)
            weigh_values(4 * H - 1)

            pe.wait_ge(o_evac, 4 * H)
            for k in range(4):
                for q in range(TT_N):
                    ins = pe.transpose(bank[k][:, P * q:P * q + P], otok[:, q, P * k:P * k + P], ident[:, :])
                ins.then_inc(o_T, 1)
            for p in range(2):
                wh, wl = panel(S_OF["wo"][p], 4, 512)
                for mi in range(4):
                    m = 4 * p + mi
                    if m >= 2:
                        pe.wait_ge(mg_f, m - 1)
                    for k in range(4):
                        if m == 0:
                            pe.wait_ge(oT_lo_r, k + 1)
                        ins = product(bank[6 + m % 2], three(wh[:, k, P * mi:P * mi + P], wl[:, k, P * mi:P * mi + P],
                                                             oT_hi[:, k, :], oT_lo[:, k, :]), first=k == 0, last=k == 3)
                    ins.then_inc(tile_done, 1)
            def square_sums(m):
                pe.wait_ge(sqx_ready, m + 1)
                for q in range(TT_N):
                    ins = pe.matmul(bank[0][:, TT_N * m + q:TT_N * m + q + 1], sqx[:, m, P * q:P * q + P], ones[:, 0:1], start=True, stop=True)
                return ins

            for p in range(4):
                wh, wl = panel(S_OF["wout"][p], KD, 256)
                for mi in range(2):
                    m = 2 * p + mi
                    if m == 0:
                        pe.wait_ge(mg_f, KD)
                    if m >= 2:
                        pe.wait_ge(x1_ready, m - 1)
                    for k in range(KD):
                        if m == 0:
                            pe.wait_ge(mg_l, k + 1)
                        ins = product(bank[6 + m % 2], three(wh[:, k, P * mi:P * mi + P], wl[:, k, P * mi:P * mi + P],
                                                             mg_hi[:, k, :], mg_lo[:, k, :]), first=k == 0, last=k == KD - 1)
                    ins.then_inc(tile_done, 1)
                    if m >= 2:
                        square_sums(m - 2)

            square_sums(KD - 2)
            square_sums(KD - 1).then_inc(stat2_mm, 1)
            pe.wait_ge(diag3_ready, TT_N)
            for q in range(TT_N):
                ins = pe.matmul(bank[1][:, P * q:P * q + P], ones[:, :], diag3[:, q, :], start=True, stop=True)
            ins.then_inc(rstd3_mm, 1)

            s0 = S_OF["up"][0]

            def up_panel(i, j):
                s = s0 + j
                pe.wait_ge(lo_ready, s + 1 + 2 * i)
                return [b_[s % 2][:, :].rearrange("p (k v n) -> p k v n", k=KD, v=2) for b_ in (whi, wlo)]

            def up_products(i, j):
                wh, wl = up_panel(i, j)
                for v in range(2):
                    product(bank[4 + 2 * j + v], [q_ for k in range(KD) for q_ in three(
                        wh[:, k, v, :], wl[:, k, v, :], h2_hi[:, k, :], h2_lo[:, k, :])]).then_inc(tile_done, 1)

            wh, wl = up_panel(0, 0)
            for k in range(KD):
                pe.wait_ge(h2_l, k + 1)
                for v in range(2):
                    ins = product(bank[4 + v], three(wh[:, k, v, :], wl[:, k, v, :], h2_hi[:, k, :], h2_lo[:, k, :]),
                                  first=k == 0, last=k == KD - 1)
                    if k == KD - 1:
                        ins.then_inc(tile_done, 1)
            up_products(0, 1)
            with pe.Fori(1, 11) as i:
                for j in range(2):
                    pe.wait_ge(cv_d, 4 * i + 2 * j - 2)
                    up_products(i, j)

            s0 = S_OF["down"][0]
            pe.wait_ge(cv_d, 2 * KF)

            def turn_out(pair):
                for mi in range(2):
                    pe.wait_ge(xo_ready, 2 * pair + mi + 1)
                    if pair >= 2 and mi == 0:
                        pe.wait_ge(ost_ready, pair - 1)
                    for tt_ in range(TT_N):
                        ins = pe.transpose(bank[2 * (pair % 2) + mi][:, P * tt_:P * tt_ + P],
                                           xo[pair % 2][:, mi, P * tt_:P * tt_ + P], ident[:, :])
                    ins.then_inc(xo_T, 1)

            for pair in range(4):
                for kk in range(3):
                    n_k = (8, 8, 6)[kk]
                    wh, wl = panel(s0 + 3 * pair + kk, n_k, 256)
                    pe.wait_ge(act_l, 8 * kk + n_k)
                    for mi in range(2):
                        m = 2 * pair + mi
                        if kk == 0 and m >= 4:
                            pe.wait_ge(xo_ready, m - 3)
                        ins = product(bank[4 + m % 4], [q_ for k in range(n_k) for q_ in three(
                            wh[:, k, P * mi:P * mi + P], wl[:, k, P * mi:P * mi + P],
                            act_hi[:, 8 * kk + k, :], act_lo[:, 8 * kk + k, :])], first=kk == 0, last=kk == 2)
                        if kk == 2:
                            ins.then_inc(tile_done, 1)
                    if kk < 2:
                        ins.then_inc(down_used, 1)
                    if kk == 0 and pair >= 1:
                        turn_out(pair - 1)
            turn_out(3)


NAMES = ["x", "ctx", "w_mod", "w_in", "w_uq", "w_ukv", "q_norm_g", "k_norm_g", "w_o_attn", "w_glu", "w_out", "w_up", "w_down"]


def vector_columns(one):
    def cols(v):
        return v.reshape(-1, P).T

    def pair_states(v):
        return v.reshape(NP, 2, NS).reshape(NP, P).T

    parts = [cols(one[n]) for n in ("b_mod", "norm1_g", "norm2_g", "d_skip", "q_a_g", "kv_a_g")]
    parts += [cols(one["conv_w"][w]) for w in range(3)] + [cols(one["conv_b"])]
    parts += [pair_states(one[n]) for n in ("lam_re_f", "lam_im_f", "lam_re_b", "lam_im_b")]
    parts += [pair_states(np.repeat(one[n], NS)) for n in ("log_dt_f", "log_dt_b")]
    parts += [one[n].reshape(P, KD) for n in ("c", "c_ctx")]
    return np.ascontiguousarray(np.concatenate(parts, axis=1))


def kernel(**inputs):
    import concourse.bacc as bacc
    from concourse.bass_utils import run_bass_kernel_spmd

    nc = bacc.Bacc("TRN2", target_bir_lowering=False, num_devices=1)
    one = {name: np.asarray(v) if name == "c_ctx" else np.asarray(v)[0] for name, v in inputs.items()}
    arrays = {"in_" + name: np.ascontiguousarray(one[name]) for name in NAMES}
    arrays["in_vectors"] = vector_columns(one)
    pairs = [one[n].reshape(NP, 2, NS, GC).transpose(1, 2, 0, 3).reshape(P, NP, GC) for n in ("b_re", "b_im")]
    arrays["in_b"] = np.ascontiguousarray(np.stack(pairs, axis=1))
    pairs = [one[n].reshape(NP, 2, GC, NS).transpose(1, 3, 0, 2).reshape(P, NP, GC)
             for n in ("c_re_f", "c_im_f", "c_re_b", "c_im_b")]
    arrays["in_c_states"] = np.ascontiguousarray(np.stack(pairs, axis=1).reshape(P, 2, 2, NP, GC))
    arrays["in_rope"] = rope_tables()
    a = {name[3:]: nc.dram_tensor(name, v.shape, F32, kind="ExternalInput").ap() for name, v in arrays.items()}
    out = nc.dram_tensor("out_x", (T, D), F32, kind="ExternalOutput").ap()
    build(nc, a, out)
    result = run_bass_kernel_spmd(nc, [arrays], core_ids=[0])
    return result.results[0]["out_x"].reshape(1, T, D)
```

```python
from contextlib import ExitStack

import numpy as np

import concourse.bass as bass
from concourse import mybir
from concourse.alu_op_type import AluOpType as ALU

F32 = mybir.dt.float32
F32R = mybir.dt.float32r
I32 = mybir.dt.int32
ACT = mybir.ActivationFunctionType
AX = mybir.AxisListType

P = 128
D = 1024
KD = D // P
T = 512
C = 256
TT_N, CT_N = T // P, C // P
H, NOPE, ROPE, VD = 8, 64, 32, 64
QK = NOPE + ROPE
QL, KVL = 384, 256
SSM = 512
G, GC, NS = 32, 16, 64
NP = G // 2
L = 8
CK, CC = T // L, C // L
NK = CC + CK
NB, GB, PB = 4, 8, 4
FF = 2816
KF = FF // P
IN_W = QL + KVL + ROPE + SSM + 2 * D
U0 = QL + KVL + ROPE
GATE0 = U0 + SSM
PW = 2048
EPS = 1e-6
SCALE = QK ** -0.5

V_BMOD, V_N1, V_N2, V_DSKIP, V_QAG, V_KVAG = 0, 48, 56, 64, 68, 71
V_W0, V_W1, V_W2, V_CB = 73, 117, 161, 205
V_LAM, V_LDT, V_C, V_END = 249, 313, 345, 361

GATE_ORDER = ("gate", "mod2", "gate") * 4
EARLY_MOD2 = 8
STREAM = ["mod1"] * 2 + ["lat", "mod2", "lat", "mod2", "u"] + ["mod2"] * 3 + ["u"] + ["mod2"] * 2 + ["lat", "mod2"] \
    + list(GATE_ORDER) + ["uq"] * 2 + ["ukv"] + ["glu"] * 4 + ["wo"] * 2 + ["mod2"] * 4 + ["wout"] * 4 + ["up"] * 22 + ["down"] * 12


def positions():
    n_of, s_of, s_at, is_split = {}, {}, [], []
    s = 0
    for n, stage in enumerate(STREAM):
        n_of.setdefault(stage, []).append(n)
        split = not stage.startswith("mod")
        is_split.append(split)
        s_at.append(s)
        if split:
            s_of.setdefault(stage, []).append(s)
            s += 1
    return n_of, s_of, s_at, is_split


N_OF, S_OF, S_AT, IS_SPLIT = positions()
N_OF_SPLIT = [n for n in range(len(STREAM)) if IS_SPLIT[n]]

TILES = {"lat": 5, "u": 12, "lat2": 4, "gate": 16, "uq": 8, "ukv": 12, "glu": 16, "wo": 8, "wout": 8,
         "up": 44, "down": 8}
TILE0 = {}
_t = 0
for _name, _n in TILES.items():
    TILE0[_name] = _t
    _t += _n


class Chain:

    def __init__(self, eng, sem):
        self.eng, self.sem, self.base, self.local = eng, sem, 0, 0

    def __call__(self, ins):
        ins.then_inc(self.sem, 1)
        self.local += 1

    def wait(self):
        self.eng.wait_ge(self.sem, self.base + self.local)

    def step(self, ins):
        self(ins)
        self.wait()

    def enter(self, i, per_round):
        self.outer = self.base + self.local
        self.per_round = per_round
        self.base, self.local = self.outer + i * per_round, 0

    def leave(self, rounds):
        assert self.local == self.per_round, (self.local, self.per_round)
        self.base, self.local = self.outer + rounds * self.per_round, 0


def rope_tables():
    pos = np.arange(T)
    freqs = (10000.0 ** (-np.arange(ROPE // 4, dtype=np.float32) / (ROPE // 4))).astype(np.float32)
    row = (pos // 64).astype(np.float32)[:, None] * freqs
    col = (pos % 64).astype(np.float32)[:, None] * freqs
    ang = np.concatenate([row, col], axis=-1).astype(np.float64)
    return np.concatenate([np.cos(ang), np.sin(ang)], axis=-1).astype(np.float32)


def build(nc, a, out):
    ctx = ExitStack()
    with ctx:
        def sem(name):
            return ctx.enter_context(nc.semaphore(name))

        ORIGIN = 16512

        def at(name, kb, shape, dt=F32):
            return nc.alloc_sbuf_tensor_at(name, shape, dt, offset=ORIGIN + int(kb * 1024))

        raw = [at(f"raw{i}", 8 * i, [P, PW]) for i in range(2)]
        whi = [at(f"w_hi{i}", 16 + 8 * i, [P, PW], F32R) for i in range(2)]
        wlo = [at(f"w_lo{i}", 32 + 8 * i, [P, PW], F32R) for i in range(2)]
        early = [at(f"early{i}", kb, [P, PW]) for i, kb in enumerate((16, 24, 32, 40, 130, 114))]
        xT = at("xT", 48, [P, KD, T])
        o = [64.0]

        def small(name, shape, dt=F32):
            t = at(name, o[0], shape, dt)
            n = 1
            for d in shape[1:]:
                n *= d
            o[0] += ((n * 4 + 31) // 32 * 32) / 1024
            assert o[0] <= 70.01, (name, o[0])
            return t

        ident = small("ident", [P, P])
        ones = small("ones", [P, P])
        VEC = small("VEC", [P, V_END])
        modb = small("modb", [P, 48, 2])
        gain1 = small("gain1", [P, 2, KD])
        gain2 = small("gain2", [P, KD])
        LP = small("LP", [P, 2, 9, 32])
        r8 = small("r8", [P, 32])
        cs = small("cs", [P, KD, 2])
        dmask = small("dmask", [P, GC])
        rl = small("rl", [P, 10])
        stv = small("stv", [P, 10])
        sty = small("sty", [P, 10])
        stt = small("stt", [P, 10])
        smx = small("smx", [P, 4, 4])

        h_hi = at("h_hi", 70, [P, KD, T], F32R)
        h_lo = at("h_lo", 86, [P, KD, T], F32R)
        cq = at("cq", 102, [P, 3, T])
        ckv = at("ckv", 108, [P, 2, C + T])
        hc_hi = at("hc_hi", 114, [P, KD, C], F32R)
        hc_lo = at("hc_lo", 122, [P, KD, C], F32R)
        utok = at("utok", 130, [P, NB, GB * L * GC])
        ustage = at("ustage", 179, [P, L, SSM])
        macc = at("macc", 48, [P, EARLY_MOD2, 256])
        CP_ = [at("CP0", 146, [P, 2, 2, PB, 9 * GC]), at("CP1", 54, [P, 2, 2, PB, 9 * GC])]
        BP = at("BP", 155, [P, 2, 2, PB, P])
        bbd = at("bbd", 163, [P, 2, 2, PB, 32])
        E_ = [at("E0", 165, [P, 2, 8, NK]), at("E1", 48, [P, 2, 8, NK])]
        CT = at("CT", 171, [P, 2, 2, NP, GC])
        BB = at("BB", 175, [P, 2, 2, NP, GC])
        xtok = at("xtok", 70, [P, TT_N, D])
        ctok = at("ctok", 86, [P, CT_N, D])
        junk = at("junk", 122, [P, D])
        diag = at("diag", 126, [P, 6, P])
        Bld = at("Bld", 152, [P, 2, NP, GC])
        TMP = at("TMP", 146, [P, 44, 32])
        bbt = at("bbt", 154, [P, 2, NP, GC])
        mrow = at("mrow", 102, [2, 2 * D])
        xn = at("xn", 179, [P, KD, T])
        cn = at("cn", 94, [P, KD, C])
        rstdb = at("rstdb", 203, [P, C + T])
        hf = [at(f"hf{i}", 130 + 3 * i, [P, C + T]) for i in range(2)]
        krT = at("krT", 197, [ROPE, C + T])
        ust = [at(f"ust{i}", 191 + i, [P, 256]) for i in range(4)]
        WinT = at("WinT", 114, [P, 2, 2, PB, P])
        TTm = at("TTm", 122, [P, GB, P])
        SBD = [at("SBD0", 126, [P, 2, PB, 2, CK]), at("SBD1", 191, [P, 2, PB, 2, CK])]
        U = at("U", 179, [P, GB, NK])
        Ub = at("Ub", 182, [P, GB, NK])
        W = at("W", 185, [P, 2, 2, PB, NK])
        Ysb = at("Ysb", 185, [P, GB, CK])
        zp = at("zp", 200, [P, 7, 2, 32])
        pt1 = at("pt1", 195, [P, 512])
        ytok = at("ytok", 187, [64, L, P])
        tmpC = at("tmpC", 197, [P, PB * 9 * GC])
        tmpA = at("tmpA", 197, [P, PB, NK])
        tmpB = at("tmpB", 198.5, [P, PB, NK])
        Kf = at("Kf", 190, [P, 15 * GC])
        gst = [at(f"gst{i}", 202 + 2 * i, [P, T]) for i in range(2)]
        kr = at("kr", 206, [P, 6, ROPE])
        y_hi = at("y_hi", 70, [P, 4, T], F32R)
        y_lo = at("y_lo", 78, [P, 4, T], F32R)
        sT = at("sT", 86, [P, KD, T])
        q_hi = at("q_hi", 102, [QK, H, T], F32R)
        q_lo = at("q_lo", 48, [QK, H, T], F32R)
        V = at("V", 118, [P, 6, H * VD])
        k_hi = at("k_hi", 130, [QK, H, C + T], F32R)
        k_lo = [at(f"k_lo{h}", kb, [QK, C + T], F32R) for h, kb in enumerate((74, 77, 80, 83, 200, 203, 162, 165))]
        cq_hi = at("cq_hi", 86, [P, 3, T], F32R)
        cq_lo = at("cq_lo", 92, [P, 3, T], F32R)
        ckv_hi = at("ckv_hi", 158, [P, 2, C + T], F32R)
        ckv_lo = at("ckv_lo", 164, [P, 2, C + T], F32R)
        gload = [at(f"gload{i}", 154 + 2 * i, [P, T]) for i in range(4)]
        sg = [at(f"sg{i}", 162 + 2 * i, [P, T]) for i in range(2)]
        qsb = at("qsb", 170, [P, TT_N, H, QK])
        ksb = at("ksb", 182, [P, 6, H, QK])
        sqt = [at(f"sqt{i}", 200 + 2 * i, [P, T]) for i in range(2)]
        tq = at("tq", 130, [P, 4, 512])
        qkg = at("qkg", 204, [P, 2, QK])
        rope = at("rope", 204.75, [P, TT_N, 32])
        stq = at("stq", 205.25, [P, 2, 80])
        stq3 = at("stq3", 206.75, [P, 6])
        Pm = [at(f"Pm{i}", 170 + 3 * i, [P, C + T]) for i in range(2)]
        PT = [at(f"PT{i}", 176 + 3 * i, [P, 6, P]) for i in range(2)]
        otok = at("otok", 182, [P, TT_N, H * VD])
        oT_hi = at("oT_hi", 190, [P, 4, T], F32R)
        oT_lo = at("oT_lo", 198, [P, 4, T], F32R)
        mg_hi = at("mg_hi", 102, [P, KD, T], F32R)
        mg_lo = at("mg_lo", 118, [P, KD, T], F32R)
        mgf = [at(f"mgf{i}", 162 + 2 * i, [P, T]) for i in range(2)]
        macc_late = at("macc_late", 70, [P, 4, 256])
        sqx = at("sqx", 134, [P, KD, T])
        h2_hi = at("h2_hi", 70, [P, KD, T], F32R)
        h2_lo = at("h2_lo", 86, [P, KD, T], F32R)
        nx = [at(f"nx{i}", 190 + 2 * i, [P, T]) for i in range(2)]
        nh = [at(f"nh{i}", 194 + 2 * i, [P, T]) for i in range(2)]
        diag3 = at("diag3", 198, [P, TT_N, P])
        act_hi = at("act_hi", 102, [P, KF, T], F32R)
        act_lo = at("act_lo", 146, [P, KF, T], F32R)
        cv = [[at(f"cv{v}{i}", 190 + 4 * v + 2 * i, [P, T]) for i in range(2)] for v in range(2)]
        sl = [at(f"sl{i}", 198 + 2 * i, [P, T]) for i in range(2)]
        xo = [at(f"xo{i}", 70 + 4 * i, [P, 2, T]) for i in range(2)]
        ost = [at(f"ost{i}", 78 + 4 * i, [P, TT_N, 256]) for i in range(2)]

        ps = ctx.enter_context(nc.psum_tensor("ps", [P, 8, 512], F32))
        bank = [ps[:, i, :] for i in range(8)]

        u_dram = nc.dram_tensor("u_scratch", (C + T, SSM), F32, kind="Internal").ap()
        kf_dram = nc.dram_tensor("kf_scratch", (NB, P, 15 * GC), F32, kind="Internal").ap()
        xT_dram = nc.dram_tensor("xT_scratch", (P, KD, T), F32, kind="Internal").ap()
        gate_dram = nc.dram_tensor("gate_scratch", (16, P, T), F32, kind="Internal").ap()

        def rows(w):
            return w.rearrange("(k p) n -> p k n", p=P)

        w_mod_v = a["w_mod"].rearrange("(p k) n -> p k n", k=KD)
        w_in_v, w_uq_v, w_ukv_v, w_o_v, w_glu_v = (rows(a[n]) for n in ("w_in", "w_uq", "w_ukv", "w_o_attn", "w_glu"))
        w_out_v, w_up_v, w_down_v = (rows(a[n]) for n in ("w_out", "w_up", "w_down"))

        def width(stage, p):
            return {"lat": (2048, 2048, 1280)[p] if stage == "lat" else 0, "uq": 1152,
                    "down": (2048, 2048, 1536)[p % 3]}.get(stage, 2048)

        def parts(stage, p, buf):
            if stage in ("mod1", "mod2"):
                c0 = p * 256 + (2048 if stage == "mod2" else 0)
                return [(buf[:, :].rearrange("p (k n) -> p k n", k=8), w_mod_v[:, :, bass.ds(c0, 256)])]
            if stage == "lat":
                w = width(stage, p) // 8
                return [(buf[:, 0:8 * w].rearrange("p (k n) -> p k n", k=8), w_in_v[:, :, 256 * p:256 * p + w])]
            if stage in ("u", "gate"):
                c0 = (U0 if stage == "u" else GATE0) + p * 256
                return [(buf[:, :].rearrange("p (k n) -> p k n", k=8), w_in_v[:, :, bass.ds(c0, 256)])]
            if stage == "uq":
                return [(buf[:, 0:1152].rearrange("p (k n) -> p k n", k=3), w_uq_v[:, :, 384 * p:384 * p + 384])]
            if stage == "ukv":
                return [(buf[:, :].rearrange("p (k n) -> p k n", k=2), w_ukv_v[:, :, :])]
            if stage == "glu":
                b = buf[:, :].rearrange("p (k v n) -> p k v n", k=4, v=2)
                return [(b[:, :, v, :], w_glu_v[:, :, bass.ds(p * 256 + v * D, 256)]) for v in range(2)]
            if stage == "wo":
                return [(buf[:, :].rearrange("p (k n) -> p k n", k=4), w_o_v[:, :, 512 * p:512 * p + 512])]
            if stage == "wout":
                return [(buf[:, :].rearrange("p (k n) -> p k n", k=8), w_out_v[:, :, bass.ds(p * 256, 256)])]
            if stage == "up":
                b = buf[:, :].rearrange("p (k v n) -> p k v n", k=8, v=2)
                return [(b[:, :, v, :], w_up_v[:, :, bass.ds(p * 128 + v * FF, 128)]) for v in range(2)]
            raise ValueError(stage)

        def down_part(pair, kk, buf):
            n = (8, 8, 6)[kk]
            return buf[:, 0:n * 256].rearrange("p (k n) -> p k n", k=n), w_down_v[:, 8 * kk:8 * kk + n, bass.ds(pair * 256, 256)]

        def sems(names):
            return [sem(n) for n in names.split()]

        raw_in = sems("raw_in0 raw_in1")
        hi_ready, lo_ready, tile_done, tile_free, down_used = sems("hi_ready lo_ready tile_done tile_free down_used")
        vec_ready, c_in, b_in, x_in, ctx_in, attn_consts_in = sems("vec_ready c_in b_in x_in ctx_in attn_consts_in")
        pool_chain, dve_chain, act_chain = sems("pool_chain dve_chain act_chain")
        consts_ready, cs_ready, sumsq1, diag1_ready, rstd1_mm, rstd1_ready = sems("consts_ready cs_ready sumsq1 diag1_ready rstd1_mm rstd1_ready")
        xT_mm, xT_ready, xn_ready, cn_ready, xT_out, xT_back = sems("xT_mm xT_ready xn_ready cn_ready xT_out xT_back")
        early_in = sems("early_in0 early_in1 early_in2 early_in3 early_in4 early_in5")
        mod1_pe, mrow_ready, mod1_T, mod2_used, mod2_mm = sems("mod1_pe mrow_ready mod1_T mod2_used mod2_mm")
        gain1_ready, gain2_ready, hf_ready, h_split = sems("gain1_ready gain2_ready hf_ready h_split")
        sq_lat, stat_mm, stat_read, kr_T, kr_ready = sems("sq_lat stat_mm stat_read kr_T kr_ready")
        sin_arg, sin_done, den_ready = sems("sin_arg sin_done den_ready")
        bp_ready, cp_ready, cpD_ready, e_ready, bbd_ready, sbd_zero = sems("bp_ready cp_ready cpD_ready e_ready bbd_ready sbd_zero")
        u_out, utok_in = sems("u_out0 u_out1 u_out2 u_out3"), sem("utok_in")
        ug_A, ug_D, u_T, u_evacA, u_evacD = sems("ug_A ug_D u_T u_evacA u_evacD")
        bp_T, winT_A, winT_D, t_mm, kf_ready, kf_out, tt_in = sems("bp_T winT_A winT_D t_mm kf_ready kf_out tt_in")
        v_mm, v_read, state_ready, y_mm, y_evac = sems("v_mm v_read state_ready y_mm y_evac")
        y_T, ytok_A, ytok_D, y_T2, gelu_done = sems("y_T ytok_A ytok_D y_T2 gelu_done")
        gate_out, gload_in = sems("gate_out0 gate_out1"), sems("gload_in0 gload_in1 gload_in2 gload_in3")
        prep_hi, prep_lo, yprep_hi, yprep_lo = sems("prep_hi prep_lo yprep_hi yprep_lo")
        q_sq, sq_used, v_copy, q_ready, k_ready, qk_T, qk_A, qk_D = sems("q_sq sq_used v_copy q_ready k_ready qk_T qk_A qk_D")
        sg_ready, sgs_ready, s_ready = sems("sg_ready sgs_ready s_ready")
        s_mm, max_ready, exp_ready, p_T, pt_A, pt_D, o_mm, o_evac = sems("s_mm max_ready exp_ready p_T pt_A pt_D o_mm o_evac")
        o_T, oT_hi_r, oT_lo_r, mg_f, mg_h, mg_l = sems("o_T oT_hi_r oT_lo_r mg_f mg_h mg_l")
        x1_ready, sqx_ready, stat2_mm, diag3_ready, rstd3_mm = sems("x1_ready sqx_ready stat2_mm diag3_ready rstd3_mm")
        nx_ready, nh_ready, h2_h, h2_l = sems("nx_ready nh_ready h2_h h2_l")
        cv_a, cv_d, silu_done, act_f, act_h, act_l = sems("cv_a cv_d silu_done act_f act_h act_l")
        xo_ready, xo_T, ost_ready, out_done = sem("xo_ready"), sem("xo_T"), sem("ost_ready"), sems("out_done0 out_done1")

        def transfers(stage):
            return 2 if stage in ("glu", "up") else 1

        def raw_in_count(n):
            return 16 * sum(transfers(STREAM[m]) for m in range(n % 2, n + 1, 2))

        tiles_through = {}
        for p_, e_ in enumerate((2, 5, TILE0["lat2"] + 4 - TILE0["lat"])):
            tiles_through[N_OF["lat"][p_]] = TILE0["lat"] + e_
        for p_ in range(2):
            tiles_through[N_OF["u"][p_]] = TILE0["u"] + 6 * p_ + 6
            tiles_through[N_OF["uq"][p_]] = TILE0["uq"] + 4 * p_ + 4
            tiles_through[N_OF["wo"][p_]] = TILE0["wo"] + 4 * p_ + 4
        for i_ in range(8):
            tiles_through[N_OF["gate"][i_]] = TILE0["gate"] + 2 * i_ + 2
        tiles_through[N_OF["ukv"][0]] = TILE0["ukv"] + 12
        for p_ in range(4):
            tiles_through[N_OF["glu"][p_]] = TILE0["glu"] + 4 * p_ + 4
            tiles_through[N_OF["wout"][p_]] = TILE0["wout"] + 2 * p_ + 2
        for p_ in range(22):
            tiles_through[N_OF["up"][p_]] = TILE0["up"] + 2 * p_ + 2

        def wait_used(eng, n):
            if STREAM[n] == "mod1":
                return eng.wait_ge(mod1_pe, n + 1)
            if STREAM[n] == "mod2":
                return eng.wait_ge(mod2_used, N_OF["mod2"].index(n) + 1)
            if STREAM[n] == "down":
                p = n - N_OF["down"][0]
                if p % 3 == 2:
                    eng.wait_ge(tile_done, TILE0["down"] + 2 * (p // 3) + 2)
                else:
                    eng.wait_ge(down_used, 2 * (p // 3) + p % 3 + 1)
            else:
                eng.wait_ge(tile_done, tiles_through[n])

        def split_hi(act, s):
            n = N_OF_SPLIT[s]
            w = width(STREAM[n], N_OF[STREAM[n]].index(n))
            act.wait_ge(raw_in[n % 2], raw_in_count(n))
            if s >= 2:
                wait_used(act, N_OF_SPLIT[s - 2])
            else:
                act.wait_ge(mod1_pe, 3 + s)
            act.activation(whi[s % 2][:, 0:w], raw[n % 2][:, 0:w], ACT.Copy).then_inc(hi_ready, 1)

        def split_lo(dve, s):
            n = N_OF_SPLIT[s]
            w = width(STREAM[n], N_OF[STREAM[n]].index(n))
            dve.wait_ge(hi_ready, s + 1)
            if s < 2:
                dve.wait_ge(mod1_pe, 5 + s)
            dve.tensor_tensor(wlo[s % 2][:, 0:w], raw[n % 2][:, 0:w], whi[s % 2][:, 0:w].bitcast(F32),
                              ALU.subtract).then_inc(lo_ready, 1)

        LATE_QK = 3 * H - 4

        def qk_tile(i):
            if i < H:
                return q_hi[:, i, :], q_lo[:, i, :], T
            h, part = (i - H) // 2, (i - H) % 2
            keys = slice(T, C + T) if part else slice(0, T)
            return k_hi[:, h, keys], k_lo[h][:, keys], C if part else T

        def qk_bank(i):
            return bank[i % 4] if i < LATE_QK else bank[4 + i % 4]

        block = ctx.enter_context(nc.Block())

        @block.sync
        def _(sp):
            def load(n, p=None):
                stage = STREAM[n]
                p = N_OF[stage].index(n) if p is None else p
                if n >= 2:
                    if IS_SPLIT[n - 2]:
                        sp.wait_ge(lo_ready, S_AT[n - 2] + 1)
                    else:
                        wait_used(sp, n - 2)
                for dst, src in parts(stage, p, raw[n % 2]):
                    sp.dma_start(dst, src).then_inc(raw_in[n % 2], 16)

            def load_down(n, pair, kk):
                sp.wait_ge(lo_ready, S_AT[n - 2] + 1)
                dst, src = down_part(pair, kk, raw[n % 2])
                sp.dma_start(dst, src).then_inc(raw_in[n % 2], 16)

            def load_mod1(p, buf, signal):
                for dst, src in parts("mod1", p, buf):
                    sp.dma_start(dst, src).then_inc(signal, 16)

            sp.dma_start(VEC[:, :], a["vectors"]).then_inc(vec_ready, 16)
            load_mod1(0, raw[0], raw_in[0])
            load_mod1(1, raw[1], raw_in[1])
            sp.dma_start(xtok[:, :, :], a["x"].rearrange("(t p) n -> p t n", p=P)).then_inc(x_in, 16)
            sp.dma_start(ctok[:, :, :], a["ctx"].rearrange("(t p) n -> p t n", p=P)).then_inc(ctx_in, 16)
            for p in range(2, 8):
                load_mod1(p, early[p - 2], early_in[p - 2])
            for n in range(N_OF["lat"][0], N_OF["uq"][0]):
                if n == N_OF["gate"][0]:
                    for i in range(4):
                        sp.wait_ge(u_out[i], 16 * 3)
                    for j in range(L):
                        sp.dma_start(ustage[0:NK, L - 1 - j, :],
                                     u_dram.rearrange("(k j) c -> j k c", j=L)[j]).then_inc(utok_in, 16)
                load(n)
                if n == N_OF["lat"][0]:
                    sp.dma_start(Bld[:, :, :, :], a["b"]).then_inc(b_in, 16)
                    sp.dma_start(CT[:, :, :, :, :], a["c_states"]).then_inc(c_in, 16)
                    sp.wait_ge(xT_ready, KD)
                    sp.dma_start(xT_dram, xT[:, :, :]).then_inc(xT_out, 16)
            for n in N_OF["uq"] + N_OF["ukv"]:
                load(n)
            for n in range(N_OF["glu"][0], N_OF["wout"][0]):
                load(n)
            sp.wait_ge(s_mm, 4 * H)
            sp.wait_ge(xT_out, 16)
            sp.dma_start(xT[:, :, :], xT_dram).then_inc(xT_back, 16)
            for n in range(N_OF["wout"][0], N_OF["up"][2]):
                load(n)
            n0 = N_OF["up"][0]
            with sp.Fori(1, 11) as i:
                for j in range(2):
                    sp.wait_ge(lo_ready, S_AT[n0] + 2 * i + j - 1)
                    for dst, src in parts("up", 2 * i + j, raw[(n0 + j) % 2]):
                        sp.dma_start(dst, src).then_inc(raw_in[(n0 + j) % 2], 16)
            n0 = N_OF["down"][0]
            for j in range(2):
                load_down(n0 + j, 0, j)
            sp.wait_ge(lo_ready, S_AT[n0] + 1)
            dst, src = down_part(0, 2, raw[(n0 + 2) % 2])
            sp.dma_start(dst, src).then_inc(raw_in[(n0 + 2) % 2], 16)
            for j in range(3):
                load_down(n0 + 3 + j, 1, j)
            with sp.Fori(1, 2) as i:
                for j in range(6):
                    sp.wait_ge(lo_ready, S_AT[n0] + 6 * i + j - 1)
                    dst, src = down_part(2 * i + j // 3, j % 3, raw[(n0 + j) % 2])
                    sp.dma_start(dst, src).then_inc(raw_in[(n0 + j) % 2], 16)
            for pair in range(4):
                sp.wait_ge(ost_ready, 2 * pair + 2)
                sp.dma_start(out[:, pair * 256:(pair + 1) * 256].rearrange("(t p) n -> p t n", p=P),
                             ost[pair % 2][:, :, :]).then_inc(out_done[pair % 2], 16)
            for i in range(2):
                sp.wait_ge(out_done[i], 32)

        @block.gpsimd
        def _(pool):
            ch = Chain(pool, pool_chain)
            ch(pool.memset(ident[:, :], 0.0))
            ch(pool.memset(bbd[:, :, :, :, :], 0.0))
            ch.wait()
            ch.step(pool.affine_select(out=ident[:, :], in_=ident[:, :], compare_op=ALU.not_equal, fill=1.0, base=0,
                                       pattern=[[-1, P]], channel_multiplier=1))
            pool.memset(ones[:, :], 1.0).then_inc(consts_ready, 1)

            def tt(o_, x_, y_, op):
                return pool.tensor_tensor(o_, x_, y_, op)

            def ts(o_, x_, s1, s2=None, op0=ALU.mult, op1=ALU.add):
                if s2 is None:
                    return pool.tensor_scalar(o_, x_, s1, None, op0)
                return pool.tensor_scalar(o_, x_, s1, s2, op0, op1)

            def stt_(o_, x_, s, y_, op0, op1):
                ch.step(ts(TMP[:, 43, :], x_, s, None, op0))
                return tt(o_, TMP[:, 43, :], y_, op1)

            pool.wait_ge(vec_ready, 16)
            tmp = [TMP[:, k, :] for k in range(44)]

            def dm(v):
                return v.rearrange("p (d m) -> p d m", d=2)

            def exp(y, x, s):
                xc, n, f, q = s
                ch.step(ts(xc, x, -87.0, 88.0, ALU.max, ALU.min))
                ch.step(ts(n, xc, 1.4426950408889634, 12582912.0, ALU.mult, ALU.add))
                ch.step(ts(n, n, -12582912.0, None, ALU.add))
                ch.step(stt_(f, n, -0.693359375, xc, ALU.mult, ALU.add))
                ch.step(stt_(f, n, 2.12194440e-4, f, ALU.mult, ALU.add))
                ch.step(ts(q, f, 1.0 / 5040))
                for c_ in (1.0 / 720, 1.0 / 120, 1.0 / 24, 1.0 / 6, 0.5, 1.0):
                    ch.step(stt_(q, q, c_, f, ALU.add, ALU.mult))
                ch.step(ts(n.bitcast(I32), n, 8388608.0, 127.0 * 8388608.0))
                ch.step(stt_(y, q, 1.0, n, ALU.add, ALU.mult))
                ch.step(stt_(y, x, -87.0, y, ALU.is_ge, ALU.mult))

            lam = VEC[:, V_LAM:V_LAM + 64].rearrange("p (d r m) -> p r d m", d=2, r=2)
            lre, lim = lam[:, 0], lam[:, 1]
            dt, mag, th, n_ = tmp[0], tmp[1], tmp[2], tmp[3]
            exp(dt, VEC[:, V_LDT:V_LDT + 32], tmp[4:8])
            ch.step(tt(dm(th), lim, dm(dt), ALU.mult))
            ch.step(ts(n_, th, 0.15915494309189535, 12582912.0, ALU.mult, ALU.add))
            ch.step(ts(n_, n_, -12582912.0, None, ALU.add))
            ch.step(stt_(th, n_, -6.28125, th, ALU.mult, ALU.add))
            ch.step(stt_(th, n_, -0.0019350051879882812, th, ALU.mult, ALU.add))
            ch.step(stt_(th, n_, -3.0199159819567e-07, th, ALU.mult, ALU.add))
            ch.step(ts(tmp[8], th, 3.1415925, -3.1415925, ALU.min, ALU.max))
            ts(tmp[9], tmp[8], 0.5).then_inc(sin_arg, 1)
            pool.wait_ge(rstd1_ready, 2)
            for k in range(KD):
                tt(xn[:, k, :], xT[:, k, :], rstdb[:, C:], ALU.mult).then_inc(xn_ready, 1)

            ch.step(tt(dm(tmp[12]), lre, dm(dt), ALU.mult))
            exp(mag, tmp[12], tmp[4:8])
            pool.wait_ge(sin_done, 1)
            c1, s1 = tmp[13], tmp[14]
            ch.step(tt(c1, tmp[11], tmp[11], ALU.mult))
            ch.step(ts(c1, c1, -2.0, 1.0))
            ch.step(pool.tensor_copy(s1, tmp[10]))

            def cmul(o_, x_, y_, t, shape=None):
                b_ = (lambda v: v.to_broadcast(shape)) if shape else (lambda v: v)
                ch(tt(o_[0], x_[0], b_(y_[0]), ALU.mult))
                ch(tt(t[0], x_[1], b_(y_[1]), ALU.mult))
                ch(tt(o_[1], x_[1], b_(y_[0]), ALU.mult))
                ch(tt(t[1], x_[0], b_(y_[1]), ALU.mult))
                ch.wait()
                ch(tt(o_[0], o_[0], t[0], ALU.subtract))
                ch(tt(o_[1], o_[1], t[1], ALU.add))
                ch.wait()

            lp = lambda q: (LP[:, 0, q, :], LP[:, 1, q, :])
            ch(pool.memset(LP[:, 0, 0, :], 1.0))
            ch(pool.memset(LP[:, 1, 0, :], 0.0))
            ch(tt(LP[:, 0, 1, :], mag, c1, ALU.mult))
            ch(tt(LP[:, 1, 1, :], mag, s1, ALU.mult))
            ch.wait()
            tm = (tmp[15], tmp[16])
            cmul(lp(2), lp(1), lp(1), tm)
            cmul(lp(3), lp(2), lp(1), tm)
            cmul(lp(4), lp(2), lp(2), tm)
            for q in range(1, 5):
                cmul(lp(4 + q), lp(4), lp(q), tm)
            ch.step(tt(tmp[17], mag, mag, ALU.mult))
            ch.step(tt(tmp[17], tmp[17], tmp[17], ALU.mult))
            ch.step(tt(r8[:, :], tmp[17], tmp[17], ALU.mult))
            cmul((tmp[18], tmp[19]), (c1, s1), (c1, s1), tm)
            cmul((tmp[20], tmp[21]), (tmp[18], tmp[19]), (tmp[18], tmp[19]), tm)
            z = lambda i: (zp[:, i, 0, :], zp[:, i, 1, :])
            cmul(z(0), (tmp[20], tmp[21]), (tmp[20], tmp[21]), tm)
            for i in range(6):
                cmul(z(i + 1), z(i), z(i), tm)
            nr, _, den, qr, qi = tmp[22:27]
            ch(ts(nr, LP[:, 0, 1, :], -1.0, None, ALU.add))
            ch.wait()
            pool.wait_ge(den_ready, 1)
            ch(tt(dm(qr), dm(nr), lre, ALU.mult))
            ch(tt(dm(tmp[28]), dm(LP[:, 1, 1, :]), lim, ALU.mult))
            ch(tt(dm(qi), dm(LP[:, 1, 1, :]), lre, ALU.mult))
            ch(tt(dm(tmp[29]), dm(nr), lim, ALU.mult))
            ch.wait()
            ch(tt(qr, qr, tmp[28], ALU.add))
            ch(tt(qi, qi, tmp[29], ALU.subtract))
            ch.wait()
            ch(tt(qr, qr, den, ALU.mult))
            ch(tt(qi, qi, den, ALU.mult))
            pool.wait_ge(b_in, 16)
            ch.wait()
            sh = [P, NP, GC]
            for d in range(2):
                re_, im_ = BB[:, 0, d], BB[:, 1, d]
                q0, q1 = dm(qr)[:, d, :, None].to_broadcast(sh), dm(qi)[:, d, :, None].to_broadcast(sh)
                ch(tt(re_, Bld[:, 0], q0, ALU.mult))
                ch(tt(bbt[:, 0], Bld[:, 1], q1, ALU.mult))
                ch(tt(im_, Bld[:, 1], q0, ALU.mult))
                ch(tt(bbt[:, 1], Bld[:, 0], q1, ALU.mult))
                ch.wait()
                ch(tt(re_, re_, bbt[:, 0], ALU.subtract))
                ch.step(tt(im_, im_, bbt[:, 1], ALU.add))
                ins = ts(im_, im_, -1.0)
                ch.step(ins)

            pool.wait_ge(c_in, 16)

            def mul(o_, x_, y_, shape):
                ch(pool.tensor_tensor(o_, x_.to_broadcast(shape), y_.to_broadcast(shape), ALU.mult))

            def turn(d, part, pairs, forward):
                v = LP[:, part, 0:9, :].rearrange("p q (d m) -> p d m q", d=2)[:, d, pairs, :]
                return (v if forward else v[:, :, ::-1])

            for b in range(NB):
                pairs = slice(PB * b, PB * b + PB)
                if b >= 1:
                    pool.wait_ge(bp_T, b)
                for d in range(2):
                    sh = [P, PB, 8, GC]
                    br, bi = BB[:, 0, d, pairs, :][:, :, None, :], BB[:, 1, d, pairs, :][:, :, None, :]
                    if d == 0:
                        lr, li = turn(0, 0, pairs, True)[:, :, 0:8], turn(0, 1, pairs, True)[:, :, 0:8]
                    else:
                        lr, li = turn(1, 0, pairs, False)[:, :, 1:9], turn(1, 1, pairs, False)[:, :, 1:9]
                    lr, li = lr[:, :, :, None], li[:, :, :, None]
                    re = BP[:, 0, d].rearrange("p m (q c) -> p m q c", c=GC)
                    im = BP[:, 1, d].rearrange("p m (q c) -> p m q c", c=GC)
                    t1 = pt1[:, :].rearrange("p (m q c) -> p m q c", m=PB, c=GC)
                    mul(re, br, lr, sh)
                    mul(t1, bi, li, sh)
                    ch.wait()
                    ch(pool.tensor_tensor(re, re, t1, ALU.add))
                    ch.wait()
                    mul(im, bi, lr, sh)
                    mul(t1, br, li, sh)
                    ch.wait()
                    pool.tensor_tensor(im, im, t1, ALU.subtract).then_inc(bp_ready, 1)
                    pool.wait_ge(bp_ready, 2 * b + d + 1)
                CP, E = CP_[b % 2], E_[b % 2]
                if b == 1:
                    pool.wait_ge(xT_out, 16)
                    pool.wait_ge(t_mm, 1)
                if b >= 2:
                    pool.wait_ge(y_mm, b - 1)
                for d in range(2 if b == 0 else 1):
                    for hp in range(2):
                        sh = [P, 2, 9, GC]
                        two = slice(PB * b + 2 * hp, PB * b + 2 * hp + 2)
                        cr, ci = CT[:, d, 0, two, :][:, :, None, :], CT[:, d, 1, two, :][:, :, None, :]
                        lr, li = turn(d, 0, two, d == 0)[:, :, :, None], turn(d, 1, two, d == 0)[:, :, :, None]
                        re = CP[:, 0, d, 2 * hp:2 * hp + 2].rearrange("p m (q c) -> p m q c", c=GC)
                        im = CP[:, 1, d, 2 * hp:2 * hp + 2].rearrange("p m (q c) -> p m q c", c=GC)
                        t1 = pt1[:, 0:288].rearrange("p (m q c) -> p m q c", m=2, c=GC)
                        mul(re, cr, lr, sh)
                        mul(t1, ci, li, sh)
                        ch.wait()
                        ch(pool.tensor_tensor(re, re, t1, ALU.subtract))
                        ch.wait()
                        mul(im, cr, li, sh)
                        mul(t1, ci, lr, sh)
                        ch.wait()
                        last = pool.tensor_tensor(im, im, t1, ALU.add)
                        if hp == 0:
                            ch.step(last)
                        else:
                            last.then_inc(cp_ready, 1)
                    pool.wait_ge(cp_ready, b + 1 + (d if b == 0 else 1))
                if b >= 2:
                    pool.wait_ge(state_ready, 2 * b - 2)
                ch(pool.memset(E[:, 0, :, 0:1], 1.0))
                ch(pool.memset(E[:, 1, :, 0:1], 0.0))
                ch.wait()
                at_, i = 1, 0
                while at_ < NK:
                    n = min(at_, NK - at_)
                    z = [zp[:, i, r, :].rearrange("p (d m) -> p d m", d=2)[:, :, pairs] for r in range(2)]
                    sh = [P, 2, PB, n]
                    e = [E[:, r, :, :].rearrange("p (d m) k -> p d m k", d=2) for r in range(2)]
                    t1 = pt1[:, 0:8 * n].rearrange("p (d m k) -> p d m k", d=2, m=PB)
                    new = slice(at_, at_ + n)
                    mul(e[0][:, :, :, new], e[0][:, :, :, 0:n], z[0][:, :, :, None], sh)
                    mul(t1, e[1][:, :, :, 0:n], z[1][:, :, :, None], sh)
                    ch.wait()
                    ch(pool.tensor_tensor(e[0][:, :, :, new], e[0][:, :, :, new], t1, ALU.subtract))
                    ch.wait()
                    mul(e[1][:, :, :, new], e[1][:, :, :, 0:n], z[0][:, :, :, None], sh)
                    mul(t1, e[0][:, :, :, 0:n], z[1][:, :, :, None], sh)
                    ch.wait()
                    last = pool.tensor_tensor(e[1][:, :, :, new], e[1][:, :, :, new], t1, ALU.add)
                    at_ += n
                    i += 1
                    if at_ < NK:
                        ch(last)
                        ch.wait()
                    else:
                        last.then_inc(e_ready, 1)
                        pool.wait_ge(e_ready, b + 1)
            pool.wait_ge(tile_done, TILE0["uq"])
            for b in range(NB):
                pool.wait_ge(gelu_done, b + 1)
                y_b, parts_ = utok[:, b, 0:L * CK].rearrange("p (j k) -> p j k", j=L), [
                    v[:, b, :].rearrange("p (k j) -> p j k", j=L) for v in (y_hi, y_lo)]
                pool.tensor_copy(parts_[0], y_b).then_inc(yprep_hi, 1)
                pool.wait_ge(yprep_hi, b + 1)
                pool.tensor_tensor(parts_[1], y_b, parts_[0].bitcast(F32), ALU.subtract).then_inc(yprep_lo, 1)
            pool.wait_ge(tile_done, TILE0["ukv"] + 12)
            def load_gate(t):
                pool.dma_start(gload[t % 4][:, :], gate_dram[8 + t if t < 8 else t - 8]).then_inc(gload_in[t % 4], 16)

            for i in range(2):
                pool.wait_ge(gate_out[i], 16 * 8)
            for t in range(4):
                load_gate(t)
            for m in range(8):
                pool.wait_ge(sg_ready, m + 1)
                pool.wait_ge(gload_in[m % 4], 16 * (m // 4 + 1))
                pool.tensor_tensor(sg[m % 2][:, :], sg[m % 2][:, :], gload[m % 4][:, :], ALU.mult).then_inc(sgs_ready, 1)
                pool.wait_ge(sgs_ready, m + 1)
                load_gate(m + 4)
            for t in range(12, 16):
                pool.wait_ge(mg_f, t - 11)
                load_gate(t)

        @block.scalar
        def _(act):
            ch = Chain(act, act_chain)
            act.wait_ge(vec_ready, 16)
            act.activation(cs[:, :, :].rearrange("p k r -> p r k"), VEC[:, V_C:V_END].rearrange("p (r k) -> p r k", r=2),
                           ACT.Silu).then_inc(cs_ready, 1)
            def sum_squares(t, src):
                return act.activation(junk[:, :], src, ACT.Square, accum_out=stv[:, t:t + 1])

            def mod1_row(p):
                act.wait_ge(mod1_pe, p + 1)
                act.activation(mrow[:, 256 * p:256 * p + 256], bank[6 + p % 2][0:2, 0:256], ACT.Copy).then_inc(mrow_ready, 1)

            mod1_row(0)
            mod1_row(1)
            act.wait_ge(x_in, 16)
            for k in range(KD):
                act.wait_ge(xT_mm, k + 1)
                act.activation(xT[:, k, :], bank[k % 6][:, :], ACT.Copy).then_inc(xT_ready, 1)
                if k % 2:
                    ch.step(sum_squares(k // 2, xtok[:, k // 2, :]))
            mod1_row(2)
            act.wait_ge(ctx_in, 16)
            ch.step(sum_squares(4, ctok[:, 0, :]))
            sum_squares(5, ctok[:, 1, :]).then_inc(sumsq1, 1)
            for p in range(3, 6):
                mod1_row(p)
            act.wait_ge(rstd1_mm, 1)
            act.activation(rstdb[:, C:], bank[1][:, :], ACT.Copy).then_inc(rstd1_ready, 1)
            act.activation(rstdb[:, 0:C], bank[0][:, 0:C], ACT.Copy).then_inc(rstd1_ready, 1)
            mod1_row(6)
            split_hi(act, 0)
            mod1_row(7)
            act.wait_ge(sin_arg, 1)
            act.activation(TMP[:, 10:12, :], TMP[:, 8:10, :], ACT.Sin).then_inc(sin_done, 1)
            act.wait_ge(gain1_ready, 2)
            for k in range(KD):
                act.wait_ge(xn_ready, k + 1)
                if k >= 2:
                    act.wait_ge(h_split, k - 1)
                ch(act.activation(hf[k % 2][:, C:], xn[:, k, :], ACT.Identity, scale=gain1[:, 0, k:k + 1], bias=modb[:, k, 0:1]))
                act.activation(h_hi[:, k, :], xn[:, k, :], ACT.Identity, scale=gain1[:, 0, k:k + 1],
                               bias=modb[:, k, 0:1]).then_inc(hf_ready, 1)
            split_hi(act, 1)

            def lat_tile(t, i, dst, width_, gain):
                act.wait_ge(tile_done, t + 1)
                if i >= 2:
                    act.wait_ge(stat_mm, i - 1)
                src = bank[6 + t % 2][:, 0:width_]
                act.activation(gst[i % 2][:, 0:width_], src, ACT.Square).then_inc(sq_lat, 1)
                act.activation(dst, src, ACT.Identity, scale=VEC[:, gain:gain + 1]).then_inc(tile_free, 1)

            lat_tiles = [(cq[:, 0, :], T, V_QAG), (cq[:, 1, :], T, V_QAG + 1), (cq[:, 2, :], T, V_QAG + 2),
                         (ckv[:, 0, C:], T, V_KVAG), (ckv[:, 0, 0:C], C, V_KVAG),
                         (ckv[:, 1, C:], T, V_KVAG + 1), (ckv[:, 1, 0:C], C, V_KVAG + 1)]
            for t in range(5):
                if t == 4:
                    split_hi(act, 2)
                lat_tile(t, t, *lat_tiles[t])
            t0 = TILE0["u"]
            for t in range(12):
                if t % 6 == 4:
                    split_hi(act, 3 + t // 6)
                if t >= 4:
                    act.wait_ge(u_out[t % 4], 16 * (t // 4))
                act.wait_ge(tile_done, t0 + t + 1)
                act.activation(ust[t % 4][:, :], bank[(t0 + t) % 2 + 6][:, 0:256], ACT.Copy).then_inc(tile_free, 1)
                act.wait_ge(tile_free, t0 + t + 1)
                act.dma_start(u_dram[P * (t % 6):P * (t % 6) + P, 256 * (t // 6):256 * (t // 6) + 256],
                              ust[t % 4][:, :]).then_inc(u_out[t % 4], 16)
            t0 = TILE0["lat2"]
            for i, (dst, width_) in enumerate(((krT[:, C:], T), (krT[:, 0:C], C))):
                act.wait_ge(tile_done, t0 + i + 1)
                act.activation(dst, bank[6 + (t0 + i) % 2][0:ROPE, 0:width_], ACT.Copy).then_inc(tile_free, 1)
            for i in range(2):
                lat_tile(t0 + 2 + i, 5 + i, *lat_tiles[5 + i])
                if i == 0:
                    split_hi(act, S_OF["gate"][0])

            def group_order(b):
                act.activation(utok[0:NK, b, :].rearrange("p (g j c) -> p g j c", g=GB, j=L),
                               ustage[0:NK, :, P * b:P * b + P].rearrange("p j (g c) -> p g j c", c=GC),
                               ACT.Copy).then_inc(ug_A, 1)

            act.wait_ge(kr_T, 1)
            act.activation(kr[:, :, :].rearrange("p t r -> p (t r)"), bank[5][:, 0:6 * ROPE], ACT.Copy).then_inc(kr_ready, 1)
            act.wait_ge(utok_in, 16 * L)
            group_order(1)
            group_order(3)

            def gate_tile(m, t):
                if m >= 2:
                    act.wait_ge(gate_out[m % 2], 16 * (m // 2))
                act.wait_ge(tile_done, t + 1)
                act.activation(gst[m % 2][:, :], bank[6 + t % 2][:, :], ACT.Sigmoid).then_inc(tile_free, 1)
                act.wait_ge(tile_free, t + 1)
                act.dma_start(gate_dram[m], gst[m % 2][:, :]).then_inc(gate_out[m % 2], 16)

            act.wait_ge(ug_A, 2)
            act.wait_ge(ug_D, 2)
            for b in range(NB):
                t = TILE0["gate"] + 4 * b
                for i in range(2):
                    act.wait_ge(u_T, 2 * b + 1 + i)
                    act.activation(U[:, 4 * i:4 * i + 4, :].rearrange("p g k -> p (g k)"), bank[i][:, 0:4 * NK], ACT.Copy).then_inc(u_evacA, 1)
                act.wait_ge(bp_T, b + 1)
                for d in range(2):
                    act.activation(WinT[:, 0, d].rearrange("p m n -> p (m n)"), bank[2 + d][:, :], ACT.Copy).then_inc(winT_A, 1)
                split_hi(act, S_OF["gate"][2 * b] + 1)
                act.wait_ge(bp_ready, 2 * b + 1)
                if b:
                    act.wait_ge(t_mm, b)
                for g2 in range(2):
                    half = slice(64 * g2, 64 * g2 + 64)
                    act.activation(bbd[half, :, :, :, GC * g2:GC * g2 + GC].rearrange("p r d m c -> p (r d) m c"),
                                   BB[half, :, :, PB * b:PB * b + PB, :].rearrange("p r d m c -> p (r d) m c"),
                                   ACT.Copy).then_inc(bbd_ready, 1)
                if b == 0:
                    act.wait_ge(stat_mm, 7)
                gate_tile(4 * b, t)
                act.wait_ge(kf_ready, b + 1)
                act.dma_start(kf_dram[b], Kf[:, :]).then_inc(kf_out, 16)
                gate_tile(4 * b + 1, t + 1)
                act.wait_ge(kf_out, 16 * b + 16)
                for j in range(L):
                    act.dma_start(TTm[GC * j:GC * j + GC, :, :],
                                  kf_dram[b].rearrange("(g c) m -> c g m", c=GC)[:, :, GC * j:GC * j + P]).then_inc(tt_in, 16)
                gate_tile(4 * b + 2, t + 2)
                split_hi(act, S_OF["gate"][2 * b] + 2)
                gate_tile(4 * b + 3, t + 3)
                if b == NB - 1:
                    act.wait_ge(cp_ready, NB + 1)
                    act.activation(cq_hi[:, :, :], cq[:, :, :], ACT.Copy).then_inc(prep_hi, 1)
                    act.wait_ge(state_ready, 2 * NB)
                    act.activation(ckv_hi[:, :, :], ckv[:, :, :], ACT.Copy).then_inc(prep_hi, 1)
                act.wait_ge(y_mm, b + 1)
                act.activation(Ysb[:, :, :].rearrange("p g k -> p (g k)"), bank[0][:, :], ACT.Copy).then_inc(y_evac, 1)
                act.wait_ge(y_T, b + 1)
                act.activation(ytok[:, :, 0:64].rearrange("p j (g c) -> p g j c", c=GC),
                               bank[1][0:64, :].rearrange("p (g j c) -> p g j c", g=4, j=L), ACT.Copy).then_inc(ytok_A, 1)
                act.wait_ge(y_T2, b + 1)
                act.activation(utok[:, b, 0:L * CK].rearrange("p (j k) -> p j k", j=L), bank[3][:, :].rearrange("p (j k) -> p j k", j=L),
                               ACT.Gelu_apprx_tanh).then_inc(gelu_done, 1)

            for i in range(2):
                act.wait_ge(gate_out[i], 16 * 8)
            for r, name in enumerate(("q_norm_g", "k_norm_g")):
                act.dma_start(qkg[:, r, :], a[name].rearrange("(o n) -> o n", o=1).to_broadcast([P, QK])).then_inc(attn_consts_in, 16)
            act.dma_start(rope[:, :, :], a["rope"].rearrange("(t p) n -> p t n", p=P)).then_inc(attn_consts_in, 16)
            t0 = TILE0["uq"]
            for t in range(8):
                if t % 4 == 0:
                    split_hi(act, S_OF["uq"][0] + 1 + t // 4)
                if t >= 2:
                    act.wait_ge(sq_used, t - 1)
                act.wait_ge(tile_done, t0 + t + 1)
                act.activation(sqt[t % 2][:, 0:384], bank[4 + t % 4][:, 0:384], ACT.Square).then_inc(q_sq, 1)
                act.activation(qsb[:, t % 4, 4 * (t // 4):4 * (t // 4) + 4, :].rearrange("p h d -> p (h d)"),
                               bank[4 + t % 4][:, 0:384], ACT.Copy).then_inc(tile_free, 1)
            t0 = TILE0["ukv"]
            split_hi(act, S_OF["glu"][0])
            for t in range(12):
                act.wait_ge(sq_used, 8 + t - 1)
                act.wait_ge(tile_done, t0 + t + 1)
                nope = bank[4 + t % 4][:, :].rearrange("p (h e) -> p h e", h=4)[:, :, 0:NOPE]
                act.activation(sqt[t % 2][:, 0:256].rearrange("p (h e) -> p h e", h=4), nope, ACT.Square).then_inc(q_sq, 1)
                act.activation(ksb[:, t // 2, 4 * (t % 2):4 * (t % 2) + 4, 0:NOPE], nope, ACT.Copy).then_inc(tile_free, 1)

            s0 = S_OF["glu"][0]

            def split_hi_at(s_first, k, i, rounds, wait_sem, wait_value):
                s = s_first + k
                n = N_OF_SPLIT[s]
                act.wait_ge(raw_in[n % 2], raw_in_count(n) + 16 * transfers(STREAM[n]) * (rounds // 2) * i)
                act.wait_ge(wait_sem, wait_value)
                w = width(STREAM[n], N_OF[STREAM[n]].index(n))
                act.activation(whi[s % 2][:, 0:w], raw[n % 2][:, 0:w], ACT.Copy).then_inc(hi_ready, 1)

            t0 = TILE0["glu"]
            for p in range(4):
                split_hi(act, s0 + p + 1)
                for mi in range(2):
                    m = 2 * p + mi
                    act.wait_ge(tile_done, t0 + 2 * m + 2)
                    if m >= 2:
                        act.wait_ge(s_ready, m - 1)
                    act.activation(sg[m % 2][:, :], bank[4 + (2 * m + 1) % 4][:, :], ACT.Sigmoid).then_inc(sg_ready, 1)

            def exp(i):
                act.wait_ge(max_ready, i + 1)
                if i >= 2:
                    act.wait_ge(p_T, 2 * (i - 2) + 2)
                act.activation(Pm[i % 2][:, :], ps[:, 2 * (i % 2):2 * (i % 2) + 2, 0:384], ACT.Exp, scale=SCALE,
                               bias=smx[:, i % 4, 1:2], accum_out=smx[:, i % 4, 2:3]).then_inc(exp_ready, 1)

            split_hi(act, S_OF["wo"][1])
            for i in range(3 * H):
                act.wait_ge(qk_T, i + 1)
                hi, _, w = qk_tile(i)
                act.activation(hi, qk_bank(i)[0:QK, 0:w], ACT.Copy).then_inc(qk_A, 1)

            exp(0)
            for i in range(4 * H):
                act.wait_ge(p_T, 2 * i + 2)
                if i >= 2:
                    act.wait_ge(o_mm, i - 1)
                act.activation(PT[i % 2][:, 3:6, :].rearrange("p a b -> p (a b)"), bank[5][:, 0:384], ACT.Copy).then_inc(pt_A, 1)
                if i + 1 < 4 * H:
                    exp(i + 1)
            for k in range(4):
                act.wait_ge(o_T, k + 1)
                act.activation(oT_hi[:, k, :], bank[k][:, :], ACT.Copy).then_inc(oT_hi_r, 1)
            for m in range(KD):
                if m == 4:
                    split_hi(act, S_OF["wout"][0])
                act.wait_ge(mg_f, m + 1)
                act.activation(mg_hi[:, m, :], mgf[m % 2][:, :], ACT.Copy).then_inc(mg_h, 1)

            for p in range(4):
                split_hi(act, S_OF["wout"][p] + 1)
                for mi in range(2):
                    m = 2 * p + mi
                    act.wait_ge(x1_ready, m + 1)
                    act.activation(sqx[:, m, :], xT[:, m, :], ACT.Square).then_inc(sqx_ready, 1)
            act.wait_ge(gain2_ready, 1)
            for k in range(KD):
                act.wait_ge(nx_ready, k + 1)
                if k >= 2:
                    act.wait_ge(h2_l, k - 1)
                act.activation(nh[k % 2][:, :], nx[k % 2][:, :], ACT.Identity, scale=gain2[:, k:k + 1],
                               bias=modb[:, 24 + k, 0:1]).then_inc(nh_ready, 1)
                act.activation(h2_hi[:, k, :], nx[k % 2][:, :], ACT.Identity, scale=gain2[:, k:k + 1],
                               bias=modb[:, 24 + k, 0:1]).then_inc(h2_h, 1)

            s0, t0 = S_OF["up"][0], TILE0["up"]

            def up_round(i, j, more):
                f = 2 * i + j
                if more:
                    split_hi_at(s0 + 1, j, i, 2, tile_done, t0 + 4 * i + 2 * j)
                for v in range(2):
                    act.wait_ge(tile_done, t0 + 4 * i + 2 * j + v + 1)
                    act.activation(cv[v][j][:, :], bank[4 + 2 * j + v][:, :], ACT.Identity,
                                   scale=VEC[:, bass.ds(V_W1 + 22 * v + f, 1)],
                                   bias=VEC[:, bass.ds(V_CB + 22 * v + f, 1)]).then_inc(cv_a, 1)
                act.wait_ge(cv_d, 4 * i + 2 * j + 2)
                act.activation(sl[j][:, :], cv[1][j][:, :], ACT.Silu).then_inc(silu_done, 1)
                act.wait_ge(act_f, f + 1)
                act.activation(act_hi[:, bass.ds(f, 1), :], cv[0][j][:, None, :], ACT.Copy).then_inc(act_h, 1)

            up_round(0, 0, True)
            up_round(0, 1, True)
            with act.Fori(1, 10) as i:
                for j in range(2):
                    up_round(i, j, True)
            up_round(10, 0, True)
            split_hi(act, S_OF["down"][0])
            up_round(10, 1, False)

            s0, t0 = S_OF["down"][0], TILE0["down"]

            def rows_out(pair, par):
                for mi in range(2):
                    act.wait_ge(xo_T, 2 * pair + mi + 1)
                    act.activation(ost[par][:, :, P * mi:P * mi + P],
                                   bank[2 * par + mi][:, :].rearrange("p (t n) -> p t n", t=TT_N),
                                   ACT.Copy).then_inc(ost_ready, 1)

            for p in range(11):
                split_hi(act, s0 + 1 + p)
                if p in (4, 7, 10):
                    pair = p // 3 - 1
                    if pair >= 2:
                        act.wait_ge(out_done[pair % 2], 16 * (pair // 2))
                    rows_out(pair, pair % 2)
            act.wait_ge(out_done[1], 16)
            rows_out(3, 1)

        @block.vector
        def _(dve):
            ch = Chain(dve, dve_chain)
            V_ = dve

            def tt(o_, x_, y_, op):
                return V_.tensor_tensor(o_, x_, y_, op)

            def ts(o_, x_, s1, s2=None, op0=ALU.mult, op1=ALU.add):
                if s2 is None:
                    return V_.tensor_scalar(o_, x_, s1, None, op0)
                return V_.tensor_scalar(o_, x_, s1, s2, op0, op1)

            def stt_(o_, x_, s, y_, op0, op1):
                return V_.scalar_tensor_tensor(out=o_, in0=x_, scalar=s, in1=y_, op0=op0, op1=op1)

            def rsqrt(y, v, t):
                ch.step(ts(y.bitcast(I32), v.bitcast(I32), -0.5, 1597463007.0))
                for _ in range(3):
                    ch.step(stt_(t, y, -0.5, y, ALU.mult, ALU.mult))
                    ch.step(tt(t, t, v, ALU.mult))
                    ch.step(stt_(y, t, 1.5, y, ALU.add, ALU.mult))

            V_.wait_ge(consts_ready, 1)
            ch.step(V_.tensor_reduce(dmask[:, :], ident[:, :].rearrange("p (g c) -> p c g", c=GC), AX.X, ALU.add))

            def mod_panel(w, acc, r):
                for k in range(KD):
                    if k == 0:
                        ch.step(ts(acc, w[:, k, :], cs[:, k, r:r + 1]))
                    elif k < KD - 1:
                        ch.step(stt_(acc, w[:, k, :], cs[:, k, r:r + 1], acc, ALU.mult, ALU.add))
                    else:
                        return stt_(acc, w[:, k, :], cs[:, k, r:r + 1], acc, ALU.mult, ALU.add)

            V_.wait_ge(cs_ready, 1)
            V_.wait_ge(sumsq1, 1)
            ch.step(ts(stv[:, 0:6], stv[:, 0:6], 1.0 / D, EPS))
            rsqrt(sty[:, 0:6], stv[:, 0:6], stt[:, 0:6])
            for t in range(6):
                ts(diag[:, t, :], ident[:, :], sty[:, t:t + 1]).then_inc(diag1_ready, 1)

            dm = lambda v: v.rearrange("p (d m) -> p d m", d=2)
            lam = VEC[:, V_LAM:V_LAM + 64].rearrange("p (d r m) -> p r d m", d=2, r=2)
            ch(tt(dm(TMP[:, 24, :]), lam[:, 0], lam[:, 0], ALU.mult))
            ch(tt(dm(TMP[:, 30, :]), lam[:, 1], lam[:, 1], ALU.mult))
            ch.wait()
            ch.step(tt(TMP[:, 24, :], TMP[:, 24, :], TMP[:, 30, :], ALU.add))
            V_.reciprocal(TMP[:, 24, :], TMP[:, 24, :]).then_inc(den_ready, 1)

            V_.wait_ge(rstd1_ready, 2)
            for k in range(4):
                V_.wait_ge(xT_mm, KD + k + 1)
                tt(cn[:, 2 * k:2 * k + 2, :], bank[(KD + k) % 6][:, :].rearrange("p (a t) -> p a t", a=2),
                   rstdb[:, None, 0:C].to_broadcast([P, 2, C]), ALU.mult).then_inc(cn_ready, 1)
            split_lo(dve, 0)
            V_.wait_ge(mod1_T, 1)
            ch.step(tt(modb[:, 0:16, :], bank[0][:, 0:32].rearrange("p (m r) -> p m r", r=2),
                       VEC[:, V_BMOD:V_BMOD + 16, None].to_broadcast([P, 16, 2]), ALU.add))
            for r in range(2):
                stt_(gain1[:, r, :], modb[:, 8:16, r], 1.0, VEC[:, V_N1:V_N1 + 8], ALU.add, ALU.mult).then_inc(gain1_ready, 1)
            V_.wait_ge(gain1_ready, 2)
            for k in range(KD):
                hc = hf[k % 2][:, 0:C]
                ch(ts(hc, cn[:, k, :], gain1[:, 1, k:k + 1], modb[:, k, 1:2]))
                V_.wait_ge(hf_ready, k + 1)
                ch.wait()
                ch(V_.tensor_copy(hc_hi[:, k, :], hc))
                ch(tt(h_lo[:, k, :], hf[k % 2][:, C:], h_hi[:, k, :].bitcast(F32), ALU.subtract))
                ch.wait()
                tt(hc_lo[:, k, :], hc, hc_hi[:, k, :].bitcast(F32), ALU.subtract).then_inc(h_split, 1)
            def mod2_panel(q, acc):
                n = N_OF["mod2"][q]
                V_.wait_ge(raw_in[n % 2], raw_in_count(n))
                mod_panel(raw[n % 2][:, :].rearrange("p (k n) -> p k n", k=KD), acc, 0).then_inc(mod2_used, 1)

            V_.wait_ge(xT_out, 16)
            V_.wait_ge(xn_ready, KD)
            q = 0
            for s, panels in ((1, 1), (2, 1), (3, 3), (4, 2), (5, 1)):
                if s == 1:
                    split_lo(dve, 1)
                for _ in range(panels):
                    mod2_panel(q, macc[:, q, :])
                    q += 1
                if s > 1:
                    split_lo(dve, s)

            V_.wait_ge(tile_done, TILE0["u"] + 12)
            V_.wait_ge(utok_in, 16 * L)
            for b in (0, 2):
                V_.tensor_copy(utok[0:NK, b, :].rearrange("p (g j c) -> p g j c", g=GB, j=L),
                               ustage[0:NK, :, P * b:P * b + P].rearrange("p j (g c) -> p g j c", c=GC)).then_inc(ug_D, 1)
            V_.wait_ge(ug_A, 2)
            V_.wait_ge(ug_D, 2)
            for r in range(2):
                V_.memset(SBD[r][0:64, :, :, 1, :], 0.0).then_inc(sbd_zero, 1)
                V_.memset(SBD[r][64:128, :, :, 0, :], 0.0).then_inc(sbd_zero, 1)
            V_.wait_ge(stat_mm, 7)
            ch(V_.tensor_reduce(stv[:, 0:4], bank[4][:, 0:12].rearrange("p (k t) -> p t k", t=TT_N), AX.X, ALU.add))
            V_.tensor_reduce(stv[:, 4:10], bank[4][:, 12:24].rearrange("p (k t) -> p t k", t=CT_N + TT_N), AX.X, ALU.add).then_inc(stat_read, 1)

            for b in range(NB):
                for i in range(2):
                    V_.wait_ge(u_evacA, 2 * b + 1 + i)
                    src = U[:, 4 * i:4 * i + 4, :]
                    ch(V_.tensor_copy(Ub[:, 4 * i:4 * i + 4, 0:CC], src[:, :, CC - 1::-1]))
                    V_.tensor_copy(Ub[:, 4 * i:4 * i + 4, CC:], src[:, :, NK - 1:CC - 1:-1]).then_inc(u_evacD, 1)
                V_.wait_ge(bp_T, b + 1)
                for d in range(2):
                    V_.tensor_copy(WinT[:, 1, d].rearrange("p m n -> p (m n)"), bank[4 + d][:, :]).then_inc(winT_D, 1)
                split_lo(dve, S_OF["gate"][2 * b] + 1)
                mod2_panel(EARLY_MOD2 + b, utok[:, b, 512:768])
                V_.wait_ge(t_mm, b + 1)
                if b:
                    V_.wait_ge(kf_out, 16 * b)
                ch(V_.tensor_copy(Kf[:, 0:P], bank[1][:, 0:P]))
                ch(V_.tensor_copy(Kf[:, P:], bank[0][:, GC:P]))
                ch.wait()
                m0, m1 = (16, 16 + 2 * EARLY_MOD2) if b == 0 else (14 + 2 * EARLY_MOD2 + 2 * b, 16 + 2 * EARLY_MOD2 + 2 * b)
                ch(tt(modb[:, m0:m1, 0], bank[0][:, 256:256 + m1 - m0], VEC[:, V_BMOD + m0:V_BMOD + m1], ALU.add))
                ch.step(tt(Kf[:, P - GC:P], bank[0][:, 0:GC], Kf[:, P - GC:P], ALU.add))
                stt_(Kf[:, P - GC:P], dmask[:, :], VEC[:, V_DSKIP + b:V_DSKIP + b + 1], Kf[:, P - GC:P],
                     ALU.mult, ALU.add).then_inc(kf_ready, 1)
                V_.wait_ge(e_ready, b + 1)
                if b:
                    V_.wait_ge(y_T2, b)
                for d in range(2):
                    V_.wait_ge(v_mm, 2 * b + 1 + d)
                    if d:
                        V_.wait_ge(kf_out, 16 * b + 16)
                    vr, vi = (bank[2 + 2 * r + d][:, 0:4 * NK].rearrange("p (m k) -> p m k", m=PB) for r in range(2))
                    E = E_[b % 2]
                    ec, es = E[:, 0, 4 * d:4 * d + 4, :], E[:, 1, 4 * d:4 * d + 4, :]
                    ch(tt(W[:, 0, d], vr, ec, ALU.mult))
                    ch(tt(tmpA[:, :, :], vi, es, ALU.mult))
                    ch(tt(W[:, 1, d], vi, ec, ALU.mult))
                    tt(tmpB[:, :, :], vr, es, ALU.mult).then_inc(v_read, 1)
                    V_.wait_ge(v_read, 2 * b + 1 + d)
                    ch.wait()
                    ch(tt(W[:, 0, d], W[:, 0, d], tmpA[:, :, :], ALU.subtract))
                    ch(tt(W[:, 1, d], W[:, 1, d], tmpB[:, :, :], ALU.add))
                    ch.wait()
                    for r in range(2):
                        for m in range(PB):
                            col = 16 * d + PB * b + m
                            w = W[:, r, d, m, :]
                            ch(V_.tensor_tensor_scan(w, r8[:, col:col + 1].to_broadcast([P, NK]), w, 0.0, ALU.mult, ALU.add))
                    ch.wait()
                    at_ = slice(CC - 1, NK - 1) if d == 0 else slice(NK - 2, CC - 2, -1)
                    wr, wi, ec, es = W[:, 0, d][:, :, at_], W[:, 1, d][:, :, at_], ec[:, :, at_], es[:, :, at_]
                    for r, (x1_, y1_, op) in enumerate(((wr, wi, ALU.add), (wi, wr, ALU.subtract))):
                        ch(tt(tmpA[:, :, 0:CK], x1_, ec, ALU.mult))
                        ch(tt(tmpB[:, :, 0:CK], y1_, es, ALU.mult))
                        ch.wait()
                        for g2 in range(2):
                            half = slice(64 * g2, 64 * g2 + 64)
                            ins = tt(SBD[r][half, d, :, g2, :], tmpA[half, :, 0:CK], tmpB[half, :, 0:CK], op)
                            if r == 1 and g2 == 1:
                                ins.then_inc(state_ready, 1)
                                V_.wait_ge(state_ready, 2 * b + 1 + d)
                            else:
                                ch(ins)
                        ch.wait()
                split_lo(dve, S_OF["gate"][2 * b] + 2)
                if b + 1 < NB:
                    if b == 0:
                        V_.wait_ge(c_in, 16)
                        V_.wait_ge(t_mm, 1)
                    else:
                        V_.wait_ge(y_mm, b)
                    CPn, pr, sh = CP_[(b + 1) % 2], slice(PB * (b + 1), PB * (b + 2)), [P, PB, 9, GC]
                    cr, ci = (CT[:, 1, r, pr, :][:, :, None, :].to_broadcast(sh) for r in range(2))
                    lr, li = (LP[:, r, 0:9, :].rearrange("p q (d m) -> p d m q", d=2)[:, 1, pr, ::-1][:, :, :, None].to_broadcast(sh)
                              for r in range(2))
                    re, im = (CPn[:, r, 1].rearrange("p m (q c) -> p m q c", c=GC) for r in range(2))
                    t1 = tmpC[:, :].rearrange("p (m q c) -> p m q c", m=PB, c=GC)
                    ch(tt(re, cr, lr, ALU.mult))
                    ch(tt(t1, ci, li, ALU.mult))
                    ch.wait()
                    ch(tt(re, re, t1, ALU.subtract))
                    ch(tt(im, cr, li, ALU.mult))
                    ch.wait()
                    ch(tt(t1, ci, lr, ALU.mult))
                    ch.wait()
                    tt(im, im, t1, ALU.add).then_inc(cpD_ready, 1)
                if b == NB - 1:
                    for i, (full, hi, lo) in enumerate(((cq, cq_hi, cq_lo), (ckv, ckv_hi, ckv_lo))):
                        V_.wait_ge(prep_hi, i + 1)
                        tt(lo[:, :, :], full[:, :, :], hi[:, :, :].bitcast(F32), ALU.subtract).then_inc(prep_lo, 1)
                V_.wait_ge(y_T, b + 1)
                V_.tensor_copy(ytok[:, :, 64:128].rearrange("p j (g c) -> p g j c", c=GC),
                               bank[2][0:64, :].rearrange("p (g j c) -> p g j c", g=4, j=L)).then_inc(ytok_D, 1)

            ch(ts(stv[:, 0:4], stv[:, 0:4], 1.0 / QL, EPS))
            ch(ts(stv[:, 4:10], stv[:, 4:10], 1.0 / KVL, EPS))
            ch.wait()
            rsqrt(rl[:, :], stv[:, :], stt[:, :])

            V_.wait_ge(attn_consts_in, 48)
            for t in range(8):
                if t % 4 == 0:
                    split_lo(dve, S_OF["uq"][0] + 1 + t // 4)
                V_.wait_ge(q_sq, t + 1)
                c0 = 8 * (t % 4) + 4 * (t // 4)
                V_.tensor_reduce(stq[:, 0, c0:c0 + 4], sqt[t % 2][:, 0:384].rearrange("p (h d) -> p h d", h=4),
                                 AX.X, ALU.add).then_inc(sq_used, 1)
            split_lo(dve, S_OF["glu"][0])
            t0 = TILE0["ukv"]
            for t in range(12):
                V_.wait_ge(tile_free, t0 + t + 1)
                ts(V[:, t // 2, 256 * (t % 2):256 * (t % 2) + 256].rearrange("p (h e) -> p h e", h=4),
                   bank[4 + t % 4][:, :].rearrange("p (h e) -> p h e", h=4)[:, :, NOPE:],
                   rl[:, 4 + t // 2:5 + t // 2]).then_inc(v_copy, 1)
                V_.wait_ge(q_sq, 8 + t + 1)
                c0 = 32 + 8 * (t // 2) + 4 * (t % 2)
                V_.tensor_reduce(stq[:, 0, c0:c0 + 4], sqt[t % 2][:, 0:256].rearrange("p (h d) -> p h d", h=4),
                                 AX.X, ALU.add).then_inc(sq_used, 1)

            qg, kg = qkg[:, 0, :], qkg[:, 1, :]
            rq = stq[:, 0, 0:32].rearrange("p (t h) -> p t h", t=TT_N)[:, :, :, None]
            rk = stq[:, 1, 32:80].rearrange("p (t h) -> p t h", t=6)[:, :, :, None]
            V_.wait_ge(mod2_mm, 1)
            ch.step(tt(modb[:, 38:40, 0], bank[0][:, 0:2], VEC[:, V_BMOD + 38:V_BMOD + 40], ALU.add))
            stt_(gain2[:, :], modb[:, 32:40, 0], 1.0, VEC[:, V_N2:V_N2 + 8], ALU.add, ALU.mult).then_inc(gain2_ready, 1)
            rkn = stq[:, 0, 32:80].rearrange("p (t h) -> p t h", t=6)[:, :, :, None]
            tq_ = [tq[:, i, :].rearrange("p (t h c) -> p t h c", t=TT_N, h=H) for i in range(4)]

            def qk_norm_part(m):
                if m == 0:
                    V_.wait_ge(sq_used, 20)
                    V_.wait_ge(kr_ready, 1)
                    V_.wait_ge(tile_free, TILE0["glu"])
                    ch.step(tt(sqt[0][:, 0:192].rearrange("p (t r) -> p t r", t=6), kr[:, :, :], kr[:, :, :], ALU.mult))
                    ch.step(V_.tensor_reduce(stq3[:, :], sqt[0][:, 0:192].rearrange("p (t r) -> p t r", t=6), AX.X, ALU.add))
                    ks = stq[:, 0, 32:80].rearrange("p (t h) -> p t h", t=6)
                    qs, r_q = stq[:, 0, 0:32].rearrange("p (t h) -> p t h", t=TT_N), rl[:, 0:4, None].to_broadcast([P, TT_N, H])
                    r_k = rl[:, 4:10, None].to_broadcast([P, 6, H])
                    for _ in range(2):
                        ch(tt(qs, qs, r_q, ALU.mult))
                        ch.step(tt(ks, ks, r_k, ALU.mult))
                    ch.step(tt(ks, ks, stq3[:, :, None].to_broadcast([P, 6, H]), ALU.add))
                    ch.step(ts(stq[:, 0, :], stq[:, 0, :], 1.0 / QK, EPS))
                    rsqrt(stq[:, 1, :], stq[:, 0, :], sqt[1][:, 0:80])
                    ch(tt(qs, stq[:, 1, 0:32].rearrange("p (t h) -> p t h", t=TT_N), r_q, ALU.mult))
                    ch.step(tt(ks, stq[:, 1, 32:80].rearrange("p (t h) -> p t h", t=6), r_k, ALU.mult))
                elif m == 1:
                    ch.step(tt(qsb[:, :, :, :], qsb[:, :, :, :], rq.to_broadcast([P, TT_N, H, QK]), ALU.mult))
                elif m == 2:
                    ch.step(tt(qsb[:, :, :, :], qsb[:, :, :, :], qg[:, None, None, :].to_broadcast([P, TT_N, H, QK]), ALU.mult))
                elif m == 3:
                    r1, r2 = qsb[:, :, :, 64:80], qsb[:, :, :, 80:96]
                    sh4 = [P, TT_N, H, 16]
                    co, si = rope[:, :, None, 0:16].to_broadcast(sh4), rope[:, :, None, 16:32].to_broadcast(sh4)
                    ch(tt(tq_[0], r1, co, ALU.mult))
                    ch(tt(tq_[1], r2, si, ALU.mult))
                    ch(tt(tq_[2], r1, si, ALU.mult))
                    ch(tt(tq_[3], r2, co, ALU.mult))
                    ch.wait()
                    ch(tt(r1, tq_[0], tq_[1], ALU.subtract))
                    tt(r2, tq_[2], tq_[3], ALU.add).then_inc(q_ready, 1)
                elif m == 4:
                    kn = ksb[:, :, :, 0:NOPE]
                    ch.step(tt(kn, kn, rkn.to_broadcast([P, 6, H, NOPE]), ALU.mult))
                elif m == 5:
                    kn = ksb[:, :, :, 0:NOPE]
                    ch(tt(kn, kn, kg[:, None, None, 0:NOPE].to_broadcast([P, 6, H, NOPE]), ALU.mult))
                elif m == 6:
                    V_.wait_ge(q_ready, 1)
                    ch.step(tt(kr[:, :, :], kr[:, :, :], kg[:, None, NOPE:].to_broadcast([P, 6, ROPE]), ALU.mult))
                    r1, r2 = kr[:, CT_N:, 0:16], kr[:, CT_N:, 16:32]
                    co, si = rope[:, :, 0:16], rope[:, :, 16:32]
                    tk = [tq[:, i, 0:64].rearrange("p (t c) -> p t c", t=TT_N) for i in range(4)]
                    ch(tt(tk[0], r1, co, ALU.mult))
                    ch(tt(tk[1], r2, si, ALU.mult))
                    ch(tt(tk[2], r1, si, ALU.mult))
                    ch(tt(tk[3], r2, co, ALU.mult))
                    ch.wait()
                    ch(tt(r1, tk[0], tk[1], ALU.subtract))
                    ch.step(tt(r2, tk[2], tk[3], ALU.add))
                    tt(ksb[:, :, :, NOPE:], kr[:, :, None, :].to_broadcast([P, 6, H, ROPE]),
                       rk.to_broadcast([P, 6, H, ROPE]), ALU.mult).then_inc(k_ready, 1)

            t0 = TILE0["glu"]
            for m in range(KD):
                if m % 2 == 0:
                    split_lo(dve, S_OF["glu"][m // 2] + 1)
                qk_norm_part(m)
                V_.wait_ge(sgs_ready, m + 1)
                V_.wait_ge(tile_done, t0 + 2 * m + 1)
                tt(sT[:, m, :], bank[4 + (2 * m) % 4][:, :], sg[m % 2][:, :], ALU.mult).then_inc(s_ready, 1)

            def row_max(i):
                V_.wait_ge(s_mm, i + 1)
                if i >= 4:
                    V_.wait_ge(exp_ready, i - 3)
                ch.step(V_.tensor_reduce(smx[:, i % 4, 0:1], ps[:, 2 * (i % 2):2 * (i % 2) + 2, 0:384], AX.XY, ALU.max))
                ts(smx[:, i % 4, 1:2], smx[:, i % 4, 0:1], -SCALE).then_inc(max_ready, 1)

            for i in range(3 * H):
                if i == LATE_QK:
                    row_max(0)
                V_.wait_ge(qk_A, i + 1)
                hi, lo, w = qk_tile(i)
                tt(lo, qk_bank(i)[0:QK, 0:w], hi.bitcast(F32), ALU.subtract).then_inc(qk_D, 1)
            split_lo(dve, S_OF["wo"][1])

            def o_out(i):
                h, q = i // 4, i % 4
                V_.wait_ge(exp_ready, i + 1)
                ch.step(V_.reciprocal(smx[:, i % 4, 3:4], smx[:, i % 4, 2:3]))
                V_.wait_ge(o_mm, i + 1)
                ts(otok[:, q, VD * h:VD * h + VD], bank[6 + i % 2][:, 0:VD], smx[:, i % 4, 3:4]).then_inc(o_evac, 1)

            def late_mod2_step(p, k):
                n = N_OF["mod2"][EARLY_MOD2 + NB + p]
                if k == 0:
                    V_.wait_ge(raw_in[n % 2], raw_in_count(n))
                w, acc = raw[n % 2][:, :].rearrange("p (k n) -> p k n", k=KD)[:, k, :], macc_late[:, p, :]
                if k == 0:
                    ch(ts(acc, w, cs[:, k, 0:1]))
                else:
                    ins = stt_(acc, w, cs[:, k, 0:1], acc, ALU.mult, ALU.add)
                    if k < KD - 1:
                        ch(ins)
                    else:
                        ins.then_inc(mod2_used, 1)

            for i in range(4 * H):
                if i + 1 < 4 * H:
                    row_max(i + 1)
                V_.wait_ge(p_T, 2 * i + 1)
                if i >= 2:
                    V_.wait_ge(o_mm, i - 1)
                V_.tensor_copy(PT[i % 2][:, 0:3, :].rearrange("p a b -> p (a b)"), bank[4][:, 0:384]).then_inc(pt_D, 1)
                if i >= 1:
                    o_out(i - 1)
                late_mod2_step(i // KD, i % KD)
            o_out(4 * H - 1)
            for k in range(4):
                V_.wait_ge(oT_hi_r, k + 1)
                tt(oT_lo[:, k, :], bank[k][:, :], oT_hi[:, k, :].bitcast(F32), ALU.subtract).then_inc(oT_lo_r, 1)

            def merged_lo(m):
                V_.wait_ge(mg_h, m + 1)
                tt(mg_lo[:, m, :], mgf[m % 2][:, :], mg_hi[:, m, :].bitcast(F32), ALU.subtract).then_inc(mg_l, 1)

            t0 = TILE0["wo"]
            for m in range(KD):
                V_.wait_ge(tile_done, t0 + m + 1)
                V_.wait_ge(gload_in[m % 4], 16 * (2 + m // 4 + 1))
                if m >= 2:
                    V_.wait_ge(mg_l, m - 1)
                ch.step(tt(mgf[m % 2][:, :], bank[6 + m % 2][:, :], gload[m % 4][:, :], ALU.mult))
                tt(mgf[m % 2][:, :], mgf[m % 2][:, :], sT[:, m, :], ALU.add).then_inc(mg_f, 1)
                if m >= 1:
                    merged_lo(m - 1)
                if m == 5:
                    split_lo(dve, S_OF["wout"][0])
            merged_lo(KD - 1)

            t0 = TILE0["wout"]
            V_.wait_ge(xT_back, 16)
            for p in range(4):
                split_lo(dve, S_OF["wout"][p] + 1)
                for mi in range(2):
                    m = 2 * p + mi
                    V_.wait_ge(tile_done, t0 + m + 1)
                    stt_(xT[:, m, :], bank[4 + m % 2][:, :], modb[:, 16 + m, 0:1], xT[:, m, :], ALU.mult, ALU.add).then_inc(x1_ready, 1)
            V_.wait_ge(stat2_mm, 1)
            ch.step(V_.tensor_reduce(stv[:, 0:4], bank[0][:, 0:32].rearrange("p (m q) -> p q m", q=TT_N), AX.X, ALU.add))
            ch.step(ts(stv[:, 0:4], stv[:, 0:4], 1.0 / D, EPS))
            rsqrt(sty[:, 0:4], stv[:, 0:4], stt[:, 0:4])
            for t in range(TT_N):
                ts(diag3[:, t, :], ident[:, :], sty[:, t:t + 1]).then_inc(diag3_ready, 1)
            V_.wait_ge(rstd3_mm, 1)
            ch(tt(modb[:, 40:48, 0], bank[2][:, 0:8], VEC[:, V_BMOD + 40:V_BMOD + 48], ALU.add))
            for k in range(KD + 1):
                if k < KD:
                    if k >= 2:
                        V_.wait_ge(nh_ready, k - 1)
                    tt(nx[k % 2][:, :], xT[:, k, :], bank[1][:, :], ALU.mult).then_inc(nx_ready, 1)
                if k >= 1:
                    V_.wait_ge(h2_h, k)
                    tt(h2_lo[:, k - 1, :], nh[(k - 1) % 2][:, :], h2_hi[:, k - 1, :].bitcast(F32), ALU.subtract).then_inc(h2_l, 1)

            s0, t0 = S_OF["up"][0], TILE0["up"]

            def up_round(i, j, more):
                f = 2 * i + j
                if more:
                    s = s0 + 1 + j
                    V_.wait_ge(hi_ready, s + 1 + 2 * i)
                    V_.tensor_tensor(wlo[s % 2][:, :], raw[N_OF_SPLIT[s] % 2][:, :], whi[s % 2][:, :].bitcast(F32),
                                     ALU.subtract).then_inc(lo_ready, 1)
                for v in range(2):
                    u_ = bank[4 + 2 * j + v]
                    V_.wait_ge(cv_a, 4 * i + 2 * j + v + 1)
                    ch.step(stt_(cv[v][j][:, 1:], u_[:, 0:T - 1], VEC[:, bass.ds(V_W0 + 22 * v + f, 1)], cv[v][j][:, 1:],
                                 ALU.mult, ALU.add))
                    stt_(cv[v][j][:, 0:T - 1], u_[:, 1:], VEC[:, bass.ds(V_W2 + 22 * v + f, 1)], cv[v][j][:, 0:T - 1],
                         ALU.mult, ALU.add).then_inc(cv_d, 1)
                V_.wait_ge(silu_done, f + 1)
                tt(cv[0][j][:, :], cv[0][j][:, :], sl[j][:, :], ALU.mult).then_inc(act_f, 1)
                V_.wait_ge(act_h, f + 1)
                tt(act_lo[:, bass.ds(f, 1), :], cv[0][j][:, None, :], act_hi[:, bass.ds(f, 1), :].bitcast(F32),
                   ALU.subtract).then_inc(act_l, 1)

            up_round(0, 0, True)
            up_round(0, 1, True)
            with dve.Fori(1, 10) as i:
                ch.enter(i - 1, 4)
                for j in range(2):
                    up_round(i, j, True)
                ch.leave(9)
            up_round(10, 0, True)
            split_lo(dve, S_OF["down"][0])
            up_round(10, 1, False)

            s0, t0 = S_OF["down"][0], TILE0["down"]
            for p in range(12):
                if p < 11:
                    split_lo(dve, s0 + p + 1)
                if p % 3 == 2:
                    pair = p // 3
                    if pair >= 2:
                        V_.wait_ge(xo_T, 2 * (pair - 2) + 2)
                    for mi in range(2):
                        m = 2 * pair + mi
                        V_.wait_ge(tile_done, t0 + m + 1)
                        stt_(xo[pair % 2][:, mi, :], bank[4 + m % 4][:, :], modb[:, 40 + m, 0:1], xT[:, m, :],
                             ALU.mult, ALU.add).then_inc(xo_ready, 1)

        @block.tensor
        def _(pe):
            def product(out_, wx, last=True, first=True):
                ins = None
                for i, (w_, x_) in enumerate(wx):
                    ins = pe.matmul(out_, w_, x_, start=(first and i == 0), stop=(last and i == len(wx) - 1))
                return ins

            def three(s_hi, s_lo, m_hi, m_lo):
                return [(s_hi, m_hi), (s_hi, m_lo), (s_lo, m_hi)]

            def tok(k, t):
                if t < CT_N:
                    return hc_hi[:, k, P * t:P * t + P], hc_lo[:, k, P * t:P * t + P]
                return h_hi[:, k, P * (t - CT_N):P * (t - CT_N) + P], h_lo[:, k, P * (t - CT_N):P * (t - CT_N) + P]

            def panel(s, k_tiles, w):
                pe.wait_ge(lo_ready, s + 1)
                return [b_[s % 2][:, 0:k_tiles * w].rearrange("p (k n) -> p k n", k=k_tiles) for b_ in (whi, wlo)]

            def mod1_products(p, buf, signal, value):
                pe.wait_ge(signal, value)
                if p >= 2:
                    pe.wait_ge(mrow_ready, p - 1)
                w = buf[:, :].rearrange("p (k n) -> p k n", k=KD)
                product(bank[6 + p % 2][0:2, 0:256], [(cs[:, k, :], w[:, k, :]) for k in range(KD)]).then_inc(mod1_pe, 1)

            pe.wait_ge(cs_ready, 1)
            for p in range(2):
                mod1_products(p, raw[p], raw_in[p], 16)

            pe.wait_ge(consts_ready, 1)
            pe.wait_ge(x_in, 16)
            for k in range(KD):
                if k >= 6:
                    pe.wait_ge(xT_ready, k - 5)
                for t in range(TT_N):
                    ins = pe.transpose(bank[k % 6][:, P * t:P * t + P], xtok[:, t, P * k:P * k + P], ident[:, :])
                ins.then_inc(xT_mm, 1)

            pe.wait_ge(ctx_in, 16)
            for k2 in range(KD // 2):
                pe.wait_ge(xT_ready, k2 + 3)
                for a_ in range(2):
                    for t in range(CT_N):
                        ins = pe.transpose(bank[(KD + k2) % 6][:, C * a_ + P * t:C * a_ + P * t + P],
                                           ctok[:, t, P * (2 * k2 + a_):P * (2 * k2 + a_) + P], ident[:, :])
                ins.then_inc(xT_mm, 1)
            for p in range(2, 6):
                mod1_products(p, early[p - 2], early_in[p - 2], 16)

            pe.wait_ge(diag1_ready, TT_N + CT_N)
            pe.wait_ge(xT_ready, KD)
            for t in range(TT_N + CT_N):
                ins = pe.matmul(bank[0 if t >= TT_N else 1][:, P * (t % TT_N):P * (t % TT_N) + P], ones[:, :], diag[:, t, :], start=True, stop=True)
            ins.then_inc(rstd1_mm, 1)
            for p in range(6, 8):
                mod1_products(p, early[p - 2], early_in[p - 2], 16)

            pe.wait_ge(mrow_ready, 8)
            pe.wait_ge(rstd1_ready, 2)
            for m in range(16):
                ins = pe.transpose(bank[0][:, 2 * m:2 * m + 2], mrow[:, P * m:P * m + P], ident[0:2, 0:2])
            ins.then_inc(mod1_T, 1)

            def next_tile(t):
                if t >= 2:
                    pe.wait_ge(tile_free, t - 1)
                return bank[6 + t % 2]

            def lat_products(t, out_, wh, wl, cols, x, ks):
                xh, xl = x
                for k in ks:
                    ins = product(out_, three(wh[:, k, cols], wl[:, k, cols], xh[:, k, :], xl[:, k, :]),
                                  first=k == 0, last=k == KD - 1)
                if KD - 1 in ks:
                    ins.then_inc(tile_done, 1)

            low, high, of_x, of_ctx = slice(0, P), slice(P, 2 * P), (h_hi, h_lo), (hc_hi, hc_lo)
            wh, wl = panel(S_OF["lat"][0], KD, 256)
            for k in range(KD):
                pe.wait_ge(h_split, k + 1)
                lat_products(0, bank[6], wh, wl, low, of_x, [k])
                lat_products(1, bank[7], wh, wl, high, of_x, [k])
            def stat_job(i):
                pe.wait_ge(sq_lat, i + 1)
                if i < 3:
                    tiles, c0 = TT_N, TT_N * i
                else:
                    k, of_c = (i - 3) // 2, (i - 3) % 2
                    tiles, c0 = (CT_N, 12 + 6 * k) if of_c else (TT_N, 12 + 6 * k + CT_N)
                for tt_ in range(tiles):
                    ins = pe.matmul(bank[4][:, c0 + tt_:c0 + tt_ + 1], gst[i % 2][:, P * tt_:P * tt_ + P], ones[:, 0:1], start=True, stop=True)
                ins.then_inc(stat_mm, 1)

            t = 2
            wh, wl = panel(S_OF["lat"][1], KD, 256)
            pe.wait_ge(cn_ready, 4)
            for i, (cols, x) in enumerate(((low, of_x), (high, of_x), (high, of_ctx))):
                lat_products(t, next_tile(t)[:, 0:C if x is of_ctx else T], wh, wl, cols, x, range(KD))
                stat_job(i)
                t += 1

            for p in range(2):
                wh, wl = panel(S_OF["u"][p], KD, 256)
                for tt_ in range(CT_N + TT_N):
                    product(next_tile(t)[:, 0:256],
                            [q_ for k in range(KD) for q_ in three(*tok(k, tt_), wh[:, k, :], wl[:, k, :])]).then_inc(tile_done, 1)
                    t += 1
                    if p == 0 and tt_ < 2:
                        stat_job(3 + tt_)

            wh, wl = panel(S_OF["lat"][2], KD, 160)
            for cols, x in ((slice(P, P + ROPE), of_x), (slice(P, P + ROPE), of_ctx), (low, of_x), (low, of_ctx)):
                rows_ = cols.stop - cols.start
                lat_products(t, next_tile(t)[0:rows_, 0:C if x is of_ctx else T], wh, wl, cols, x, range(KD))
                t += 1
            for tt_ in range(CT_N + TT_N):
                ins = pe.transpose(bank[5][:, ROPE * tt_:ROPE * tt_ + ROPE], krT[:, P * tt_:P * tt_ + P], ident[0:ROPE, 0:ROPE])
            ins.then_inc(kr_T, 1)

            def gate_products(m, t):
                wh, wl = panel(S_OF["gate"][m // 2], KD, 256)
                col = P * (m % 2)
                product(next_tile(t), [q_ for k in range(KD) for q_ in three(
                    wh[:, k, col:col + P], wl[:, k, col:col + P], h_hi[:, k, :], h_lo[:, k, :])]).then_inc(tile_done, 1)

            for b in range(NB):
                t = TILE0["gate"] + 4 * b
                pe.wait_ge(ug_D, 1 if b == 0 else 2)
                if b == 1:
                    pe.wait_ge(ug_A, 2)
                for g in range(GB):
                    if b >= 1 and g == 0:
                        pe.wait_ge(y_evac, b)
                    if b >= 1 and g == 4:
                        pe.wait_ge(ytok_A, b)
                    ins = pe.transpose(bank[g // 4][:, NK * (g % 4):NK * (g % 4) + NK],
                                       utok[0:NK, b, P * g:P * g + P], ident[0:NK, 0:NK])
                    if g % 4 == 3:
                        ins.then_inc(u_T, 1)
                if b == 0:
                    stat_job(5)
                    stat_job(6)
                    pe.wait_ge(stat_read, 1)
                    pe.wait_ge(kr_ready, 1)
                pe.wait_ge(bp_ready, 2 * b + 2)
                if b >= 1:
                    pe.wait_ge(v_read, 2 * b)
                    pe.wait_ge(ytok_D, b)
                    pe.wait_ge(gelu_done, b)
                for r in range(2):
                    for d in range(2):
                        for m in range(PB):
                            ins = pe.transpose(bank[2 + 2 * r + d][:, P * m:P * m + P], BP[:, r, d, m, :], ident[:, :])
                ins.then_inc(bp_T, 1)
                gate_products(4 * b, t)
                pe.wait_ge(cp_ready, 2 + b)
                if b:
                    pe.wait_ge(cpD_ready, b)
                pe.wait_ge(u_evacA, 2 * b + 2)
                pe.wait_ge(u_evacD, 2 * b + 2)
                pe.wait_ge(bbd_ready, 2 * b + 2)
                pe.wait_ge(mod2_used, EARLY_MOD2 + b)
                for q in range(2 * EARLY_MOD2 if b == 0 else 2):
                    part = macc[:, q // 2, P * (q % 2):P * (q % 2) + P] if b == 0 else utok[:, b - 1, 512 + P * q:640 + P * q]
                    pe.matmul(bank[0][:, 256 + q:257 + q], part, ones[:, 0:1], start=True, stop=True)
                for m in range(PB):
                    for d in range(2):
                        c0 = GC * d
                        ins = product(bank[d][32 * m:32 * m + 32, 0:P],
                                      [(bbd[:, r, d, m, :], CP_[b % 2][:, r, d, m, c0:c0 + P]) for r in range(2)])
                ins.then_inc(t_mm, 1)
                pe.wait_ge(winT_A, 2 * b + 2)
                pe.wait_ge(winT_D, 2 * b + 2)
                for d in range(2):
                    u_ = Ub if d else U
                    for r in range(2):
                        for m in range(PB):
                            for g2 in range(2):
                                ins = pe.matmul(bank[2 + 2 * r + d][64 * g2:64 * g2 + 64, NK * m:NK * m + NK],
                                                WinT[:, r, d, m, 64 * g2:64 * g2 + 64], u_[:, 2 * m + g2, :], start=True, stop=True)
                    ins.then_inc(v_mm, 1)
                for i in range(1, 4):
                    gate_products(4 * b + i, t + i)
                pe.wait_ge(kf_ready, b + 1)
                pe.wait_ge(state_ready, 2 * b + 2)
                pe.wait_ge(sbd_zero, 4)
                pe.wait_ge(tt_in, 16 * L * (b + 1))
                for m in range(PB):
                    product(bank[0][:, P * m:P * m + P],
                            [(CP_[b % 2][:, r, d, m, GC * (1 - d):GC * (1 - d) + P], SBD[r][:, d, m].rearrange("p g k -> p (g k)"))
                             for d in range(2) for r in range(2)], last=False)
                    for g2 in range(2):
                        g = 2 * m + g2
                        ins = pe.matmul(bank[0][:, CK * g:CK * g + CK], TTm[:, g, :], U[:, g, CC:], start=False, stop=g2 == 1)
                ins.then_inc(y_mm, 1)
                pe.wait_ge(y_evac, b + 1)
                for g in range(GB):
                    ins = pe.transpose(bank[1 + g // 4][0:CK, P * (g % 4):P * (g % 4) + P], Ysb[:, g, :], ident[:, :])
                ins.then_inc(y_T, 1)
                pe.wait_ge(ytok_A, b + 1)
                pe.wait_ge(ytok_D, b + 1)
                for j in range(L):
                    ins = pe.transpose(bank[3][:, CK * j:CK * j + CK], ytok[:, j, :], ident[0:CK, 0:CK])
                ins.then_inc(y_T2, 1)

            def token_tile(n_):
                if n_ in (2, 3):
                    pe.wait_ge(tile_free, TILE0["uq"])
                elif n_ >= 4:
                    pe.wait_ge(tile_free, TILE0["uq"] + n_ - 3)
                if n_ >= 12:
                    pe.wait_ge(v_copy, n_ - 11)
                return bank[4 + n_ % 4]

            pe.wait_ge(prep_lo, 1)
            for p in range(2):
                wh, wl = panel(S_OF["uq"][p], 3, 384)
                for tt_ in range(TT_N):
                    product(token_tile(4 * p + tt_)[:, 0:384], [q_ for k in range(3) for q_ in three(
                        cq_hi[:, k, P * tt_:P * tt_ + P], cq_lo[:, k, P * tt_:P * tt_ + P], wh[:, k, :], wl[:, k, :])]).then_inc(tile_done, 1)
            pe.wait_ge(prep_lo, 2)
            wh, wl = panel(S_OF["ukv"][0], 2, 1024)
            for tt_ in range(CT_N + TT_N):
                for half in range(2):
                    product(token_tile(8 + 2 * tt_ + half), [q_ for k in range(2) for q_ in three(
                        ckv_hi[:, k, P * tt_:P * tt_ + P], ckv_lo[:, k, P * tt_:P * tt_ + P],
                        wh[:, k, 512 * half:512 * half + 512], wl[:, k, 512 * half:512 * half + 512])]).then_inc(tile_done, 1)

            pe.wait_ge(mod2_used, EARLY_MOD2 + NB)
            for q in range(2):
                ins = pe.matmul(bank[0][:, q:q + 1], utok[:, NB - 1, 512 + P * q:640 + P * q], ones[:, 0:1], start=True, stop=True)
            ins.then_inc(mod2_mm, 1)

            pe.wait_ge(yprep_lo, NB)
            for p in range(4):
                wh, wl = panel(S_OF["glu"][p], 4, 512)
                for mi in range(2):
                    m = 2 * p + mi
                    if m < 2:
                        pe.wait_ge(v_copy, 10 + 2 * m)
                    if m >= 2:
                        pe.wait_ge(s_ready, m - 1)
                        pe.wait_ge(sg_ready, m - 1)
                    for v in range(2):
                        col = 256 * v + P * mi
                        product(bank[4 + (2 * m + v) % 4], [q_ for k in range(4) for q_ in three(
                            wh[:, k, col:col + P], wl[:, k, col:col + P], y_hi[:, k, :], y_lo[:, k, :])]).then_inc(tile_done, 1)

            def scores(i):
                h, q = i // 4, i % 4
                if i >= 2:
                    pe.wait_ge(exp_ready, i - 1)
                for j in range(2):
                    rows_, keys = slice(P * q, P * q + P), slice(384 * j, 384 * j + 384)
                    ins = product(bank[2 * (i % 2) + j][:, 0:384], three(
                        q_hi[:, h, rows_], q_lo[:, h, rows_], k_hi[:, h, keys], k_lo[h][:, keys]))
                ins.then_inc(s_mm, 1)

            pe.wait_ge(q_ready, 1)
            for i in range(3 * H):
                if i == H:
                    pe.wait_ge(k_ready, 1)
                if i == LATE_QK:
                    pe.wait_ge(qk_D, LATE_QK - 2)
                    scores(0)
                    pe.wait_ge(s_ready, KD)
                if 4 <= i < LATE_QK:
                    pe.wait_ge(qk_D, i - 3)
                if i < H:
                    src = [qsb[:, tt_, i, :] for tt_ in range(TT_N)]
                else:
                    h, part = (i - H) // 2, (i - H) % 2
                    src = [ksb[:, tt_, h, :] for tt_ in ((4, 5) if part else (0, 1, 2, 3))]
                for j, s_ in enumerate(src):
                    ins = pe.transpose(qk_bank(i)[0:QK, P * j:P * j + P], s_, ident[:, :])
                ins.then_inc(qk_T, 1)

            def turn_probs(i):
                pe.wait_ge(exp_ready, i + 1)
                for half in range(2):
                    if i >= 1:
                        pe.wait_ge(pt_A if half else pt_D, i)
                    for j in range(3):
                        ins = pe.transpose(bank[4 + half][:, P * j:P * j + P],
                                           Pm[i % 2][:, P * (3 * half + j):P * (3 * half + j) + P], ident[:, :])
                    ins.then_inc(p_T, 1)

            def weigh_values(i):
                h = i // 4
                pe.wait_ge(pt_D, i + 1)
                pe.wait_ge(pt_A, i + 1)
                if i >= 2:
                    pe.wait_ge(o_evac, i - 1)
                product(bank[6 + i % 2][:, 0:VD], [(PT[i % 2][:, kt, :], V[:, kt, VD * h:VD * h + VD]) for kt in range(6)]).then_inc(o_mm, 1)

            for i in range(4 * H):
                if i == 0:
                    pe.wait_ge(qk_D, LATE_QK)
                if i + 1 < 4 * H:
                    scores(i + 1)
                if i == 0:
                    pe.wait_ge(qk_D, 3 * H)
                turn_probs(i)
                if i >= 1:
                    weigh_values(i - 1)
            weigh_values(4 * H - 1)

            pe.wait_ge(o_evac, 4 * H)
            for k in range(4):
                for q in range(TT_N):
                    ins = pe.transpose(bank[k][:, P * q:P * q + P], otok[:, q, P * k:P * k + P], ident[:, :])
                ins.then_inc(o_T, 1)
            for p in range(2):
                wh, wl = panel(S_OF["wo"][p], 4, 512)
                for mi in range(4):
                    m = 4 * p + mi
                    if m >= 2:
                        pe.wait_ge(mg_f, m - 1)
                    for k in range(4):
                        if m == 0:
                            pe.wait_ge(oT_lo_r, k + 1)
                        ins = product(bank[6 + m % 2], three(wh[:, k, P * mi:P * mi + P], wl[:, k, P * mi:P * mi + P],
                                                             oT_hi[:, k, :], oT_lo[:, k, :]), first=k == 0, last=k == 3)
                    ins.then_inc(tile_done, 1)
            def square_sums(m):
                pe.wait_ge(sqx_ready, m + 1)
                for q in range(TT_N):
                    ins = pe.matmul(bank[0][:, TT_N * m + q:TT_N * m + q + 1], sqx[:, m, P * q:P * q + P], ones[:, 0:1], start=True, stop=True)
                return ins

            for p in range(4):
                wh, wl = panel(S_OF["wout"][p], KD, 256)
                for mi in range(2):
                    m = 2 * p + mi
                    if m >= 2:
                        pe.wait_ge(x1_ready, m - 1)
                    for k in range(KD):
                        if m == 0:
                            pe.wait_ge(mg_l, k + 1)
                        ins = product(bank[4 + m % 2], three(wh[:, k, P * mi:P * mi + P], wl[:, k, P * mi:P * mi + P],
                                                             mg_hi[:, k, :], mg_lo[:, k, :]), first=k == 0, last=k == KD - 1)
                    ins.then_inc(tile_done, 1)
                    if m >= 2:
                        square_sums(m - 2)

            square_sums(KD - 2)
            square_sums(KD - 1).then_inc(stat2_mm, 1)
            pe.wait_ge(mod2_used, 2 * KD)
            for q in range(8):
                pe.matmul(bank[2][:, q:q + 1], macc_late[:, q // 2, P * (q % 2):P * (q % 2) + P], ones[:, 0:1], start=True, stop=True)
            pe.wait_ge(diag3_ready, TT_N)
            for q in range(TT_N):
                ins = pe.matmul(bank[1][:, P * q:P * q + P], ones[:, :], diag3[:, q, :], start=True, stop=True)
            ins.then_inc(rstd3_mm, 1)

            s0 = S_OF["up"][0]

            def up_panel(i, j):
                s = s0 + j
                pe.wait_ge(lo_ready, s + 1 + 2 * i)
                return [b_[s % 2][:, :].rearrange("p (k v n) -> p k v n", k=KD, v=2) for b_ in (whi, wlo)]

            def up_products(i, j):
                wh, wl = up_panel(i, j)
                for v in range(2):
                    product(bank[4 + 2 * j + v], [q_ for k in range(KD) for q_ in three(
                        wh[:, k, v, :], wl[:, k, v, :], h2_hi[:, k, :], h2_lo[:, k, :])]).then_inc(tile_done, 1)

            wh, wl = up_panel(0, 0)
            for k in range(KD):
                pe.wait_ge(h2_l, k + 1)
                for v in range(2):
                    ins = product(bank[4 + v], three(wh[:, k, v, :], wl[:, k, v, :], h2_hi[:, k, :], h2_lo[:, k, :]),
                                  first=k == 0, last=k == KD - 1)
                    if k == KD - 1:
                        ins.then_inc(tile_done, 1)
            up_products(0, 1)
            with pe.Fori(1, 11) as i:
                for j in range(2):
                    pe.wait_ge(cv_d, 4 * i + 2 * j - 2)
                    up_products(i, j)

            s0 = S_OF["down"][0]
            pe.wait_ge(cv_d, 2 * KF - 2)

            def turn_out(pair):
                for mi in range(2):
                    pe.wait_ge(xo_ready, 2 * pair + mi + 1)
                    if pair >= 2 and mi == 0:
                        pe.wait_ge(ost_ready, 2 * (pair - 1))
                    for tt_ in range(TT_N):
                        ins = pe.transpose(bank[2 * (pair % 2) + mi][:, P * tt_:P * tt_ + P],
                                           xo[pair % 2][:, mi, P * tt_:P * tt_ + P], ident[:, :])
                    ins.then_inc(xo_T, 1)

            for pair in range(4):
                for kk in range(3):
                    n_k = (8, 8, 6)[kk]
                    wh, wl = panel(s0 + 3 * pair + kk, n_k, 256)
                    pe.wait_ge(act_l, 8 * kk + n_k)
                    for mi in range(2):
                        m = 2 * pair + mi
                        if kk == 0 and m == 2:
                            pe.wait_ge(cv_d, 2 * KF)
                        if kk == 0 and m >= 4:
                            pe.wait_ge(xo_ready, m - 3)
                        ins = product(bank[4 + m % 4], [q_ for k in range(n_k) for q_ in three(
                            wh[:, k, P * mi:P * mi + P], wl[:, k, P * mi:P * mi + P],
                            act_hi[:, 8 * kk + k, :], act_lo[:, 8 * kk + k, :])], first=kk == 0, last=kk == 2)
                        if kk == 2:
                            ins.then_inc(tile_done, 1)
                    if kk < 2:
                        ins.then_inc(down_used, 1)
                    if kk == 0 and pair >= 1:
                        turn_out(pair - 1)
            turn_out(3)


NAMES = ["x", "ctx", "w_mod", "w_in", "w_uq", "w_ukv", "q_norm_g", "k_norm_g", "w_o_attn", "w_glu", "w_out", "w_up", "w_down"]


def vector_columns(one):
    def cols(v):
        return v.reshape(-1, P).T

    def pair_states(v):
        return v.reshape(NP, 2, NS).reshape(NP, P).T

    parts = [cols(one[n]) for n in ("b_mod", "norm1_g", "norm2_g", "d_skip", "q_a_g", "kv_a_g")]
    parts += [cols(one["conv_w"][w]) for w in range(3)] + [cols(one["conv_b"])]
    parts += [pair_states(one[n]) for n in ("lam_re_f", "lam_im_f", "lam_re_b", "lam_im_b")]
    parts += [pair_states(np.repeat(one[n], NS)) for n in ("log_dt_f", "log_dt_b")]
    parts += [one[n].reshape(P, KD) for n in ("c", "c_ctx")]
    return np.ascontiguousarray(np.concatenate(parts, axis=1))


def kernel(**inputs):
    import concourse.bacc as bacc
    from concourse.bass_utils import run_bass_kernel_spmd

    nc = bacc.Bacc("TRN2", target_bir_lowering=False, num_devices=1)
    one = {name: np.asarray(v) if name == "c_ctx" else np.asarray(v)[0] for name, v in inputs.items()}
    arrays = {"in_" + name: np.ascontiguousarray(one[name]) for name in NAMES}
    arrays["in_vectors"] = vector_columns(one)
    pairs = [one[n].reshape(NP, 2, NS, GC).transpose(1, 2, 0, 3).reshape(P, NP, GC) for n in ("b_re", "b_im")]
    arrays["in_b"] = np.ascontiguousarray(np.stack(pairs, axis=1))
    pairs = [one[n].reshape(NP, 2, GC, NS).transpose(1, 3, 0, 2).reshape(P, NP, GC)
             for n in ("c_re_f", "c_im_f", "c_re_b", "c_im_b")]
    arrays["in_c_states"] = np.ascontiguousarray(np.stack(pairs, axis=1).reshape(P, 2, 2, NP, GC))
    arrays["in_rope"] = rope_tables()
    a = {name[3:]: nc.dram_tensor(name, v.shape, F32, kind="ExternalInput").ap() for name, v in arrays.items()}
    out = nc.dram_tensor("out_x", (T, D), F32, kind="ExternalOutput").ap()
    build(nc, a, out)
    result = run_bass_kernel_spmd(nc, [arrays], core_ids=[0])
    return result.results[0]["out_x"].reshape(1, T, D)
```
